# Optimizing a Trainium2 kernel written in Bass

```python
import math
import jax, jax.numpy as jnp
from jax import lax
import numpy as np

D_MODEL = 1024
BATCH = 1
SEQ = 1024
DEPTH = 1

CHUNK = 64
Q_BLOCK = 128
H_A = 4
HD_A = 64
VD_A = 2 * HD_A
H_B = 8
KV_B = 2
HD_B = 64
WINDOW = 128
W_CHUNKS = WINDOW // CHUNK
NUM_BUCKETS = 32
MAX_DISTANCE = 1024
N_EXPERTS = 16
N_GROUPS = 4
EXPERTS_PER_GROUP = N_EXPERTS // N_GROUPS
TOP_K = 2
D_EXPERT = 512
MOE_BLOCK = 256
ALPHA = (2 * DEPTH) ** 0.25
BETA = (8 * DEPTH) ** -0.25
LN_EPS = 1e-5
RMS_EPS = 1e-5
QA = H_A * 2 * HD_A
KA = H_A * 2 * HD_A
VA = H_A * VD_A
QB = H_B * HD_B
KB = KV_B * HD_B
VB = KV_B * HD_B
N_BRANCH = 2
IN_COLS = QA + KA + VA + QB + KB + VB + N_BRANCH * D_MODEL
SPLIT_POINTS = (QA, QA + KA, QA + KA + VA, QA + KA + VA + QB,
                QA + KA + VA + QB + KB, QA + KA + VA + QB + KB + VB)

kernel_name = "hybrid_diffattn_swa_sink_grouped_moe_deepnorm"

def layer_norm(x, g=None, b=None):
    xf = x.astype(jnp.float32)
    mu = jnp.mean(xf, -1, keepdims=True)
    var = jnp.mean(jnp.square(xf - mu), -1, keepdims=True)
    y = (xf - mu) * lax.rsqrt(var + LN_EPS)
    if g is not None:
        y = y * g.astype(jnp.float32) + b.astype(jnp.float32)
    return y.astype(x.dtype)

def rel_bucket(rel):
    nb = NUM_BUCKETS // 2
    max_exact = nb // 2
    ret = jnp.where(rel > 0, nb, 0)
    n = jnp.abs(rel)
    n_f = jnp.maximum(n, 1).astype(jnp.float32)
    large = max_exact + (jnp.log(n_f / max_exact) / math.log(MAX_DISTANCE / max_exact)
                         * (nb - max_exact)).astype(jnp.int32)
    large = jnp.minimum(large, nb - 1)
    return ret + jnp.where(n < max_exact, n, large)

def adaln(c, w, b):
    mod = jax.nn.silu(c) @ w + b
    shift, scale, gate = jnp.split(mod, 3, axis=-1)
    return shift[:, None], scale[:, None], gate[:, None]

def diff_attention(qa, ka, va, lam, lam_init, subln_w, bias_table):
    B, S, _ = qa.shape
    q = jnp.transpose(qa.reshape(B, S, H_A, 2, HD_A), (0, 2, 3, 1, 4))
    k = jnp.transpose(ka.reshape(B, S, H_A, 2, HD_A), (0, 2, 3, 1, 4))
    v = jnp.transpose(va.reshape(B, S, H_A, VD_A), (0, 2, 1, 3))
    lam_f = lam.astype(jnp.float32)
    lam_val = (jnp.exp(jnp.sum(lam_f[0] * lam_f[1])) - jnp.exp(jnp.sum(lam_f[2] * lam_f[3]))
               + lam_init)
    scale = HD_A ** -0.5
    pos = jnp.arange(S)
    outs = []
    for i in range(S // Q_BLOCK):
        q0 = i * Q_BLOCK
        kend = q0 + Q_BLOCK
        logits = jnp.einsum('bhmqd,bhmkd->bhmqk', q[:, :, :, q0:kend],
                            k[:, :, :, :kend]).astype(jnp.float32) * scale
        qp = pos[q0:kend]
        kp = pos[:kend]
        bias = bias_table[rel_bucket(kp[None, :] - qp[:, None])]
        bias = jnp.transpose(bias, (2, 0, 1))[:, None].astype(jnp.float32)
        mask = (kp[None, :] // CHUNK) <= (qp[:, None] // CHUNK)
        logits = jnp.where(mask, logits + bias, -jnp.inf)
        p = jax.nn.softmax(logits, axis=-1)
        attn = p[:, :, 0] - lam_val * p[:, :, 1]
        outs.append(jnp.einsum('bhqk,bhkv->bhqv', attn.astype(v.dtype), v[:, :, :kend]))
    o = jnp.concatenate(outs, axis=2).astype(jnp.float32)
    o = o * lax.rsqrt(jnp.mean(jnp.square(o), -1, keepdims=True) + RMS_EPS)
    o = o * subln_w.astype(jnp.float32) * (1.0 - lam_init)
    return jnp.transpose(o, (0, 2, 1, 3)).reshape(B, S, VA).astype(qa.dtype)

def swa_sinks(qb, kb, vb, sinks, bias_table):
    B, S, _ = qb.shape
    NC = S // CHUNK
    G = H_B // KV_B
    KW = W_CHUNKS * CHUNK
    qc = qb.reshape(B, NC, CHUNK, KV_B, G, HD_B)

    def band(t):
        tc = t.reshape(B, NC, CHUNK, KV_B, HD_B)
        tp = jnp.pad(tc, ((0, 0), (W_CHUNKS - 1, 0), (0, 0), (0, 0), (0, 0)))
        return jnp.concatenate([tp[:, j:j + NC] for j in range(W_CHUNKS)], axis=2)

    kband, vband = band(kb), band(vb)
    logits = jnp.einsum('bnqhgd,bnkhd->bnhgqk', qc, kband).astype(jnp.float32) * HD_B ** -0.5
    qi = jnp.arange(CHUNK)
    kj = jnp.arange(KW)
    rel = (kj[None, :] - (W_CHUNKS - 1) * CHUNK) - qi[:, None]
    bias = bias_table[rel_bucket(rel)]
    bias = jnp.transpose(bias, (2, 0, 1)).reshape(KV_B, G, CHUNK, KW).astype(jnp.float32)
    valid = (jnp.arange(NC)[:, None] + kj[None, :] // CHUNK - (W_CHUNKS - 1)) >= 0
    logits = jnp.where(valid[None, :, None, None, None, :], logits + bias, -jnp.inf)
    sink = jnp.broadcast_to(sinks.astype(jnp.float32).reshape(1, 1, KV_B, G, 1, 1),
                            logits.shape[:-1] + (1,))
    p = jax.nn.softmax(jnp.concatenate([logits, sink], axis=-1), axis=-1)[..., :-1]
    o = jnp.einsum('bnhgqk,bnkhd->bnqhgd', p.astype(vb.dtype), vband)
    return o.reshape(B, S, QB)

def mixer(h, w_in, lam, lam_init, subln_w, sinks, w_branch_a, w_branch_b, w_out, rel_bias):
    B, S, D = h.shape
    proj = h @ w_in
    qa, ka, va, qb, kb, vb, gl = jnp.split(proj, SPLIT_POINTS, axis=-1)
    oa = diff_attention(qa, ka, va, lam, lam_init, subln_w, rel_bias[:, :H_A])
    ob = swa_sinks(qb, kb, vb, sinks, rel_bias[:, H_A:])
    g = jax.nn.sigmoid(gl.astype(jnp.float32)).reshape(B, S, N_BRANCH, D).astype(h.dtype)
    merged = g[:, :, 0] * (oa @ w_branch_a) + g[:, :, 1] * (ob @ w_branch_b)
    return merged @ w_out

def route(ht, router_w, router_b):
    T = ht.shape[0]
    scores = jax.nn.sigmoid((ht @ router_w).astype(jnp.float32))
    biased = scores + router_b.astype(jnp.float32)
    grp = biased.reshape(T, N_GROUPS, EXPERTS_PER_GROUP)
    grp_score = jnp.sum(lax.top_k(grp, TOP_K)[0], axis=-1)
    g_idx = jnp.argmax(grp_score, axis=-1)
    within = jnp.take_along_axis(grp, g_idx[:, None, None], axis=1)[:, 0]
    _, local = lax.top_k(within, TOP_K)
    e_idx = g_idx[:, None] * EXPERTS_PER_GROUP + local
    w = jnp.take_along_axis(scores, e_idx, axis=1)
    w = w / jnp.sum(w, axis=-1, keepdims=True)
    return e_idx, w

def moe(h, router_w, router_b, w1, w3, w2):
    B, S, D = h.shape
    T = B * S
    ht = h.reshape(T, D)
    e_idx, gate = route(ht, router_w, router_b)
    M = T * TOP_K
    flat_e = e_idx.reshape(M)
    flat_tok = jnp.arange(M, dtype=jnp.int32) // TOP_K
    flat_w = gate.reshape(M)
    order = jnp.argsort(flat_e, stable=True)
    se = flat_e[order]
    counts = jnp.bincount(flat_e, length=N_EXPERTS)
    starts = jnp.cumsum(counts) - counts
    padded = (counts + MOE_BLOCK - 1) // MOE_BLOCK * MOE_BLOCK
    pends = jnp.cumsum(padded)
    pstarts = pends - padded
    dest = pstarts[se] + (jnp.arange(M) - starts[se])
    P = M + N_EXPERTS * MOE_BLOCK
    NB = P // MOE_BLOCK
    tok_buf = jnp.full((P,), T, jnp.int32).at[dest].set(flat_tok[order])
    w_buf = jnp.zeros((P,), jnp.float32).at[dest].set(flat_w[order])
    blk_e = jnp.minimum(jnp.searchsorted(pends, jnp.arange(NB) * MOE_BLOCK, side='right'),
                        N_EXPERTS - 1)
    h_pad = jnp.concatenate([ht, jnp.zeros((1, D), ht.dtype)], axis=0)
    xb = h_pad[tok_buf].reshape(NB, MOE_BLOCK, D)

    def expert_block(args):
        xblk, e = args
        return (jax.nn.silu(xblk @ w1[e]) * (xblk @ w3[e])) @ w2[e]

    yb = lax.map(expert_block, (xb, blk_e)).reshape(P, D)
    y = jnp.zeros((T + 1, D), h.dtype).at[tok_buf].add(yb * w_buf[:, None].astype(h.dtype))
    return y[:T].reshape(B, S, D)

def setup_inputs(seed: int = 0) -> dict:
    key = jax.random.key(seed)
    ks = jax.random.split(key, 20)
    D = D_MODEL
    f32 = jnp.float32
    nrm = lambda k, shp, s: jax.random.normal(k, shp, f32) * s
    col_scale = jnp.concatenate([
        jnp.ones((QA + KA,), f32), jnp.full((VA,), BETA, f32),
        jnp.ones((QB + KB,), f32), jnp.full((VB,), BETA, f32),
        jnp.ones((N_BRANCH * D,), f32)])
    return {
        "x": nrm(ks[0], (BATCH, SEQ, D), 1.0),
        "c": nrm(ks[1], (BATCH, D), 1.0),
        "ada_w": nrm(ks[2], (DEPTH, 2, D, 3 * D), D ** -0.5),
        "ada_b": nrm(ks[3], (DEPTH, 2, 3 * D), 0.02),
        "w_in": nrm(ks[4], (DEPTH, D, IN_COLS), D ** -0.5) * col_scale,
        "lam": nrm(ks[5], (DEPTH, 4, HD_A), 0.1),
        "subln_w": 1.0 + nrm(ks[6], (DEPTH, VD_A), 0.02),
        "sinks": nrm(ks[7], (DEPTH, H_B), 1.0),
        "w_branch_a": nrm(ks[8], (DEPTH, VA, D), VA ** -0.5 * BETA),
        "w_branch_b": nrm(ks[9], (DEPTH, QB, D), QB ** -0.5 * BETA),
        "w_out": nrm(ks[10], (DEPTH, D, D), D ** -0.5 * BETA),
        "ln_g": 1.0 + nrm(ks[11], (DEPTH, 2, D), 0.02),
        "ln_b": nrm(ks[12], (DEPTH, 2, D), 0.02),
        "rel_bias": nrm(ks[13], (NUM_BUCKETS, H_A + H_B), 0.5),
        "router_w": nrm(ks[14], (D, N_EXPERTS), D ** -0.5),
        "router_b": nrm(ks[15], (N_EXPERTS,), 0.01),
        "exp_w1": nrm(ks[16], (DEPTH, N_EXPERTS, D, D_EXPERT), D ** -0.5),
        "exp_w3": nrm(ks[17], (DEPTH, N_EXPERTS, D, D_EXPERT), D ** -0.5),
        "exp_w2": nrm(ks[18], (DEPTH, N_EXPERTS, D_EXPERT, D), D_EXPERT ** -0.5 * BETA),
    }

def reference(x, c, ada_w, ada_b, w_in, lam, subln_w, sinks, w_branch_a, w_branch_b,
              w_out, ln_g, ln_b, rel_bias, router_w, router_b, exp_w1, exp_w3, exp_w2):
    for l in range(DEPTH):
        lam_init = 0.8 - 0.6 * math.exp(-0.3 * l)
        shift, scale, gate = adaln(c, ada_w[l, 0], ada_b[l, 0])
        h = layer_norm(x) * (1.0 + scale) + shift
        y = mixer(h, w_in[l], lam[l], lam_init, subln_w[l], sinks[l],
                  w_branch_a[l], w_branch_b[l], w_out[l], rel_bias)
        x = layer_norm(ALPHA * x + gate * y, ln_g[l, 0], ln_b[l, 0])
        shift, scale, gate = adaln(c, ada_w[l, 1], ada_b[l, 1])
        h = layer_norm(x) * (1.0 + scale) + shift
        y = moe(h, router_w, router_b, exp_w1[l], exp_w3[l], exp_w2[l])
        x = layer_norm(ALPHA * x + gate * y, ln_g[l, 1], ln_b[l, 1])
    return x


_drawn_inputs = setup_inputs


def setup_inputs(seed=0):
    import zlib

    import numpy as np

    out = dict(_drawn_inputs(seed))
    spreads = {}
    factors = {'lam': 6.96, 'subln_w': 8.0, 'sinks': 8.0}
    for name, (base, spread) in spreads.items():
        noise = np.random.default_rng([zlib.crc32(name.encode()), seed]).standard_normal(out[name].shape)
        drawn = base * np.exp(spread * noise) if base else spread * noise
        out[name] = __import__('jax').numpy.asarray(drawn.astype(out[name].dtype))
    for name, factor in factors.items():
        out[name] = (out[name] * factor).astype(out[name].dtype)
    return out
```

```python
from contextlib import ExitStack

import concourse.bass as bass
from concourse import mybir

F32 = mybir.dt.float32
U32 = mybir.dt.uint32
I32 = mybir.dt.int32
ALU = mybir.AluOpType
ACT = mybir.ActivationFunctionType
AX = mybir.AxisListType.X

P = 128
D = 1024
S = 1024
NT = S // P
NK = D // P
BANK = 512
H_A, H_B = 4, 8
QA, KA, VA, QB, KVB = 512, 512, 512, 512, 256
COL_Q, COL_K, COL_V, COL_QB, COL_KB = 0, 512, 1024, 1536, 2048
COL_G = 2304
NBUCKET = 32
TAB = 1152
ALPHA = 2.0 ** 0.25
LAM_INIT = 0.8 - 0.6
EPS = 1e-5
NEG = -1.0e30
BIG = 3.0e38
NE, NG, EPG = 16, 4, 4
FE = 512
MAXBLK = 32
KB = 256
SQ = 0.125


def mixer_moe_kernel(nc, x, c, ada_w, ada_b, w_in, lam, subln_w, sinks, w_a, w_b, w_out,
                     ln_g, ln_b, rel_bias, router_w, router_b, w1, w3, w2,
                     ident_h, onehot_h, lower_h, iota_h, rev_h, before_h, tokid_h, flip_h, out):
    base = (nc.sbuf_base + 63) // 64 * 64

    def at(name, kib, shape, dt=F32):
        return nc.alloc_sbuf_tensor_at(name, shape, dt, offset=base + int(kib * 1024))

    ctx = ExitStack()
    with ctx:
        ctx.enter_context(nc.allow_non_contiguous_dma(reason="columns of a few hundred bytes"))

        def sem(name):
            return ctx.enter_context(nc.semaphore(name))

        bias_d = nc.dram_tensor("bias_by_distance", [12, TAB], F32)
        mod_d = nc.dram_tensor("ada_mod", [12, BANK], F32)
        h2_d = nc.dram_tensor("moe_input", [S, D], F32)
        y_d = nc.dram_tensor("expert_rows", [MAXBLK * P, D], F32)

        W0 = at("W0", 0, [P, 4096])
        W1 = at("W1", 16, [P, 4096])
        W2 = at("W2", 176, [P, 4096])
        G2 = at("G2", 184, [P, 4096])
        hT = at("hT", 48, [P, NK, S])
        xs = at("xs", 80, [P, NT, D])
        Qa = at("Qa", 80, [P, H_A, S])
        Ka = at("Ka", 96, [P, H_A, S])
        Va = at("Va", 112, [P, NT, VA])
        Qb = at("Qb", 128, [P, 4, S])
        Kb = at("Kb", 144, [P, S])
        Vb = at("Vb", 148, [P, NT, P])
        biasA = at("biasA", 152, [P, H_A, S])
        biasB = at("biasB", 168, [P, H_B, 256])
        L = at("L", 176, [P, 3, 2, S])
        LB = at("LB", 176, [P, 4, 2, 256])
        aT = at("aT", 200, [P, 2, BANK])
        o = [32.0]

        def small(name, shape, dt=F32):
            n = 1
            for v in shape[1:]:
                n *= v
            t = at(name, o[0], shape, dt)
            o[0] += (n * 4 + 31) // 32 * 32 / 1024
            assert o[0] <= 48, o[0]
            return t

        ident = small("ident", [P, P])
        cc = small("cc", [P, NK])
        csil = small("csil", [P, NK])
        ce = small("ce", [P, NK])
        sscol = small("sscol", [P, 16])
        negsink = small("negsink", [P, H_B])
        sinkc = small("sinkc", [P, H_B])
        lamb = small("lamb", [P, 4, 64])
        lams = small("lams", [P, 4])
        subc = small("subc", [P, 1])
        mv = small("mv", [P, NT, 2])
        rstd = small("rstd", [P, NT])
        stat = small("stat", [P, 2, 12])
        nmA = small("nmA", [P, 32, 2])
        smA = small("smA", [P, 32, 2])
        msA = small("msA", [P, 32])
        nmB = small("nmB", [P, 32, 2])
        smB = small("smB", [P, 32, 2])
        junk = small("junk", [P, P])
        pad_at = o[0]
        qpad = small("qpad", [P, 2, 2, P])
        adab = small("adab", [P, 3, BANK])
        modrow = at("modrow", 204, [P, BANK])
        onehot = at("onehot", 128, [NBUCKET, TAB])
        relb = at("relb", 133, [NBUCKET, 12])
        btab = at("btab", 134, [12, TAB])
        flip = at("flip", 138.5, [P, P])
        skewA = at("skewA", 112, [P, H_A, S])
        skewB = at("skewB", 139, [P, H_B, 256])
        zero1k = at("zero1k", 206, [P, 256])
        mT = at("mT", 96, [P, NK, S])
        wa = at("wa", 152, [P, 4, D])
        wb = at("wb", 168, [P, 4, D])
        sg = at("sg", 144, [P, 2, 2, BANK])
        X2 = at("X2", 48, [P, NT, D])
        rowA = at("rowA", 80, [P, 4, D])
        rowB = at("rowB", 128, [P, 4, D])
        xin = at("xin", 192, [P, 1, D])
        h2 = at("h2", 196, [P, 2, D])
        h2T = at("h2T", 43, [P, NK, P])
        rw = at("rw", 204, [P, NK, NE])
        rwp = at("rwp", 39, [P, NK, P])
        lg = at("lg", 204.5, [P, NT, NE])
        assert pad_at <= 36, pad_at
        lower = at("lower", 36, [P, P])
        iota = at("iota", 36.5, [P, P])
        before = at("before", 37, [P, NE, NE])
        rev = at("rev", 38, [P, NE + NG])
        tokid = at("tokid", 38.125, [P, NT])
        rbias = at("rbias", 38.25, [P, NE])
        r = [80.0]

        def rt(name, shape, dt=F32):
            n = 1
            for v in shape[1:]:
                n *= v
            t = at(name, r[0], shape, dt)
            r[0] += (n * 4 + 31) // 32 * 32 / 1024
            assert r[0] <= 128
            return t

        rk = [205.0]

        def keep(name, shape, dt=F32):
            n = 1
            for v in shape[1:]:
                n *= v
            t = at(name, rk[0], shape, dt)
            rk[0] += (n * 4 + 31) // 32 * 32 / 1024
            assert rk[0] <= 207.75
            return t

        wk = keep("wk", [P, 2, NT])
        slot_u = keep("slot_u", [P, 2, NT], U32)
        idx_u = keep("idx_u", [P, MAXBLK], U32)
        blk_e = keep("blk_e", [P, MAXBLK], I32)
        pend_i = keep("pend_i", [P, NE], I32)
        nblk_i = keep("nblk_i", [P, 1], I32)
        idx_c = keep("idx_c", [P, 1], U32)

        s_ = rt("sco", [P, NT, NE])
        bi = rt("bia", [P, NT, NE])
        t0 = rt("t0", [P, NT, NE])
        t1 = rt("t1", [P, NT, NE])
        oh = [rt("oh0", [P, NT, NE]), rt("oh1", [P, NT, NE])]
        g0_ = rt("g0", [P, NT, NG])
        g1_ = rt("g1", [P, NT, NG])
        g2_ = rt("g2", [P, NT, NG])
        g3_ = rt("g3", [P, NT, NG])
        g4_ = rt("g4", [P, NT, NG])
        m1 = rt("m1", [P, NT])
        ms_ = rt("ms", [P, 2, NT])
        Mex = rt("Mex", [P, NT, NE])
        rank = rt("rank", [P, NT, NE])
        cnt = rt("cnt", [P, NE])
        nb_ = rt("nb", [P, NE])
        pst = rt("pst", [P, NE])
        pen = rt("pen", [P, NE])
        big = rt("big", [P, MAXBLK, NE])
        ef = rt("ef", [P, MAXBLK])
        Rk = rt("Rk", [P, 2, NT])
        Pk = rt("Pk", [P, 2, NT])
        rb_ = rt("rb", [P, 2, NT])
        c8 = rt("c8", [P, 2 * NT * 8])
        ones = rt("ones", [P, P])
        mul8 = rt("mul8", [P, 8])
        Aoh = rt("Aoh", [P, 16, P])
        Boh = rt("Boh", [P, 16, MAXBLK])
        EXP = at("EXP", 80, [P, 28 * 1024])
        ODD, EVEN = 0, 64 * KB
        xg = at("xg", 0, [P, D])
        xT = at("xT", 4, [P, NK, P])
        sig = at("sig", 8, [P, FE])
        hh = at("hh", 10, [P, FE])
        hhT = at("hhT", 12, [P, 4, P])
        ysb = at("ysb", 14, [P, D])
        yg = at("yg", 0, [P, 2, 2, D])
        r2 = at("r2", 16, [P, 2, D])

        ps = ctx.enter_context(nc.psum_tensor("ps", [P, 8 * BANK], F32))

        def bank(b, n=BANK, w=1):
            return ps[:, b * BANK:b * BANK + (w - 1) * BANK + n]

        small_in = sem("small_in")
        x_in = [sem(f"x_in{i}") for i in range(4)]
        slot_in = {n: sem(f"slot_in_{n}") for n in ("W0", "W1", "W2", "G2")}
        padz = sem("padz")
        silu_e, silu_v = sem("silu_e"), sem("silu_v")
        ln0, ln0_sq = sem("ln0"), sem("ln0_sq")
        btab_mm, btab_ev, btab_out, btab_in, mask_set = (sem("btab_mm"), sem("btab_ev"), sem("btab_out"),
                                                         sem("btab_in"), sem("mask_set"))
        flip_mm, flip_v, flip_a, zero_set, y_zero, pool_go = (sem("flip_mm"), sem("flip_v"), sem("flip_a"),
                                                              sem("zero_set"), sem("y_zero"), sem("pool_go"))
        lam_v, lam_e = sem("lam_v"), sem("lam_e")
        ada_mm, ada_ev, ada_out, ss_in, ss_one = (sem("ada_mm"), sem("ada_ev"), sem("ada_out"), sem("ss_in"),
                                                  sem("ss_one"))
        xt_mm, xt_v, xt_a = sem("xt_mm"), sem("xt_v"), sem("xt_a")
        proj_mm, proj_v, proj_a = sem("proj_mm"), sem("proj_v"), sem("proj_a")
        padA, scoreA, logitA, expA, attnA, trA, aT_ev, pvA, oA = (sem("padA"), sem("scoreA"), sem("logitA"), sem("expA"), sem("attnA"),
                                                    sem("trA"), sem("aT_ev"), sem("pvA"), sem("oA"))
        padB, scoreB, logitB, expB, trB, bT_ev, pvB, oB = (sem("padB"), sem("scoreB"), sem("logitB"), sem("expB"), sem("trB"),
                                             sem("bT_ev"), sem("pvB"), sem("oB"))
        fin_v, fin_a, finT, finT_v, finT_a = (sem("fin_v"), sem("fin_a"), sem("finT"), sem("finT_v"),
                                              sem("finT_a"))
        wab_in, merge_mm, merge_sg, merged = sem("wab_in"), sem("merge_mm"), sem("merge_sg"), sem("merged")
        rows_in, rows_one = sem("rows_in"), sem("rows_one")
        xin_in, y_mm, post_v, post_a, h2_out = (sem("xin_in"), sem("y_mm"), sem("post_v"), sem("post_a"),
                                                sem("h2_out"))
        h2T_mm, h2T_ev, rout_mm, rout_ev, rwp_v = (sem("h2T_mm"), sem("h2T_ev"), sem("rout_mm"), sem("rout_ev"),
                                                   sem("rwp_v"))
        rt_in, route, route_a, rank_mm, idx_mm, tabs = (sem("rt_in"), sem("route"), sem("route_a"), sem("rank_mm"),
                                                        sem("idx_mm"), sem("tabs"))
        exp_even, exp_odd, exp_ready = sem("exp_even"), sem("exp_odd"), sem("exp_ready")
        idx_ok, gathered, xg_tr, xT_v, xT_a = (sem("idx_ok"), sem("gathered"), sem("xg_tr"), sem("xT_v"),
                                               sem("xT_a"))
        gate_mm, up_mm, sig_a, glu_v, hh_v, hh_tr, hhT_v = (sem("gate_mm"), sem("up_mm"), sem("sig_a"),
                                                            sem("glu_v"), sem("hh_v"), sem("hh_tr"),
                                                            sem("hhT_v"))
        down_mm, y_v, y_a, y_out = sem("down_mm"), sem("y_v"), sem("y_a"), sem("y_out")
        comb_in = [sem("comb_in0"), sem("comb_in1")]
        finq, comb_r = sem("finq"), sem("comb_r")
        RANK_READY, OH_READY = [0], [0]
        comb, comb_a, res_out = sem("comb"), sem("comb_a"), [sem("res_out0"), sem("res_out1")]

        bufs = {"W0": W0, "W1": W1, "W2": W2, "G2": G2}
        w_rows = w_in.rearrange("a (k p) n -> p (a k) n", p=P)
        ada_rows = ada_w.rearrange("a s (k p) n -> p (a s) k n", p=P)
        wo_rows = w_out.rearrange("a (k p) n -> p (a k) n", p=P)
        NA_CH = 12

        def ada_src(ch):
            rd, kp = ch // 4, ch % 4
            c0 = rd * 2048
            parts = []
            while c0 < (rd + 1) * 2048:
                sub, off = c0 // 3072, c0 % 3072
                n = min(3072 - off, (rd + 1) * 2048 - c0)
                parts.append((c0 - rd * 2048, n, ada_rows[:, sub, 2 * kp:2 * kp + 2, off:off + n]))
                c0 += n
            return parts

        chunks = []

        def chunk(slot, pairs, used):
            chunks.append((slot, pairs, used))

        for ch in range(4):
            s = ("W0", "W1", "W2")[ch % 3]
            v = bufs[s][:, :].rearrange("p (k n) -> p k n", k=2)
            chunk(s, [(v[:, :, a:a + n], src) for a, n, src in ada_src(ch)], (ada_mm, ch + 1))
        groups = []
        PROJ = [("va", COL_V, 512), ("ka", COL_K, 512), ("qa", COL_Q, 512), ("kv", COL_KB, 256), ("qb", COL_QB, 512)]
        for pi, (kind, c0, n) in enumerate(PROJ):
            if kind == "va":
                groups += [(pi, "va", t) for t in range(NT)]
            elif kind == "kv":
                groups += [(pi, "kb", 0), (pi, "kb", 1), (pi, "vb", 0), (pi, "vb", 1)]
            else:
                groups += [(pi, kind, g) for g in range(8)]
            s = ("W0", "W1", "W2")[(4 + pi) % 3]
            v = bufs[s][:, 0:NK * n].rearrange("p (k n) -> p k n", k=NK)
            if kind == "qb":
                vt = bufs[s][:, 0:NK * n].rearrange("p (k t j n) -> p k t j n", k=NK, t=4, j=2)
                st = w_rows[:, :, c0:c0 + n].rearrange("p k (j t n) -> p k j t n", j=2, t=4)
                chunk(s, [(vt[:, k, :, j, :], st[:, k, j]) for k in range(NK) for j in range(2)],
                      (proj_mm, len(groups)))
            else:
                chunk(s, [(v, w_rows[:, :, c0:c0 + n])], (proj_mm, len(groups)))
        NGRP = len(groups)
        for ch in range(4, NA_CH):
            s = ("W0", "W1")[ch % 2]
            v = bufs[s][:, :].rearrange("p (k n) -> p k n", k=2)
            chunk(s, [(v[:, :, a:a + n], src) for a, n, src in ada_src(ch)], (ada_mm, ch + 1))
        C_ADA2 = 9
        C_G = len(chunks)
        for q in range(4):
            s = ("W0", "W1", "G2", "W0")[q]
            v = bufs[s][:, :].rearrange("p (k g n) -> p k g n", k=NK, g=2)
            chunk(s, [(v[:, :, g, :], w_rows[:, :, COL_G + g * D + q * 256:COL_G + g * D + (q + 1) * 256])
                      for g in range(2)], (merge_mm, 16 * (q + 1)))
        C_O = len(chunks)
        for n in range(2):
            s = ("W1", "W0")[n]
            v = bufs[s][:, :].rearrange("p (k n) -> p k n", k=NK)
            chunk(s, [(v, wo_rows[:, :, n * 512:(n + 1) * 512])], None)

        def arrived(eng, ch):
            slot = chunks[ch][0]
            n = sum(len(pr) for s, pr, _ in chunks[:ch + 1] if s == slot)
            eng.wait_ge(slot_in[slot], 16 * n)

        def cview(ch, **kw):
            return bufs[chunks[ch][0]]

        def ngrp(i):
            return i // 4 + 1

        def grp0(v):
            return (v // NT) * 12 + sum(ngrp(i) for i in range(v % NT))

        def pv_of(g):
            return g

        def proj_dst(g):
            pi, kind, q = groups[g]
            if kind == "va":
                return Va[:, q, :], 1.0
            if kind == "ka":
                return Ka[:, q // 2, (q % 2) * 512:(q % 2) * 512 + 512], 1.0
            if kind == "qa":
                return Qa[:, q // 2, (q % 2) * 512:(q % 2) * 512 + 512], SQ
            if kind == "qb":
                return Qb[:, q // 2, (q % 2) * 512:(q % 2) * 512 + 512], SQ
            if kind == "kb":
                return Kb[:, q * 512:(q + 1) * 512], 1.0
            return Vb[:, 4 * q:4 * q + 4, :].rearrange("p t n -> p (t n)"), 1.0

        def flip_group(g):
            if g < 8:
                return (skewA[:, g // 2, (g % 2) * 512:(g % 2) * 512 + 512], biasA[:, g // 2, (g % 2) * 512:(g % 2) * 512 + 512])
            g -= 8
            return (skewB[:, 2 * g:2 * g + 2, :].rearrange("p h n -> p (h n)"),
                    biasB[:, 2 * g:2 * g + 2, :].rearrange("p h n -> p (h n)"))

        block = ctx.enter_context(nc.Block())

        def bc(row, n=P):
            return bass.AP(row.tensor, row.offset, [[0, n]] + [list(v) for v in row.ap[-1:]])

        @block.sync
        def _(sp):
            xr = x.rearrange("a (t p) d -> p (a t) d", p=P)

            def load(ch):
                slot, pairs, _ = chunks[ch]
                prev = [q for q in range(ch) if chunks[q][0] == slot]
                if prev:
                    sp.wait_ge(*chunks[prev[-1]][2])
                if ch == C_G + 2:
                    sp.wait_ge(trB, 32)
                    sp.wait_ge(bT_ev, 32)
                for dst, src in pairs:
                    sp.dma_start(dst, src).then_inc(slot_in[slot], 16)

            for i in range(4):
                sp.dma_start(xs[:, 2 * i:2 * i + 2, :], xr[:, 2 * i:2 * i + 2, :]).then_inc(x_in[i], 16)
                if i < 3:
                    load(i)
            sp.wait_ge(btab_ev, 3)
            sp.dma_start(bias_d.ap(), btab[:, :]).then_inc(btab_out, 16)
            sp.wait_ge(btab_out, 16)
            sp.dma_start(skewA[:, :, :], bass.AP(bias_d, 0, [[1, P], [TAB, H_A], [1, S]])).then_inc(btab_in, 16)
            sp.dma_start(skewB[:, :, :], bass.AP(bias_d, H_A * TAB + 768, [[1, P], [TAB, H_B], [1, 256]])).then_inc(btab_in, 16)
            load(3)
            for ch in range(4, 9):
                if ch == 5:
                    sp.wait_ge(ada_ev, 1)
                    sp.dma_start(mod_d[0:4, :], modrow[0:P:32, :]).then_inc(ada_out, 16)
                    sp.wait_ge(ada_out, 16)
                    sp.dma_start(sscol[:, :], bass.AP(mod_d, 0, [[1, P], [P, 16]])).then_inc(ss_in, 16)
                load(ch)
            for ch in range(9, C_G):
                load(ch)
                if ch == 14:
                    sp.wait_ge(ada_ev, 2)
                    sp.dma_start(mod_d[4:8, :], modrow[0:P:32, :]).then_inc(ada_out, 16)
            load(C_G)
            load(C_G + 1)
            sp.wait_ge(ada_ev, 3)
            sp.dma_start(mod_d[8:12, :], modrow[0:P:32, :]).then_inc(ada_out, 16)
            sp.wait_ge(zero_set, 1)
            for q in range(4):
                sp.dma_start(y_d[16 * P:MAXBLK * P, q * 256:(q + 1) * 256].rearrange("(a p) n -> p a n", p=P),
                             zero1k[:, :].unsqueeze(1).to_broadcast([P, 16, 256])).then_inc(y_zero, 16)
            sp.wait_ge(logitA, 64)
            sp.dma_start(wa[:, :, :], w_a.rearrange("a (k p) n -> p (a k) n", p=P)).then_inc(wab_in, 16)
            sp.wait_ge(trB, 32)
            sp.wait_ge(bT_ev, 32)
            sp.wait_ge(logitB, 64)
            wbr = w_b.rearrange("a (j t p) n -> j p (a t) n", j=2, p=64)
            for j in range(2):
                sp.dma_start(wb[64 * j:64 * j + 64, :, :], wbr[j]).then_inc(wab_in, 16)
            load(C_G + 2)
            load(C_G + 3)
            load(C_O)
            sp.wait_ge(merged, 48)
            sp.wait_ge(merge_mm, 64)
            load(C_O + 1)
            sp.wait_ge(ada_out, 48)
            for dst, src in [(rowA[:, 0, :], mod_d[4:6, :]), (rowA[:, 3, :], mod_d[8:10, :]),
                             (rowB[:, 3, :], mod_d[6:8, :]), (rowB[:, 0, :], mod_d[10:12, :])]:
                sp.dma_start(dst, bass.AP(src.tensor, src.offset, [[0, P], [1, D]])).then_inc(rows_in, 16)
            for dst, src in [(rowA[:, 1, :], ln_g[0, 0]), (rowA[:, 2, :], ln_b[0, 0]),
                             (rowB[:, 1, :], ln_g[0, 1]), (rowB[:, 2, :], ln_b[0, 1])]:
                sp.dma_start(dst, bass.AP(src.tensor, src.offset, [[0, P], [1, D]])).then_inc(rows_in, 16)
            for dst, src in [(rw[:, :, :], router_w.rearrange("(k p) e -> p k e", p=P)), (lower[:, :], lower_h),
                             (iota[:, :], iota_h), (rev[:, :], rev_h),
                             (before[:, :, :], before_h.rearrange("p (a b) -> p a b", a=NE)),
                             (tokid[:, :], tokid_h), (rbias[:, :], bass.AP(router_b.tensor, 0, [[0, P], [1, NE]]))]:
                sp.dma_start(dst, src).then_inc(rt_in, 16)
            w1r = w1.rearrange("a e (k p) n -> p (a e) k n", p=P)
            w3r = w3.rearrange("a e (k p) n -> p (a e) k n", p=P)
            w2r = w2.rearrange("a e (k p) n -> p (a e) k n", p=P)

            def load_expert(e, where, signal):
                for wi, (src, k) in enumerate(((w1r, NK), (w3r, NK), (w2r, 4))):
                    dst = EXP[:, where + wi * 4096:where + (wi + 1) * 4096].rearrange("p (k n) -> p k n", k=k)
                    sp.dma_start(dst, src[:, bass.ds(e, 1), :, :].rearrange("p e k n -> p (e k) n")
                                 ).then_inc(signal, 16)

            xt = x.rearrange("a (t p) d -> t p (a d)", p=P)
            for t in range(NT):
                if t >= 1:
                    sp.wait_ge(post_v, 18 * (t - 1) + 2)
                sp.dma_start(xin[:, 0, :], xt[t]).then_inc(xin_in, 16)
                if t == 0:
                    load_expert(0, EVEN, exp_even)
                if t >= 1:
                    sp.wait_ge(post_v, 18 * t)
                    sp.dma_start(h2_d[(t - 1) * P:t * P, :], h2[:, (t - 1) % 2, :]).then_inc(h2_out, 16)
            sp.wait_ge(post_v, 18 * NT)
            sp.dma_start(h2_d[(NT - 1) * P:NT * P, :], h2[:, (NT - 1) % 2, :]).then_inc(h2_out, 16)
            sp.wait_ge(idx_mm, 1)
            sp.wait_ge(tabs, 1)
            load_expert(1, ODD, exp_odd)
            sp.wait_ge(exp_even, 48)
            sp.sem_inc(exp_ready, 1)
            with sp.Fori(1, NE // 2) as pr:
                sp.wait_ge(exp_odd, pr * 48)
                sp.sem_inc(exp_ready, 1)
                end = sp.value_load(pend_i[0:1, bass.ds(pr * 2 - 2, 1)], min_val=1, max_val=MAXBLK)
                sp.wait_ge(y_v, end)
                load_expert(pr * 2, EVEN, exp_even)
                sp.wait_ge(exp_even, pr * 48 + 48)
                sp.sem_inc(exp_ready, 1)
                end2 = sp.value_load(pend_i[0:1, bass.ds(pr * 2 - 1, 1)], min_val=1, max_val=MAXBLK)
                sp.wait_ge(y_v, end2)
                load_expert(pr * 2 + 1, ODD, exp_odd)
            sp.wait_ge(exp_odd, 48 * NE // 2)
            sp.sem_inc(exp_ready, 1)
            for t in range(NT):
                sp.wait_ge(comb, 11 * (t + 1))
                sp.dma_start(out.rearrange("a (t p) d -> t p (a d)", p=P)[t], r2[:, t % 2, :]).then_inc(res_out[t % 2], 16)
            sp.wait_ge(res_out[0], 16 * NT // 2)
            sp.wait_ge(res_out[1], 16 * NT // 2)
            sp.wait_ge(ada_out, 48)
            sp.wait_ge(h2_out, 16 * NT)

        @block.gpsimd
        def _(pool):
            nc.gpsimd.memset(qpad[:, :, :, :], 0.0).then_inc(padz, 1)
            pool.wait_ge(padz, 1)
            pool.wait_ge(flip_v, 6)
            pool.wait_ge(flip_a, 6)
            nc.gpsimd.memset(biasA[0:64, :, S - 64:S], NEG).then_inc(mask_set, 1)
            for n_, region in enumerate((biasB[0:64, :, 0:64], biasB[0:64, :, 192:256], biasB[64:128, :, 0:128])):
                pool.wait_ge(mask_set, n_ + 1)
                nc.gpsimd.memset(region, NEG).then_inc(mask_set, 1)
            pool.wait_ge(mask_set, 4)
            nc.gpsimd.memset(zero1k[:, :], 0.0).then_inc(zero_set, 1)
            pool.wait_ge(proj_v, NGRP // 2)
            pool.wait_ge(proj_a, NGRP // 2)
            for u in range(32):
                h, i = u // NT, u % NT
                if u >= 2:
                    pool.wait_ge(scoreA, 2 * (u - 1))
                for m in range(2):
                    pool.wait_ge(*((padA, 2 * u + m) if u + m else (zero_set, 1)))
                    nc.gpsimd.tensor_copy(qpad[64 * m:64 * m + 64, u % 2, m, :],
                                          Qa[64 * m:64 * m + 64, h, i * P:(i + 1) * P]).then_inc(padA, 1)
            for u in range(32):
                i, t = u // 4, u % 4
                pool.wait_ge(scoreA, 64) if u == 0 else None
                if u >= 2:
                    pool.wait_ge(scoreB, 2 * (u - 1))
                for m in range(2):
                    pool.wait_ge(*((padB, 2 * u + m) if u + m else (padA, 64)))
                    nc.gpsimd.tensor_copy(qpad[64 * m:64 * m + 64, u % 2, m, :],
                                          Qb[64 * m:64 * m + 64, t, i * P:(i + 1) * P]).then_inc(padB, 1)
            pool.wait_ge(tabs, 1)
            pool.wait_ge(h2_out, 16 * NT)
            nblk = pool.value_load(nblk_i[0:1, 0:1], min_val=16, max_val=31)

            def gather(col):
                nc.gpsimd.indirect_dma_start(
                    out=xg[:, :], out_offset=None, in_=h2_d.ap(),
                    in_offset=bass.IndirectOffsetOnAxis(ap=idx_c[:, 0:1], axis=0)).then_inc(gathered, 16)

            nc.gpsimd.tensor_copy(idx_c[:, 0:1], idx_u[:, 0:1]).then_inc(idx_ok, 1)
            pool.wait_ge(idx_ok, 1)
            gather(0)
            with pool.Fori(1, nblk + 1) as b:
                pool.wait_ge(gathered, b * 16)
                nc.gpsimd.tensor_copy(idx_c[:, 0:1], idx_u[:, bass.ds(b, 1)]).then_inc(idx_ok, 1)
                pool.wait_ge(idx_ok, b + 1)
                pool.wait_ge(xg_tr, b)
                pool.sem_inc(pool_go, 1)
                gather(b)
            pool.wait_ge(y_out, nblk * 16 + 16)
            pool.wait_ge(gathered, nblk * 16 + 16)
            pool.wait_ge(xg_tr, nblk + 1)
            pool.sem_inc(pool_go, 1)
            for t in range(NT):
                if t >= 2:
                    pool.wait_ge(comb, 11 * (t - 2) + 2)
                for k in range(2):
                    nc.gpsimd.indirect_dma_start(
                        out=yg[:, t % 2, k, :], out_offset=None, in_=y_d.ap(),
                        in_offset=bass.IndirectOffsetOnAxis(ap=slot_u[:, k, t:t + 1], axis=0)
                    ).then_inc(comb_in[t % 2], 16)

        @block.scalar
        def _(act):
            sm = [(ident[:, :], ident_h), (cc[:, :], c.rearrange("a (k p) -> p (a k)", p=P)),
                  (lamb[:, :, :], bass.AP(lam.tensor, 0, [[0, P], [64, 4], [1, 64]])),
                  (relb[:, :], rel_bias), (flip[:, :], flip_h), (onehot[:, :], onehot_h),
                  (sinkc[:, :], bass.AP(sinks.tensor, 0, [[0, P], [1, H_B]])),
                  (subc[:, :], subln_w.rearrange("a (p o) -> p (a o)", o=1))]
            for dst, src in sm:
                act.dma_start(dst, src).then_inc(small_in, 16)
            for j in range(4):
                act.dma_start(adab[32 * j:32 * j + 32, :, :],
                              bass.AP(ada_b.tensor, j * 512, [[0, 32], [2048, 3], [1, 512]])).then_inc(small_in, 16)
            act.wait_ge(small_in, 192)
            nc.scalar.activation(ce[:, :], cc[:, :], ACT.Exp, scale=-1.0).then_inc(silu_e, 1)
            act.wait_ge(lam_v, 2)
            nc.scalar.activation(lams[:, 2:4], lams[:, 0:2], ACT.Exp).then_inc(lam_e, 1)
            for g in range(3):
                if g % 2:
                    act.wait_ge(btab_mm, g + 1)
                    nc.scalar.copy(btab[:, g * 384:(g + 1) * 384], ps[0:12, (5 + g) * BANK:(5 + g) * BANK + 384]).then_inc(btab_ev, 1)
            act.wait_ge(ln0, 25)
            nc.scalar.activation(rstd[:, :], rstd[:, :], ACT.Sqrt).then_inc(ln0_sq, 1)
            for g in range(1, 12, 2):
                act.wait_ge(flip_mm, g + 1)
                nc.scalar.copy(flip_group(g)[1], bank(5 + g % 3)).then_inc(flip_a, 1)
            act.wait_ge(ss_one, 1)
            for k in range(1, NK, 2):
                act.wait_ge(xt_mm, k + 1)
                nc.scalar.activation(hT[:, k, :], ps[:, (1 + 2 * (k % 3)) * BANK:(3 + 2 * (k % 3)) * BANK], ACT.Identity,
                                     bias=sscol[:, k:k + 1], scale=sscol[:, 8 + k:9 + k]).then_inc(xt_a, 1)
            for g in range(1, NGRP, 2):
                dst, scale = proj_dst(g)
                act.wait_ge(proj_mm, g + 1)
                if g == 1:
                    act.wait_ge(xt_mm, NK)
                    act.wait_ge(btab_out, 16)
                nc.scalar.activation(dst, bank(g % 8), ACT.Copy, scale=scale).then_inc(proj_a, 1)
            for u in range(32 + 2):
                if u < 32:
                    n = P * (u % NT + 1)
                    for m in range(2):
                        act.wait_ge(logitA, 2 * u + m + 1)
                        nc.scalar.activation(L[:, u % 3, m, 0:n], L[:, u % 3, m, 0:n], ACT.Exp, bias=nmA[:, u, m:m + 1],
                                             scale=-1.0, accum_out=smA[:, u, m:m + 1]).then_inc(expA, 1)
                v = u - 2
                if v >= 0:
                    h, i = v // NT, v % NT
                    for g in range(ngrp(i)):
                        w = min(4, i + 1 - 4 * g) * P
                        act.wait_ge(trA, grp0(v) + g + 1)
                        if grp0(v) + g >= 2:
                            act.wait_ge(pvA, pv_of(grp0(v) + g - 2) + 1)
                        nc.scalar.copy(aT[:, (grp0(v) + g) % 2, 0:w], bank(4 + (grp0(v) + g) % 2, w)).then_inc(aT_ev, 1)
                    act.wait_ge(pvA, grp0(v) + ngrp(i))
                    nc.scalar.copy(Qa[:, h, i * P:(i + 1) * P], bank(6, P)).then_inc(oA, 1)
                    act.wait_ge(oA, 2 * v + 1)
                    nc.scalar.activation(junk[:, :], Qa[:, h, i * P:(i + 1) * P], ACT.Square,
                                         accum_out=msA[:, v:v + 1]).then_inc(oA, 1)
            for u in range(32 + 2):
                if u < 32:
                    i = u // 4
                    a = 0 if i else P
                    for j in range(2):
                        act.wait_ge(logitB, 2 * u + j + 1)
                        nc.scalar.activation(LB[:, u % 4, j, a:256], LB[:, u % 4, j, a:256], ACT.Exp, bias=nmB[:, u, j:j + 1],
                                             scale=-1.0, accum_out=smB[:, u, j:j + 1]).then_inc(expB, 1)
                v = u - 2
                if v >= 0:
                    i = v // 4
                    act.wait_ge(trB, v + 1)
                    if v >= 2:
                        act.wait_ge(pvB, v - 1)
                    src = bank(4 + v % 2)
                    if i:
                        nc.scalar.copy(aT[:, v % 2, :], src).then_inc(bT_ev, 1)
                    else:
                        nc.scalar.copy(aT[:, v % 2, 0:256], src[:, 0:256]).then_inc(bT_ev, 1)
            act.wait_ge(fin_v, 1)
            nc.scalar.activation(nmB[:, :, :], nmB[:, :, :], ACT.Exp).then_inc(fin_a, 1)
            act.wait_ge(fin_v, 2)
            nc.scalar.activation(msA[:, :], msA[:, :], ACT.Sqrt).then_inc(fin_a, 1)
            for f in range(1, 16, 2):
                act.wait_ge(finT, f + 1)
                if f < 8:
                    nc.scalar.activation(Qa[:, f // 2, (f % 2) * 512:(f % 2) * 512 + 512], bank(f % 8), ACT.Copy,
                                         scale=subc[:, 0:1]).then_inc(finT_a, 1)
                else:
                    q = f - 8
                    nc.scalar.copy(Qb[:, q // 2, (q % 2) * 512:(q % 2) * 512 + 512], bank(f % 8)).then_inc(finT_a, 1)
            for m in range(16):
                st = m % 2
                for g in range(2):
                    act.wait_ge(merge_mm, 4 * m + g + 1)
                    if m >= 2:
                        act.wait_ge(merged, 3 * (m - 1))
                    nc.scalar.activation(sg[:, st, g, :], bank(4 * st + g), ACT.Sigmoid).then_inc(merge_sg, 1)
            for t in range(NT):
                act.wait_ge(post_v, 18 * t + 6)
                nc.scalar.activation(rstd[:, 0:1], rstd[:, 0:1], ACT.Sqrt).then_inc(post_a, 1)
                act.wait_ge(post_v, 18 * t + 14)
                nc.scalar.activation(rstd[:, 1:2], rstd[:, 1:2], ACT.Sqrt).then_inc(post_a, 1)
                act.wait_ge(h2T_mm, t + 1)
                if t >= 1:
                    act.wait_ge(rout_mm, t)
                nc.scalar.copy(h2T[:, :, :].rearrange("p k q -> p (k q)"), bank(4, BANK, 2)).then_inc(h2T_ev, 1)
            act.wait_ge(rout_ev, NT)
            nc.scalar.activation(s_[:, :, :], lg[:, :, :], ACT.Sigmoid).then_inc(route_a, 1)
            act.wait_ge(tabs, 1)
            act.wait_ge(y_zero, 64)
            nblk = act.value_load(nblk_i[0:1, 0:1], min_val=16, max_val=31)
            xTf = xT[:, :, :].rearrange("p k q -> p (k q)")
            act.wait_ge(xg_tr, 1)
            nc.scalar.copy(xTf[:, 0:512], bank(2)).then_inc(xT_a, 1)
            act.sem_inc(y_out, 16)
            act.sem_inc(y_a, 1)
            with act.Fori(0, nblk) as b:
                act.wait_ge(gate_mm, b + 1)
                nc.scalar.activation(sig[:, :], bank(0), ACT.Sigmoid).then_inc(sig_a, 1)
                act.wait_ge(xg_tr, b + 2)
                nc.scalar.copy(xTf[:, 0:512], bank(2)).then_inc(xT_a, 1)
                act.wait_ge(down_mm, b + 1)
                act.wait_ge(y_out, b * 16 + 16)
                nc.scalar.copy(ysb[:, 0:512], bank(5)).then_inc(y_a, 1)
                act.wait_ge(y_a, b + 2)
                act.wait_ge(y_v, b + 2)
                act.dma_start(y_d[bass.ds(b * P, P), :], ysb[:, :]).then_inc(y_out, 16)
            for t in range(NT):
                act.wait_ge(comb, 11 * t + 8)
                nc.scalar.activation(rstd[:, 0:1], rstd[:, 0:1], ACT.Sqrt).then_inc(comb_a, 1)

        @block.vector
        def _(dve):
            v = nc.vector
            dve.wait_ge(small_in, 192)
            v.tensor_tensor(lamb[:, 0:3:2, :], lamb[:, 0:3:2, :], lamb[:, 1:4:2, :], ALU.mult).then_inc(lam_v, 1)
            dve.wait_ge(lam_v, 1)
            v.tensor_reduce(lams[:, 0:2], lamb[:, 0:3:2, :], AX, ALU.add).then_inc(lam_v, 1)
            dve.wait_ge(silu_e, 1)
            v.tensor_scalar(ce[:, :], ce[:, :], 1.0, None, ALU.add).then_inc(silu_v, 1)
            dve.wait_ge(silu_v, 1)
            v.reciprocal(ce[:, :], ce[:, :]).then_inc(silu_v, 1)
            dve.wait_ge(silu_v, 2)
            v.tensor_tensor(csil[:, :], ce[:, :], cc[:, :], ALU.mult).then_inc(silu_v, 1)
            v.tensor_scalar(negsink[:, :], sinkc[:, :], -1.0, None, ALU.mult).then_inc(lam_v, 1)
            dve.wait_ge(lam_e, 1)
            v.tensor_tensor(lams[:, 0:1], lams[:, 3:4], lams[:, 2:3], ALU.subtract).then_inc(lam_v, 1)
            dve.wait_ge(lam_v, 4)
            v.tensor_scalar(lams[:, 0:1], lams[:, 0:1], -LAM_INIT, None, ALU.add).then_inc(lam_v, 1)
            v.tensor_scalar(subc[:, :], subc[:, :], 1.0 - LAM_INIT, None, ALU.mult).then_inc(lam_v, 1)
            for g in (0, 2):
                dve.wait_ge(btab_mm, g + 1)
                v.tensor_copy(btab[:, g * 384:(g + 1) * 384], ps[0:12, (5 + g) * BANK:(5 + g) * BANK + 384]).then_inc(btab_ev, 1)
            for t in range(NT):
                dve.wait_ge(x_in[t // 2], 16)
                if t >= 2:
                    dve.wait_ge(ln0, 3 * (t - 1))
                for hf in range(2):
                    v.bn_stats(stat[:, t % 2, 6 * hf:6 * hf + 6], xs[:, t, hf * 512:(hf + 1) * 512]).then_inc(ln0, 1)
                dve.wait_ge(ln0, 3 * t + 2)
                v.bn_aggr(mv[:, t, :], stat[:, t % 2, :]).then_inc(ln0, 1)
            dve.wait_ge(ln0, 24)
            v.tensor_scalar(rstd[:, :], mv[:, :, 1], EPS, None, ALU.add).then_inc(ln0, 1)
            dve.wait_ge(ln0_sq, 1)
            v.reciprocal(rstd[:, :], rstd[:, :]).then_inc(ln0, 1)
            dve.wait_ge(ln0, 26)
            for t in range(NT):
                v.tensor_scalar(xs[:, t, :], xs[:, t, :], mv[:, t, 0:1], rstd[:, t:t + 1], ALU.subtract, ALU.mult).then_inc(ln0, 1)
            for g in range(0, 12, 2):
                dve.wait_ge(flip_mm, g + 1)
                v.tensor_copy(flip_group(g)[1], bank(5 + g % 3)).then_inc(flip_v, 1)
            dve.wait_ge(ada_mm, 4)
            v.tensor_tensor(modrow[:, :], bank(0), adab[:, 0, :], ALU.add).then_inc(ada_ev, 1)
            dve.wait_ge(ss_in, 16)
            v.tensor_scalar(sscol[:, 8:16], sscol[:, 8:16], 1.0, None, ALU.add).then_inc(ss_one, 1)
            dve.wait_ge(ss_one, 1)
            for k in range(0, NK, 2):
                dve.wait_ge(xt_mm, k + 1)
                v.tensor_scalar(hT[:, k, :], ps[:, (1 + 2 * (k % 3)) * BANK:(3 + 2 * (k % 3)) * BANK], sscol[:, 8 + k:9 + k],
                                sscol[:, k:k + 1], ALU.mult, ALU.add).then_inc(xt_v, 1)
            for g in range(0, NGRP, 2):
                dst, scale = proj_dst(g)
                dve.wait_ge(proj_mm, g + 1)
                if g == 0:
                    dve.wait_ge(btab_out, 16)
                    dve.wait_ge(xt_mm, NK)
                v.tensor_scalar(dst, bank(g % 8), scale, None, ALU.mult).then_inc(proj_v, 1)
            dve.wait_ge(mask_set, 4)
            for u in range(32 + 1):
                if u < 32:
                    h, i = u // NT, u % NT
                    n = P * (i + 1)
                    for m in range(2):
                        dve.wait_ge(scoreA, 2 * u + m + 1)
                        if u >= 3:
                            dve.wait_ge(trA, grp0(u - 3) + ngrp((u - 3) % NT))
                        if u == 0:
                            dve.wait_ge(proj_mm, NGRP)
                        v.tensor_tensor_reduce(L[:, u % 3, m, 0:n], bank(2 * m, n), biasA[:, h, S - n:S], -1.0, BIG,
                                               ALU.add, ALU.min, nmA[:, u, m:m + 1]).then_inc(logitA, 1)
                w = u - 1
                if w >= 0:
                    n = P * (w % NT + 1)
                    dve.wait_ge(expA, 2 * w + 2)
                    v.reciprocal(smA[:, w, :], smA[:, w, :]).then_inc(attnA, 1)
                    dve.wait_ge(attnA, 4 * w + 1)
                    v.tensor_scalar(smA[:, w, 1:2], smA[:, w, 1:2], lams[:, 0:1], None, ALU.mult).then_inc(attnA, 1)
                    dve.wait_ge(attnA, 4 * w + 2)
                    v.tensor_scalar(L[:, w % 3, 1, 0:n], L[:, w % 3, 1, 0:n], smA[:, w, 1:2], None, ALU.mult).then_inc(attnA, 1)
                    dve.wait_ge(attnA, 4 * w + 3)
                    v.scalar_tensor_tensor(L[:, w % 3, 0, 0:n], L[:, w % 3, 0, 0:n], smA[:, w, 0:1], L[:, w % 3, 1, 0:n],
                                           ALU.mult, ALU.add).then_inc(attnA, 1)
                if u in (15, 31):
                    rd = 1 if u == 15 else 2
                    dve.wait_ge(ada_mm, 4 * (rd + 1))
                    dve.wait_ge(ada_out, 16 * rd)
                    v.tensor_tensor(modrow[:, :], bank(7), adab[:, rd, :], ALU.add).then_inc(ada_ev, 1)
            for u in range(32 + 3):
                if u < 32:
                    i, t = u // 4, u % 4
                    a = 0 if i else P
                    for j in range(2):
                        hd = t + 4 * j
                        dve.wait_ge(scoreB, 2 * u + j + 1)
                        if u >= 4:
                            dve.wait_ge(trB, u - 3)
                        if u == 0:
                            dve.wait_ge(trA, 48)
                        v.tensor_tensor_reduce(LB[:, u % 4, j, a:256], ps[:, (2 * (u % 2) + j) * BANK:(2 * (u % 2) + j) * BANK + 256 - a],
                                               biasB[:, hd, a:256], -1.0, negsink[:, hd:hd + 1],
                                               ALU.add, ALU.min, nmB[:, u, j:j + 1]).then_inc(logitB, 1)
                w = u - 3
                if w >= 0:
                    i, t = w // 4, w % 4
                    dve.wait_ge(pvB, w + 1)
                    src = bank(6 + w % 2, 384).rearrange("p (j n) -> p j n", j=2)[:, :, 0:64]
                    v.tensor_copy(Qb[:, t, i * P:(i + 1) * P].rearrange("p (j n) -> p j n", j=2), src).then_inc(oB, 1)
            dve.wait_ge(expB, 64)
            n4 = nmB[:, :, :].rearrange("p (i t) j -> p i t j", i=NT)
            snk = sinkc[:, :].rearrange("p (j t) -> p t j", j=2)
            cntf = [0]

            def fin(ins):
                cntf[0] += 1
                ins.then_inc(finq, 1)
                dve.wait_ge(finq, cntf[0])

            for i in range(NT - 1):
                fin(v.tensor_tensor(n4[:, i], n4[:, i], snk, ALU.add))
            v.tensor_tensor(n4[:, NT - 1], n4[:, NT - 1], snk, ALU.add).then_inc(fin_v, 1)
            dve.wait_ge(oA, 64)
            v.tensor_scalar(msA[:, :], msA[:, :], 1.0 / P, EPS, ALU.mult, ALU.add).then_inc(fin_v, 1)
            dve.wait_ge(fin_a, 1)
            fin(v.tensor_tensor(smB[:, :, :], smB[:, :, :], nmB[:, :, :], ALU.add))
            fin(v.reciprocal(smB[:, :, :], smB[:, :, :]))
            dve.wait_ge(fin_a, 2)
            fin(v.reciprocal(msA[:, :], msA[:, :]))
            for h in range(H_A):
                qv = Qa[:, h, :].rearrange("p (i n) -> p i n", i=NT)
                v.tensor_tensor(qv, qv, msA[:, h * NT:(h + 1) * NT].unsqueeze(2).to_broadcast([P, NT, P]), ALU.mult).then_inc(fin_v, 1)
            dve.wait_ge(oB, 32)
            s4 = smB[:, :, :].rearrange("p (i t) j -> p t i j", i=NT)
            for t in range(4):
                qv = Qb[:, t, :].rearrange("p (i j n) -> p i j n", i=NT, j=2)
                v.tensor_tensor(qv, qv, s4[:, t].unsqueeze(3).to_broadcast([P, NT, 2, 64]), ALU.mult).then_inc(fin_v, 1)
            for f in range(0, 16, 2):
                dve.wait_ge(finT, f + 1)
                if f < 8:
                    v.tensor_scalar(Qa[:, f // 2, (f % 2) * 512:(f % 2) * 512 + 512], bank(f % 8), subc[:, 0:1], None,
                                    ALU.mult).then_inc(finT_v, 1)
                else:
                    q = f - 8
                    v.tensor_copy(Qb[:, q // 2, (q % 2) * 512:(q % 2) * 512 + 512], bank(f % 8)).then_inc(finT_v, 1)
            for m in range(16):
                st, d, hf = m % 2, m // 2, m % 2
                dve.wait_ge(merge_mm, 4 * m + 4)
                dve.wait_ge(merge_sg, 2 * m + 2)
                for g in range(2):
                    v.tensor_tensor(sg[:, st, g, :], sg[:, st, g, :], bank(4 * st + 2 + g), ALU.mult).then_inc(merged, 1)
                dve.wait_ge(merged, 3 * m + 2)
                v.tensor_tensor(mT[:, d, hf * 512:(hf + 1) * 512], sg[:, st, 0, :], sg[:, st, 1, :], ALU.add).then_inc(merged, 1)
            v.memset(rwp[:, :, :], 0.0).then_inc(rwp_v, 1)
            dve.wait_ge(rwp_v, 1)
            dve.wait_ge(rt_in, 16 * 7)
            v.tensor_copy(rwp[:, :, 0:NE], rw[:, :, :]).then_inc(rwp_v, 1)
            dve.wait_ge(rows_in, 128)
            v.tensor_scalar(rowA[:, 3, :], rowA[:, 3, :], 1.0, None, ALU.add).then_inc(rows_one, 1)
            dve.wait_ge(rows_one, 1)
            for t in range(NT):
                n = [18 * t]

                def st_(ins):
                    n[0] += 1
                    ins.then_inc(post_v, 1)
                    dve.wait_ge(post_v, n[0])

                X = X2[:, t, :]
                dve.wait_ge(y_mm, 2 * t + 2)
                st_(v.tensor_tensor(X, bank(2 * (t % 2), BANK, 2), rowA[:, 0, :], ALU.mult))
                dve.wait_ge(xin_in, 16 * t + 16)
                st_(v.scalar_tensor_tensor(X, xin[:, 0, :], ALPHA, X, ALU.mult, ALU.add))
                for r_ in range(2):
                    for hf in range(2):
                        st_(v.bn_stats(stat[:, 0, 6 * hf:6 * hf + 6], X2[:, t, hf * 512:(hf + 1) * 512]))
                    st_(v.bn_aggr(mv[:, 0, :], stat[:, 0, :]))
                    st_(v.tensor_scalar(rstd[:, r_:r_ + 1], mv[:, 0, 1:2], EPS, None, ALU.add))
                    dve.wait_ge(post_a, 2 * t + r_ + 1)
                    st_(v.reciprocal(rstd[:, r_:r_ + 1], rstd[:, r_:r_ + 1]))
                    if r_ == 0:
                        st_(v.tensor_scalar(X, X, mv[:, 0, 0:1], rstd[:, 0:1], ALU.subtract, ALU.mult))
                        st_(v.tensor_tensor(X, X, rowA[:, 1, :], ALU.mult))
                        st_(v.tensor_tensor(X, X, rowA[:, 2, :], ALU.add))
                    else:
                        Hh = h2[:, t % 2, :]
                        if t >= 2:
                            dve.wait_ge(h2_out, 16 * (t - 1))
                            dve.wait_ge(h2T_mm, t - 1)
                        st_(v.tensor_scalar(Hh, X, mv[:, 0, 0:1], rstd[:, 1:2], ALU.subtract, ALU.mult))
                        st_(v.tensor_tensor(Hh, Hh, rowA[:, 3, :], ALU.mult))
                        st_(v.tensor_tensor(Hh, Hh, rowB[:, 3, :], ALU.add))
                if t >= 1:
                    dve.wait_ge(rout_mm, t)
                    v.tensor_copy(lg[:, t - 1, :], ps[:, 6 * BANK:6 * BANK + NE]).then_inc(rout_ev, 1)
            dve.wait_ge(rout_mm, NT)
            v.tensor_copy(lg[:, NT - 1, :], ps[:, 6 * BANK:6 * BANK + NE]).then_inc(rout_ev, 1)
            q = [0]

            def ro(ins):
                q[0] += 1
                ins.then_inc(route, 1)
                dve.wait_ge(route, q[0])

            def b3(row, n):
                return row.unsqueeze(1).to_broadcast([P, NT, n])

            dve.wait_ge(rt_in, 16 * 7)
            ro(v.memset(ones[:, :], 1.0))
            dve.wait_ge(route_a, 1)
            ro(v.tensor_tensor(bi[:, :, :], s_[:, :, :], b3(rbias[:, :], NE), ALU.add))
            b4 = bi[:, :, :].rearrange("p t (g e) -> p t g e", g=NG)
            ro(v.tensor_tensor(g0_[:, :, :], b4[:, :, :, 0], b4[:, :, :, 1], ALU.max))
            ro(v.tensor_tensor(g1_[:, :, :], b4[:, :, :, 0], b4[:, :, :, 1], ALU.min))
            ro(v.tensor_tensor(g2_[:, :, :], b4[:, :, :, 2], b4[:, :, :, 3], ALU.max))
            ro(v.tensor_tensor(g3_[:, :, :], b4[:, :, :, 2], b4[:, :, :, 3], ALU.min))
            ro(v.tensor_tensor(g4_[:, :, :], g0_[:, :, :], g2_[:, :, :], ALU.min))
            ro(v.tensor_tensor(g1_[:, :, :], g1_[:, :, :], g3_[:, :, :], ALU.max))
            ro(v.tensor_tensor(g1_[:, :, :], g1_[:, :, :], g4_[:, :, :], ALU.max))
            ro(v.tensor_tensor(g0_[:, :, :], g0_[:, :, :], g2_[:, :, :], ALU.max))
            ro(v.tensor_tensor(g0_[:, :, :], g0_[:, :, :], g1_[:, :, :], ALU.add))

            def first_max(dst, src, n, revrow):
                ro(v.tensor_reduce(m1[:, :], src, AX, ALU.max))
                ro(v.tensor_tensor(dst, src, m1[:, :].unsqueeze(2).to_broadcast([P, NT, n]), ALU.is_equal))
                ro(v.tensor_tensor(dst, dst, b3(revrow, n), ALU.mult))
                ro(v.tensor_reduce(m1[:, :], dst, AX, ALU.max))
                ro(v.tensor_tensor(dst, dst, m1[:, :].unsqueeze(2).to_broadcast([P, NT, n]), ALU.is_equal))

            first_max(g2_[:, :, :], g0_[:, :, :], NG, rev[:, NE:NE + NG])
            gb = g2_[:, :, :].unsqueeze(3).to_broadcast([P, NT, NG, EPG])
            t14 = t1[:, :, :].rearrange("p t (g e) -> p t g e", g=NG)
            t04 = t0[:, :, :].rearrange("p t (g e) -> p t g e", g=NG)
            for t in range(NT):
                ro(v.tensor_tensor(t04[:, t], b4[:, t], gb[:, t], ALU.mult))
            ro(v.tensor_scalar(g3_[:, :, :], g2_[:, :, :], -1.0, 1e30, ALU.add, ALU.mult))
            gb3 = g3_[:, :, :].unsqueeze(3).to_broadcast([P, NT, NG, EPG])
            for t in range(NT):
                ro(v.tensor_tensor(t04[:, t], t04[:, t], gb3[:, t], ALU.add))
            first_max(oh[0][:, :, :], t0[:, :, :], NE, rev[:, 0:NE])
            ro(v.scalar_tensor_tensor(t0[:, :, :], oh[0][:, :, :], -2e30, t0[:, :, :], ALU.mult, ALU.add))
            first_max(oh[1][:, :, :], t0[:, :, :], NE, rev[:, 0:NE])
            for k in range(2):
                ro(v.tensor_tensor(t1[:, :, :], oh[k][:, :, :], s_[:, :, :], ALU.mult))
                ro(v.tensor_reduce(ms_[:, k, :], t1[:, :, :], AX, ALU.add))
            ro(v.tensor_tensor(m1[:, :], ms_[:, 0, :], ms_[:, 1, :], ALU.add))
            ro(v.reciprocal(m1[:, :], m1[:, :]))
            for k in range(2):
                ro(v.tensor_tensor(wk[:, k, :], ms_[:, k, :], m1[:, :], ALU.mult))
            ro(v.tensor_tensor(t1[:, :, :], oh[0][:, :, :], oh[1][:, :, :], ALU.add))
            ro(v.memset(Mex[:, 0, :], 0.0))
            for t in range(1, NT):
                ro(v.tensor_tensor(Mex[:, t, :], Mex[:, t - 1, :], t1[:, t - 1, :], ALU.add))
            ro(v.tensor_tensor(nb_[:, :], Mex[:, NT - 1, :], t1[:, NT - 1, :], ALU.add))
            RANK_READY[0] = q[0]
            dve.wait_ge(rank_mm, 1)
            ro(v.tensor_copy(rank[:, :, :].rearrange("p t e -> p (t e)"), bank(0, P)))
            dve.wait_ge(rank_mm, 2)
            ro(v.tensor_copy(cnt[:, :], bank(1, NE)))
            c3 = c8[:, 0:NE * 8].rearrange("p (e j) -> p e j", j=8)
            ro(v.tensor_scalar(mul8[:, :], iota[:, 0:8], 128.0, None, ALU.mult))
            ro(v.tensor_tensor(c3, cnt[:, :].unsqueeze(2).to_broadcast([P, NE, 8]),
                               mul8[:, :].unsqueeze(1).to_broadcast([P, NE, 8]), ALU.is_gt))
            ro(v.tensor_reduce(nb_[:, :], c3, AX, ALU.add))
            bg = big[:, 0:NE, :]
            ro(v.tensor_tensor(bg, before[:, :, :], nb_[:, :].unsqueeze(1).to_broadcast([P, NE, NE]), ALU.mult))
            ro(v.tensor_reduce(pst[:, :], bg, AX, ALU.add))
            ro(v.tensor_tensor(pen[:, :], pst[:, :], nb_[:, :], ALU.add))
            for k in range(2):
                ro(v.tensor_tensor(t1[:, :, :], oh[k][:, :, :], rank[:, :, :], ALU.mult))
                ro(v.tensor_reduce(Rk[:, k, :], t1[:, :, :], AX, ALU.add))
                ro(v.tensor_tensor(t1[:, :, :], oh[k][:, :, :], b3(pst[:, :], NE), ALU.mult))
                ro(v.tensor_reduce(Pk[:, k, :], t1[:, :, :], AX, ALU.add))
            c4 = c8[:, :].rearrange("p (a j) -> p a j", j=8)
            Rf = Rk[:, :, :].rearrange("p k t -> p (k t)")
            rf = rb_[:, :, :].rearrange("p k t -> p (k t)")
            Pf = Pk[:, :, :].rearrange("p k t -> p (k t)")
            ro(v.tensor_tensor(c4, Rf.unsqueeze(2).to_broadcast([P, 16, 8]),
                               mul8[:, :].unsqueeze(1).to_broadcast([P, 16, 8]), ALU.is_ge))
            ro(v.tensor_reduce(rf, c4, AX, ALU.add))
            ro(v.tensor_scalar(rf, rf, -1.0, None, ALU.add))
            ro(v.tensor_tensor(Pf, Pf, rf, ALU.add))
            ro(v.scalar_tensor_tensor(Rf, rf, -128.0, Rf, ALU.mult, ALU.add))
            ro(v.scalar_tensor_tensor(rf, Pf, 128.0, Rf, ALU.mult, ALU.add))
            ro(v.tensor_copy(slot_u[:, :, :].rearrange("p k t -> p (k t)"), rf))
            for a in range(16):
                t = a % NT
                ro(v.tensor_scalar(Aoh[:, a, :], iota[:, :], Rf[:, a:a + 1], None, ALU.is_equal))
                ro(v.tensor_scalar(Boh[:, a, :], iota[:, 0:MAXBLK], Pf[:, a:a + 1], tokid[:, t:t + 1],
                                   ALU.is_equal, ALU.mult))
            OH_READY[0] = q[0]
            ro(v.tensor_tensor(big[:, :, :], iota[:, 0:MAXBLK].unsqueeze(2).to_broadcast([P, MAXBLK, NE]),
                               pen[:, :].unsqueeze(1).to_broadcast([P, MAXBLK, NE]), ALU.is_ge))
            ro(v.tensor_reduce(ef[:, :], big[:, :, :], AX, ALU.add))
            ro(v.tensor_scalar(ef[:, :], ef[:, :], 1.0, 16.0, ALU.add, ALU.min))
            ro(v.tensor_copy(blk_e[:, :], ef[:, :]))
            ro(v.tensor_copy(nblk_i[:, :], pen[:, NE - 1:NE]))
            ro(v.tensor_scalar(pen[:, :], pen[:, :], 1.0, None, ALU.add))
            ro(v.tensor_copy(pend_i[:, :], pen[:, :]))
            dve.wait_ge(idx_mm, 1)
            v.tensor_copy(idx_u[:, :], bank(2, MAXBLK)).then_inc(tabs, 1)
            dve.wait_ge(tabs, 1)
            nblk = dve.value_load(nblk_i[0:1, 0:1], min_val=16, max_val=31)
            xTf = xT[:, :, :].rearrange("p k q -> p (k q)")
            dve.wait_ge(xg_tr, 1)
            v.tensor_copy(xTf[:, 512:1024], bank(3)).then_inc(xT_v, 1)
            dve.sem_inc(y_v, 1)
            with dve.Fori(0, nblk) as b:
                dve.wait_ge(sig_a, b + 1)
                v.tensor_tensor(sig[:, :], sig[:, :], bank(0), ALU.mult).then_inc(glu_v, 1)
                dve.wait_ge(glu_v, b + 1)
                dve.wait_ge(up_mm, b + 1)
                v.tensor_tensor(hh[:, :], sig[:, :], bank(1), ALU.mult).then_inc(hh_v, 1)
                dve.wait_ge(hh_tr, b + 1)
                v.tensor_copy(hhT[:, :, :].rearrange("p k q -> p (k q)"), bank(4)).then_inc(hhT_v, 1)
                dve.wait_ge(xg_tr, b + 2)
                v.tensor_copy(xTf[:, 512:1024], bank(3)).then_inc(xT_v, 1)
                dve.wait_ge(down_mm, b + 1)
                dve.wait_ge(y_out, b * 16 + 16)
                v.tensor_copy(ysb[:, 512:1024], bank(6)).then_inc(y_v, 1)
            for t in range(NT):
                n = [11 * t]

                def cb(ins):
                    n[0] += 1
                    ins.then_inc(comb, 1)
                    dve.wait_ge(comb, n[0])

                A_, B_, R = yg[:, t % 2, 0, :], yg[:, t % 2, 1, :], r2[:, t % 2, :]
                dve.wait_ge(comb_in[t % 2], 32 * (t // 2 + 1))
                if t >= 2:
                    dve.wait_ge(res_out[t % 2], 16 * (t // 2))
                cb(v.tensor_scalar(R, A_, wk[:, 0, t:t + 1], None, ALU.mult))
                cb(v.scalar_tensor_tensor(R, B_, wk[:, 1, t:t + 1], R, ALU.mult, ALU.add))
                cb(v.tensor_tensor(R, R, rowB[:, 0, :], ALU.mult))
                cb(v.scalar_tensor_tensor(R, X2[:, t, :], ALPHA, R, ALU.mult, ALU.add))
                for hf in range(2):
                    cb(v.bn_stats(stat[:, 0, 6 * hf:6 * hf + 6], r2[:, t % 2, hf * 512:(hf + 1) * 512]))
                cb(v.bn_aggr(mv[:, 0, :], stat[:, 0, :]))
                cb(v.tensor_scalar(rstd[:, 0:1], mv[:, 0, 1:2], EPS, None, ALU.add))
                dve.wait_ge(comb_a, t + 1)
                v.reciprocal(rstd[:, 0:1], rstd[:, 0:1]).then_inc(comb_r, 1)
                dve.wait_ge(comb_r, t + 1)
                cb(v.tensor_scalar(R, R, mv[:, 0, 0:1], rstd[:, 0:1], ALU.subtract, ALU.mult))
                cb(v.tensor_tensor(R, R, rowB[:, 1, :], ALU.mult))
                cb(v.tensor_tensor(R, R, rowB[:, 2, :], ALU.add))

        @block.tensor
        def _(pe):
            mm = nc.tensor.matmul
            pe.wait_ge(small_in, 192)
            for g in range(3):
                mm(ps[0:12, (5 + g) * BANK:(5 + g) * BANK + 384], relb[:, :], onehot[:, g * 384:(g + 1) * 384],
                   start=True, stop=True).then_inc(btab_mm, 1)

            def ada(ch, cidx, b):
                arrived(pe, cidx)
                w = cview(cidx)[:, :].rearrange("p (k n) -> p k n", k=2)
                for kk in range(2):
                    k = 2 * (ch % 4) + kk
                    for j in range(4):
                        last = mm(ps[32 * j:32 * j + 32, b * BANK:(b + 1) * BANK], csil[:, k:k + 1].to_broadcast([P, 32]),
                                  w[:, kk, j * 512:(j + 1) * 512], start=(k == 0), stop=(k == NK - 1), skip_group_check=True)
                last.then_inc(ada_mm, 1)

            pe.wait_ge(silu_v, 3)
            for ch in range(4):
                ada(ch, ch, 0)
                if ch == 2:
                    pe.wait_ge(btab_in, 32)
                    pe.wait_ge(btab_ev, 3)
                    for g in range(12):
                        if g >= 3:
                            pe.wait_ge((flip_v, flip_a)[(g - 3) % 2], (g - 3) // 2 + 1)
                        mm(bank(5 + g % 3), flip[:, :], flip_group(g)[0], start=True, stop=True).then_inc(flip_mm, 1)
            pe.wait_ge(ln0, 26 + NT)
            pe.wait_ge(flip_v, 6)
            pe.wait_ge(flip_a, 6)
            for k in range(NK):
                if k >= 3:
                    kk = k - 3
                    pe.wait_ge((xt_v, xt_a)[kk % 2], kk // 2 + 1)
                b0 = 1 + 2 * (k % 3)
                for t in range(NT):
                    last = nc.tensor.transpose(ps[:, b0 * BANK + t * P:b0 * BANK + (t + 1) * P], xs[:, t, k * P:(k + 1) * P], ident[:, :])
                last.then_inc(xt_mm, 1)
            pe.wait_ge(xt_v, 4)
            pe.wait_ge(xt_a, 4)
            for g, (pi, kind, q) in enumerate(groups):
                if g == 0 or groups[g - 1][0] != pi:
                    arrived(pe, 4 + pi)
                n = PROJ[pi][2]
                w = cview(4 + pi)[:, 0:NK * n].rearrange("p (k n) -> p k n", k=NK)
                if g >= 8:
                    pe.wait_ge((proj_v, proj_a)[g % 2], (g - 8) // 2 + 1)
                out_ = bank(g % 8)
                if kind == "vb":
                    for t4 in range(4):
                        t = 4 * q + t4
                        for k in range(NK):
                            last = mm(out_[:, t4 * P:(t4 + 1) * P], hT[:, k, t * P:(t + 1) * P], w[:, k, P:2 * P], start=(k == 0), stop=(k == NK - 1))
                    last.then_inc(proj_mm, 1)
                    continue
                for k in range(NK):
                    if kind == "va":
                        l_, r_ = hT[:, k, q * P:(q + 1) * P], w[:, k, :]
                    else:
                        r_ = hT[:, k, (q % 2) * 512:(q % 2) * 512 + 512]
                        if kind == "kb":
                            l_ = w[:, k, 0:P]
                        else:
                            l_ = w[:, k, (q // 2) * P:(q // 2 + 1) * P]
                    last = mm(out_, l_, r_, start=(k == 0), stop=(k == NK - 1))
                last.then_inc(proj_mm, 1)
            pe.wait_ge(proj_v, NGRP // 2)
            pe.wait_ge(proj_a, NGRP // 2)
            for u in range(32 + 2):
                if u < 32:
                    h, i = u // NT, u % NT
                    n = P * (i + 1)
                    pe.wait_ge(padA, 2 * u + 2)
                    for m in range(2):
                        if u >= 1:
                            pe.wait_ge(logitA, 2 * (u - 1) + m + 1)
                        for c0 in range(0, n, 512):
                            w = min(512, n - c0)
                            last = mm(ps[:, 2 * m * BANK + c0:2 * m * BANK + c0 + w], qpad[:, u % 2, m, :], Ka[:, h, c0:c0 + w], start=True, stop=True)
                        last.then_inc(scoreA, 1)
                v = u - 2
                if v >= 0:
                    h, i = v // NT, v % NT
                    pe.wait_ge(attnA, 4 * v + 4)
                    for g in range(ngrp(i)):
                        gg = grp0(v) + g
                        if gg >= 2:
                            pe.wait_ge(aT_ev, gg - 1)
                        for kt in range(4 * g, min(4 * g + 4, i + 1)):
                            last = nc.tensor.transpose(ps[:, (4 + gg % 2) * BANK + (kt % 4) * P:(4 + gg % 2) * BANK + (kt % 4 + 1) * P],
                                                       L[:, v % 3, 0, kt * P:(kt + 1) * P], ident[:, :])
                        last.then_inc(trA, 1)
                    for g in range(ngrp(i)):
                        gg = grp0(v) + g
                        pe.wait_ge(aT_ev, gg + 1)
                        if g == 0 and v >= 1:
                            pe.wait_ge(oA, 2 * (v - 1) + 1)
                        for kt in range(4 * g, min(4 * g + 4, i + 1)):
                            last = mm(bank(6, P), aT[:, gg % 2, (kt % 4) * P:(kt % 4 + 1) * P], Va[:, kt, h * P:(h + 1) * P],
                                      start=(kt == 0), stop=(kt == i))
                        last.then_inc(pvA, 1)
                if u % 4 == 3 and u < 32:
                    ch = 4 + u // 4
                    if ch == 8:
                        pe.wait_ge(ada_ev, 2)
                    ada(ch, C_ADA2 + u // 4, 7)
            pe.wait_ge(ada_ev, 3)
            pe.wait_ge(oA, 63)
            for u in range(32 + 2):
                if u < 32:
                    i, t = u // 4, u % 4
                    pe.wait_ge(padB, 2 * u + 2)
                    k0 = max(0, (i - 1) * P)
                    n = (i + 1) * P - k0
                    for j in range(2):
                        if u >= 2:
                            pe.wait_ge(logitB, 2 * (u - 2) + j + 1)
                        b0 = (2 * (u % 2) + j) * BANK
                        mm(ps[:, b0:b0 + n], qpad[:, u % 2, j, :], Kb[:, k0:k0 + n], start=True, stop=True).then_inc(scoreB, 1)
                v = u - 2
                if v >= 0:
                    i, t = v // 4, v % 4
                    nt = 2 if i else 1
                    pe.wait_ge(expB, 2 * v + 2)
                    if v >= 2:
                        pe.wait_ge(bT_ev, v - 1)
                    for j in range(2):
                        for kt in range(nt):
                            col = (4 + v % 2) * BANK + (j * nt + kt) * P
                            last = nc.tensor.transpose(ps[:, col:col + P], LB[:, v % 4, j, (2 - nt + kt) * P:(3 - nt + kt) * P], ident[:, :])
                    last.then_inc(trB, 1)
                    pe.wait_ge(bT_ev, v + 1)
                    if v >= 2:
                        pe.wait_ge(oB, v - 1)
                    for j in range(2):
                        for kt in range(nt):
                            last = mm(ps[:, (6 + v % 2) * BANK + j * P:(6 + v % 2) * BANK + (j + 1) * P], aT[:, v % 2, (j * nt + kt) * P:(j * nt + kt + 1) * P],
                                      Vb[:, i - nt + 1 + kt, :], start=(kt == 0), stop=(kt == nt - 1))
                    last.then_inc(pvB, 1)
            pe.wait_ge(logitB, 64)
            pe.wait_ge(bT_ev, 32)
            for f in range(16):
                src, q = (Qa, f) if f < 8 else (Qb, f - 8)
                pe.wait_ge(fin_v, 3 + (f // 2 if f < 8 else 4 + q // 2))
                if f >= 8:
                    pe.wait_ge((finT_v, finT_a)[f % 2], (f - 8) // 2 + 1)
                for i4 in range(4):
                    i = 4 * (q % 2) + i4
                    last = nc.tensor.transpose(ps[:, (f % 8) * BANK + i4 * P:(f % 8) * BANK + (i4 + 1) * P], src[:, q // 2, i * P:(i + 1) * P], ident[:, :])
                last.then_inc(finT, 1)
            pe.wait_ge(finT_v, 8)
            pe.wait_ge(finT_a, 8)
            for m in range(16):
                d, hf, st = m // 2, m % 2, m % 2
                if m % 4 == 0:
                    arrived(pe, C_G + m // 4)
                w = cview(C_G + m // 4)[:, :].rearrange("p (k g n) -> p k g n", k=NK, g=2)
                if m == 0:
                    pe.wait_ge(wab_in, 48)
                if m >= 2:
                    pe.wait_ge(merged, 3 * (m - 1))
                dc = (d % 2) * P
                for g in range(2):
                    for k in range(NK):
                        last = mm(bank(4 * st + g), w[:, k, g, dc:dc + P], hT[:, k, hf * 512:(hf + 1) * 512], start=(k == 0), stop=(k == NK - 1))
                    last.then_inc(merge_mm, 1)
                for g, (wt, oT) in enumerate(((wa, Qa), (wb, Qb))):
                    for k in range(4):
                        last = mm(bank(4 * st + 2 + g), wt[:, k, d * P:(d + 1) * P], oT[:, k, hf * 512:(hf + 1) * 512], start=(k == 0), stop=(k == 3))
                    last.then_inc(merge_mm, 1)
            pe.wait_ge(merged, 48)
            arrived(pe, C_O)
            for t in range(NT + 1):
                if t < NT:
                    if t >= 2:
                        pe.wait_ge(post_v, 18 * (t - 2) + 1)
                    for n in range(2):
                        if t == 0 and n == 1:
                            arrived(pe, C_O + 1)
                        w = cview(C_O + n)[:, :].rearrange("p (k n) -> p k n", k=NK)
                        for k in range(NK):
                            last = mm(bank(2 * (t % 2) + n), mT[:, k, t * P:(t + 1) * P], w[:, k, :], start=(k == 0), stop=(k == NK - 1))
                        last.then_inc(y_mm, 1)
                if t >= 1:
                    s = t - 1
                    pe.wait_ge(post_v, 18 * (s + 1))
                    if s >= 1:
                        pe.wait_ge(h2T_ev, s)
                    for k in range(NK):
                        last = nc.tensor.transpose(ps[:, 4 * BANK + k * P:4 * BANK + (k + 1) * P], h2[:, s % 2, k * P:(k + 1) * P], ident[:, :])
                    last.then_inc(h2T_mm, 1)
                    pe.wait_ge(h2T_ev, s + 1)
                    pe.wait_ge(rwp_v, 2)
                    if s >= 1:
                        pe.wait_ge(rout_ev, s)
                    for k in range(NK):
                        last = mm(bank(6, P), h2T[:, k, :], rwp[:, k, :], start=(k == 0), stop=(k == NK - 1))
                    last.then_inc(rout_mm, 1)
            pe.wait_ge(route, RANK_READY[0])
            t1f = t1[:, :, :].rearrange("p t e -> p (t e)")
            mm(bank(0, P), lower[:, :], t1f, start=True, stop=False)
            mm(bank(0, P), ones[:, :], Mex[:, :, :].rearrange("p t e -> p (t e)"), start=False, stop=True).then_inc(rank_mm, 1)
            mm(bank(1, NE), ones[:, :], nb_[:, :], start=True, stop=True).then_inc(rank_mm, 1)
            pe.wait_ge(route, OH_READY[0])
            for a in range(16):
                last = mm(bank(2, MAXBLK), Aoh[:, a, :], Boh[:, a, :], start=(a == 0), stop=(a == 15))
            last.then_inc(idx_mm, 1)
            pe.wait_ge(tabs, 1)
            nblk = pe.value_load(nblk_i[0:1, 0:1], min_val=16, max_val=31)

            def transpose_rows():
                for k in range(NK):
                    last = nc.tensor.transpose(ps[:, 2 * BANK + k * P:2 * BANK + (k + 1) * P], xg[:, k * P:(k + 1) * P], ident[:, :])
                last.then_inc(xg_tr, 1)

            pe.wait_ge(gathered, 16)
            transpose_rows()
            with pe.Fori(0, nblk) as b:
                e1 = pe.value_load(blk_e[0:1, bass.ds(b, 1)], min_val=1, max_val=NE)
                off = (e1 % 2) * EVEN
                pe.wait_ge(exp_ready, e1)
                pe.wait_ge(xT_a, b + 1)
                pe.wait_ge(xT_v, b + 1)
                for wi, done in enumerate((gate_mm, up_mm)):
                    for k in range(NK):
                        last = mm(bank(wi), xT[:, k, :], EXP[:, bass.ds(off + (wi * 4096 + k * 512), 512)], start=(k == 0), stop=(k == NK - 1))
                    last.then_inc(done, 1)
                pe.wait_ge(hh_v, b + 1)
                for k in range(4):
                    last = nc.tensor.transpose(ps[:, 4 * BANK + k * P:4 * BANK + (k + 1) * P], hh[:, k * P:(k + 1) * P], ident[:, :])
                last.then_inc(hh_tr, 1)
                pe.wait_ge(gathered, b * 16 + 32)
                transpose_rows()
                pe.wait_ge(hhT_v, b + 1)
                pe.wait_ge(y_a, b + 1)
                pe.wait_ge(y_v, b + 1)
                for k in range(4):
                    for n in range(2):
                        last = mm(bank(5 + n), hhT[:, k, :], EXP[:, bass.ds(off + (8192 + k * 1024 + n * 512), 512)], start=(k == 0), stop=(k == 3))
                last.then_inc(down_mm, 1)


_INS = ["x", "c", "ada_w", "ada_b", "w_in", "lam", "subln_w", "sinks", "w_branch_a", "w_branch_b", "w_out",
        "ln_g", "ln_b", "rel_bias", "router_w", "router_b", "exp_w1", "exp_w3", "exp_w2"]


def _constants():
    import math

    import numpy as np

    rel = np.arange(TAB) - 1023
    nb = NBUCKET // 2
    exact = nb // 2
    n = np.abs(rel)
    far = exact + (np.log(np.maximum(n, 1).astype(np.float32) / np.float32(exact)) / np.float32(math.log(1024 / exact))
                   * np.float32(nb - exact)).astype(np.int32)
    bucket = np.where(rel > 0, nb, 0) + np.where(n < exact, n, np.minimum(far, nb - 1))
    f = np.float32
    i = np.arange(P)
    rows = lambda v: np.ascontiguousarray(np.broadcast_to(np.asarray(v, f).reshape(1, -1), (P, np.size(v))))
    e = np.arange(NE)
    return {
        "ident": np.eye(P, dtype=f),
        "onehot": (bucket[None, :] == np.arange(NBUCKET)[:, None]).astype(f),
        "lower": (i[:, None] < i[None, :]).astype(f),
        "iota": rows(i),
        "rev": rows(np.concatenate([NE - e, NG - np.arange(NG)])),
        "before": rows(e[None, :] < e[:, None]),
        "tokid": (i[:, None] + P * np.arange(NT)[None, :]).astype(f),
        "flip": np.ascontiguousarray(np.eye(P, dtype=f)[::-1]),
    }


def kernel(**inputs):
    import numpy as _np
    import concourse.bacc as _bacc
    from concourse import mybir as _mybir
    from concourse.bass_utils import run_bass_kernel_spmd as _run

    nc = _bacc.Bacc("TRN2", target_bir_lowering=False, num_devices=1)
    arrays, args = {}, []
    named = [(n, inputs[n]) for n in _INS] + list(_constants().items())
    for name, value in named:
        a = _np.ascontiguousarray(value)
        arrays[f"in_{name}_dram"] = a
        args.append(nc.dram_tensor(f"in_{name}_dram", a.shape, _mybir.dt.from_np(a.dtype), kind="ExternalInput").ap())
    args.append(nc.dram_tensor("out_0_dram", (1, S, D), F32, kind="ExternalOutput").ap())
    mixer_moe_kernel(nc, *args)
    r = _run(nc, [arrays], core_ids=[0])
    return r.results[0]["out_0_dram"]
```

```python
from contextlib import ExitStack

import concourse.bass as bass
from concourse import mybir

F32 = mybir.dt.float32
F32R = mybir.dt.float32r
U32 = mybir.dt.uint32
I32 = mybir.dt.int32
ALU = mybir.AluOpType
ACT = mybir.ActivationFunctionType
AX = mybir.AxisListType.X

P = 128
D = 1024
S = 1024
NT = S // P
NK = D // P
BANK = 512
H_A, H_B = 4, 8
QA, KA, VA, QB, KVB = 512, 512, 512, 512, 256
COL_Q, COL_K, COL_V, COL_QB, COL_KB = 0, 512, 1024, 1536, 2048
COL_G = 2304
NBUCKET = 32
TAB = 1152
ALPHA = 2.0 ** 0.25
LAM_INIT = 0.8 - 0.6
EPS = 1e-5
NEG = -1.0e30
BIG = 3.0e38
NE, NG, EPG = 16, 4, 4
FE = 512
MAXBLK = 32
KB = 256
SQ = 0.125


def mixer_moe_kernel(nc, x, c, ada_w, ada_b, w_in, lam, subln_w, sinks, w_a, w_b, w_out,
                     ln_g, ln_b, rel_bias, router_w, router_b, w1, w3, w2,
                     ident_h, onehot_h, lower_h, iota_h, rev_h, before_h, tokid_h, flip_h, out):
    base = (nc.sbuf_base + 63) // 64 * 64

    def at(name, kib, shape, dt=F32):
        return nc.alloc_sbuf_tensor_at(name, shape, dt, offset=base + int(kib * 1024))

    ctx = ExitStack()
    with ctx:
        ctx.enter_context(nc.allow_non_contiguous_dma(reason="columns of a few hundred bytes"))

        def sem(name):
            return ctx.enter_context(nc.semaphore(name))

        bias_d = nc.dram_tensor("bias_by_distance", [12, TAB], F32)
        mod_d = nc.dram_tensor("ada_mod", [12, BANK], F32)
        h2_d = nc.dram_tensor("moe_input", [S, D], F32)
        gate_d = nc.dram_tensor("gates", [2 * NK, 2, P, BANK], F32)
        y_d = nc.dram_tensor("expert_rows", [MAXBLK * P, D], F32)

        o = [0.0]

        def packed(start, limit):
            at_ = [start]

            def place(name, shape, dt=F32):
                n = 1
                for v in shape[1:]:
                    n *= v
                t = at(name, at_[0], shape, dt)
                at_[0] += (n * 4 + 31) // 32 * 32 / 1024
                assert at_[0] <= limit, (name, at_[0])
                return t

            return place

        small = packed(0, 4)
        ident = small("ident", [P, P])
        cc = small("cc", [P, NK])
        csil = small("csil", [P, NK])
        ce = small("ce", [P, NK])
        sscol = small("sscol", [P, 16])
        negsink = small("negsink", [P, H_B])
        sinkc = small("sinkc", [P, H_B])
        lamb = small("lamb", [P, 4, 64])
        lams = small("lams", [P, 4])
        subc = small("subc", [P, 1])
        mv = small("mv", [P, NT, 2])
        rstd = small("rstd", [P, NT])
        nmr = small("nmr", [P, 4])
        stat = small("stat", [P, 2, 12])
        nmA = small("nmA", [P, 32, 2])
        smA = small("smA", [P, 32, 2])
        msA = small("msA", [P, 32])
        qpad = at("qpad", 4, [P, 2, 2, P])
        adab = at("adab", 6, [P, BANK])
        A0 = at("A0", 168, [P, 4096])
        A1 = at("A1", 184, [P, 4096])
        A2 = at("A2", 120, [P, 4096])
        xs = at("xs", 72, [P, NT, D])
        onehot = at("onehot", 40, [NBUCKET, TAB])
        relb = at("relb", 45, [NBUCKET, 12])
        btab = at("btab", 46, [12, TAB])
        flip = at("flip", 51, [P, P])
        skewA = at("skewA", 104, [P, H_A, S])
        skewB = at("skewB", 136, [P, H_B, 256])
        hraw = at("hraw", 120, [P, 2, S])
        hTh = at("hTh", 8, [P, NK, S], F32R)
        hTl = at("hTl", 40, [P, NK, S], F32R)
        Qa = at("Qa", 72, [P, H_A, S])
        Ka = at("Ka", 88, [P, H_A, S])
        Va = at("Va", 104, [P, NT, VA])
        Qb = at("Qb", 120, [P, 4, S])
        Kb = at("Kb", 136, [P, S])
        Vb = at("Vb", 140, [P, NT, P])
        biasA = at("biasA", 144, [P, H_A, S])
        biasB = at("biasB", 160, [P, H_B, 256])
        WR = [at(f"WR{i}", 168 + 16 * i, [P, 2048]) for i in range(2)]
        WL = [at(f"WL{i}", 168 + 16 * i, [P, 2048], F32R) for i in range(2)]
        WH = [at(f"WH{i}", 176 + 16 * i, [P, 2048], F32R) for i in range(2)]
        gst = at("gst", 200, [P, 2, BANK])
        vbT = at("vbT", 200, [P, S])
        modrow = at("modrow", 204, [P, BANK])
        zero1k = at("zero1k", 206, [P, 256])
        L = at("L", 8, [P, 3, 2, S])
        LB = at("LB", 8, [P, 4, 2, 256])
        aT = at("aT", 32, [P, 4, BANK])
        A3 = at("A3", 40, [P, 4096])
        A4 = at("A4", 56, [P, 4096])
        nmB = at("nmB", 200, [P, 32, 2])
        smB = at("smB", 200.5, [P, 32, 2])
        junk = at("junk", 201, [P, P])
        Oh = at("Oh", 8, [P, NK, S], F32R)
        Ol = at("Ol", 40, [P, NK, S], F32R)
        gin = at("gin", 136, [P, 2, 2, BANK])
        mTh = at("mTh", 72, [P, NK, S], F32R)
        mTl = at("mTl", 104, [P, NK, S], F32R)
        WOR = [at("WOR0", 144, [P, NK, BANK]), at("WOR1", 24, [P, NK, BANK])]
        WOL = [at("WOL0", 144, [P, NK, BANK], F32R), at("WOL1", 24, [P, NK, BANK], F32R)]
        WOH = [at("WOH0", 8, [P, NK, BANK], F32R), at("WOH1", 40, [P, NK, BANK], F32R)]
        X2 = at("X2", 168, [P, NT, D])
        rowA = at("rowA", 56, [P, 4, D])
        sh2 = at("sh2", 136, [P, D])
        xin = at("xin", 140, [P, 1, D])
        h2 = at("h2", 160, [P, 2, D])
        h2T = at("h2T", 200, [P, NK, P])
        rwz = at("rwz", 4, [P, 16, NE])
        lg = at("lg", 206, [P, NT, NE])
        cst = packed(5, 8)
        lower = cst("lower", [P, P])
        iota = cst("iota", [P, P])
        before = cst("before", [P, NE, NE])
        rev = cst("rev", [P, NE + NG])
        tokid = cst("tokid", [P, NT])
        rbias = cst("rbias", [P, NE])
        mul8 = cst("mul8", [P, 8])
        keep = packed(204, 206)
        wk = keep("wk", [P, 2, NT])
        slot_u = keep("slot_u", [P, 2, NT], U32)
        idx_u = keep("idx_u", [P, MAXBLK], U32)
        blk_e = keep("blk_e", [P, MAXBLK], I32)
        pend_i = keep("pend_i", [P, NE], I32)
        nblk_i = keep("nblk_i", [P, 1], I32)
        idx_c = keep("idx_c", [P, 1], U32)
        rt = packed(120, 136)
        s_ = rt("sco", [P, NT, NE])
        bi = rt("bia", [P, NT, NE])
        t0 = rt("t0", [P, NT, NE])
        t1 = rt("t1", [P, NT, NE])
        oh = [rt("oh0", [P, NT, NE]), rt("oh1", [P, NT, NE])]
        g0_, g1_, g2_, g3_, g4_ = (rt(f"g{i}", [P, NT, NG]) for i in range(5))
        m1 = rt("m1", [P, NT])
        ms_ = rt("ms", [P, 2, NT])
        Mex = rt("Mex", [P, NT, NE])
        rank = rt("rank", [P, NT, NE])
        cnt = rt("cnt", [P, NE])
        nb_ = rt("nb", [P, NE])
        pst = rt("pst", [P, NE])
        pen = rt("pen", [P, NE])
        big = rt("big", [P, MAXBLK, NE])
        ef = rt("ef", [P, MAXBLK])
        Rk = rt("Rk", [P, 2, NT])
        Pk = rt("Pk", [P, 2, NT])
        rb_ = rt("rb", [P, 2, NT])
        c8 = rt("c8", [P, 2 * NT * 8])
        ones = rt("ones", [P, P])
        Aoh = at("Aoh", 144, [P, 16, P])
        Boh = at("Boh", 152, [P, 16, MAXBLK])
        EXP = at("EXP", 8, [P, 28 * 1024])
        ODD, EVEN = 0, 64 * KB
        rowB = at("rowB", 56, [P, 3, D])
        xg = at("xg", 144, [P, D])
        xT = at("xT", 148, [P, NK, P])
        sig = at("sig", 152, [P, FE])
        hh = at("hh", 154, [P, FE])
        hhT = at("hhT", 156, [P, 4, P])
        ysb = at("ysb", 158, [P, D])
        yg = at("yg", 144, [P, 2, 2, D])
        r2 = at("r2", 160, [P, 2, D])

        ps = ctx.enter_context(nc.psum_tensor("ps", [P, 8 * BANK], F32))

        def bank(b, n=BANK, w=1):
            return ps[:, b * BANK:b * BANK + (w - 1) * BANK + n]

        small_in = sem("small_in")
        x_in = [sem(f"x_in{i}") for i in range(4)]
        slot_in = {n: sem(f"slot_in_{n}") for n in ("A0", "A1", "A2", "A3", "A4", "R0", "R1")}
        w_hi, w_lo = sem("w_hi"), sem("w_lo")
        h_hi, gst_out = sem("h_hi"), [sem("gst_out0"), sem("gst_out1")]
        gin_in = [sem("gin_in0"), sem("gin_in1")]
        wo_in, wo_hi, wo_lo = [sem("wo_in0"), sem("wo_in1")], sem("wo_hi"), sem("wo_lo")
        c_in, adab_in = sem("c_in"), sem("adab_in")
        padz = sem("padz")
        silu_e, silu_v = sem("silu_e"), sem("silu_v")
        ln0, ln0_sq = sem("ln0"), sem("ln0_sq")
        btab_mm, btab_ev, btab_out, btab_in, mask_set = (sem("btab_mm"), sem("btab_ev"), sem("btab_out"),
                                                         sem("btab_in"), sem("mask_set"))
        flip_mm, flip_v, flip_a, zero_set, y_zero, pool_go = (sem("flip_mm"), sem("flip_v"), sem("flip_a"),
                                                              sem("zero_set"), sem("y_zero"), sem("pool_go"))
        lam_v, lam_e = sem("lam_v"), sem("lam_e")
        ada_mm, ada_ev, ada_out, ss_in, ss_one = (sem("ada_mm"), sem("ada_ev"), sem("ada_out"), sem("ss_in"),
                                                  sem("ss_one"))
        xt_mm, xt_a = sem("xt_mm"), sem("xt_a")
        o_hi = sem("o_hi")
        proj_mm, proj_v, proj_a = sem("proj_mm"), sem("proj_v"), sem("proj_a")
        padA, scoreA, logitA, expA, attnA, trA, aT_ev, pvA, oA = (sem("padA"), sem("scoreA"), sem("logitA"), sem("expA"), sem("attnA"),
                                                    sem("trA"), sem("aT_ev"), sem("pvA"), sem("oA"))
        padB, scoreB, logitB, expB, trB, bT_ev, pvB, oB = (sem("padB"), sem("scoreB"), sem("logitB"), sem("expB"), sem("trB"),
                                             sem("bT_ev"), sem("pvB"), sem("oB"))
        fin_v, fin_a, finT, finT_v = sem("fin_v"), sem("fin_a"), sem("finT"), sem("finT_v")
        merge_mm, merged = sem("merge_mm"), sem("merged")
        rows_in, rows_one, rowB_in = sem("rows_in"), sem("rows_one"), sem("rowB_in")
        xin_in, y_mm, post_v, post_a, h2_out = (sem("xin_in"), sem("y_mm"), sem("post_v"), sem("post_a"),
                                                sem("h2_out"))
        h2T_mm, h2T_ev, rout_mm, rout_ev, rwp_v = (sem("h2T_mm"), sem("h2T_ev"), sem("rout_mm"), sem("rout_ev"),
                                                   sem("rwp_v"))
        rt_in, route, route_a, rank_mm, idx_mm, tabs = (sem("rt_in"), sem("route"), sem("route_a"), sem("rank_mm"),
                                                        sem("idx_mm"), sem("tabs"))
        exp_even, exp_odd, exp_ready = sem("exp_even"), sem("exp_odd"), sem("exp_ready")
        idx_ok, gathered, xg_tr, xT_v, xT_a = (sem("idx_ok"), sem("gathered"), sem("xg_tr"), sem("xT_v"),
                                               sem("xT_a"))
        gate_mm, up_mm, sig_a, glu_v, hh_v, hh_tr, hhT_v = (sem("gate_mm"), sem("up_mm"), sem("sig_a"),
                                                            sem("glu_v"), sem("hh_v"), sem("hh_tr"),
                                                            sem("hhT_v"))
        down_mm, y_v, y_a, y_out = sem("down_mm"), sem("y_v"), sem("y_a"), sem("y_out")
        comb_in = [sem("comb_in0"), sem("comb_in1")]
        finq, comb_r = sem("finq"), sem("comb_r")
        RANK_READY, OH_READY = [0], [0]
        comb, comb_a, res_out = sem("comb"), sem("comb_a"), [sem("res_out0"), sem("res_out1")]

        w_rows = w_in.rearrange("a (k p) n -> p (a k) n", p=P)
        ada_rows = ada_w.rearrange("a s (k p) n -> p (a s) k n", p=P)
        wo_rows = w_out.rearrange("a (k p) n -> p (a k) n", p=P)
        wa_rows = w_a.rearrange("a (k p) n -> p (a k) n", p=P)
        wb_rows = w_b.rearrange("a (j t p) n -> j p (a t) n", j=2, p=64)
        NA_CH = 12
        adas = {"A0": A0, "A1": A1, "A2": A2, "A3": A3, "A4": A4}
        ADA_SLOT = ["A0", "A1", "A2", "A0"] + ["A3", "A4"] * 4

        def ada_src(ch):
            rd, kp = ch // 4, ch % 4
            c0 = rd * 2048
            parts = []
            while c0 < (rd + 1) * 2048:
                sub, off = c0 // 3072, c0 % 3072
                n = min(3072 - off, (rd + 1) * 2048 - c0)
                parts.append((c0 - rd * 2048, n, ada_rows[:, sub, 2 * kp:2 * kp + 2, off:off + n]))
                c0 += n
            return parts

        chunks = ([("va", i) for i in range(2)] + [("ka", i) for i in range(2)] + [("qa", i) for i in range(2)]
                  + [("kv", 0)] + [("qb", i) for i in range(2)] + [("gl", i) for i in range(8)]
                  + [("br", i) for i in range(4)])
        NPC = 17
        COL = {"va": COL_V, "ka": COL_K, "qa": COL_Q, "kv": COL_KB, "qb": COL_QB, "gl": COL_G}
        groups = []
        for ci in range(NPC):
            kind, i = chunks[ci]
            for q in range(4):
                k2 = ("kb" if q < 2 else "vb") if kind == "kv" else kind
                eng_ = "a" if kind == "gl" or len(groups) % 2 else "v"
                groups.append((ci, k2, 4 * i + q if kind != "kv" else q % 2, eng_))
            if ci == 8:
                groups += [(ci, "vt", 0, "v"), (ci, "vt", 1, "a")]
        NGRP = len(groups)
        NVG = sum(g[3] == "v" for g in groups)
        NAG = NGRP - NVG

        LAST = [max(g for g in range(NGRP) if groups[g][0] == ci) for ci in range(NPC)]

        def used(eng, ci):
            if ci < NPC:
                eng.wait_ge(proj_mm, LAST[ci] + 1)
            else:
                eng.wait_ge(merge_mm, 8 * (ci - NPC + 1))

        def taken(g):
            return sum(x[3] == groups[g][3] for x in groups[:g + 1])

        def chunk_src(ci):
            kind, i = chunks[ci]
            if kind == "br":
                lo_ = WR[ci % 2][:, :].rearrange("p (g k n) -> p g k n", g=2, k=4)
                c0 = i * 256
                return [(lo_[:, 0], wa_rows[:, :, c0:c0 + 256])] + [
                    (lo_[64 * j:64 * j + 64, 1], wb_rows[j][:, :, c0:c0 + 256]) for j in range(2)]
            v = WR[ci % 2][:, :].rearrange("p (k n) -> p k n", k=NK)
            c0 = COL[kind]
            if kind == "qb":
                return [(v[:, :, (2 * t + j) * 64:(2 * t + j + 1) * 64],
                         w_rows[:, :, c0 + (4 * j + 2 * i + t) * 64:c0 + (4 * j + 2 * i + t + 1) * 64])
                        for t in range(2) for j in range(2)]
            return [(v[:, :, :], w_rows[:, :, c0 + i * 256:c0 + (i + 1) * 256])]

        def chunk_in(eng, ci):
            n = sum(len(chunk_src(q)) for q in range(ci % 2, ci + 1, 2))
            eng.wait_ge(slot_in[f"R{ci % 2}"], 16 * n)

        def ada_in(eng, ch):
            n = sum(len(ada_src(q)) for q in range(ch + 1) if ADA_SLOT[q] == ADA_SLOT[ch])
            eng.wait_ge(slot_in[ADA_SLOT[ch]], 16 * n)

        def ngrp(i):
            return i // 4 + 1

        def grp0(v):
            return (v // NT) * 12 + sum(ngrp(i) for i in range(v % NT))

        def proj_dst(g):
            _, kind, q, _ = groups[g]
            if kind == "va":
                return Va[:, 2 * (q % 4):2 * (q % 4) + 2, (q // 4) * 256:(q // 4) * 256 + 256], 1.0
            cols = slice((q % 2) * 512, (q % 2) * 512 + 512)
            if kind == "ka":
                return Ka[:, q // 2, cols], 1.0
            if kind == "qa":
                return Qa[:, q // 2, cols], SQ
            if kind == "qb":
                return Qb[:, q // 2, cols], SQ
            if kind == "kb":
                return Kb[:, cols], 1.0
            if kind == "vb":
                return vbT[:, cols], 1.0
            if kind == "vt":
                return Vb[:, 4 * q:4 * q + 4, :].rearrange("p t n -> p (t n)"), 1.0
            raise ValueError(kind)

        def flip_group(g):
            if g < 8:
                return (skewA[:, g // 2, (g % 2) * 512:(g % 2) * 512 + 512], biasA[:, g // 2, (g % 2) * 512:(g % 2) * 512 + 512])
            g -= 8
            return (skewB[:, 2 * g:2 * g + 2, :].rearrange("p h n -> p (h n)"),
                    biasB[:, 2 * g:2 * g + 2, :].rearrange("p h n -> p (h n)"))

        block = ctx.enter_context(nc.Block())

        def bc(row, n=P):
            return bass.AP(row.tensor, row.offset, [[0, n]] + [list(v) for v in row.ap[-1:]])

        def load_adab(eng, rd):
            for j in range(4):
                eng.dma_start(adab[32 * j:32 * j + 32, :], bass.AP(ada_b.tensor, (4 * rd + j) * 512, [[0, 32], [1, 512]])
                              ).then_inc(adab_in, 16)

        @block.sync
        def _(sp):
            xr = x.rearrange("a (t p) d -> p (a t) d", p=P)

            def load_ada(ch):
                slot = ADA_SLOT[ch]
                prev = [q for q in range(ch) if ADA_SLOT[q] == slot]
                if prev:
                    sp.wait_ge(ada_mm, prev[-1] + 1)
                v = adas[slot][:, :].rearrange("p (k n) -> p k n", k=2)
                for a, n, src in ada_src(ch):
                    sp.dma_start(v[:, :, a:a + n], src).then_inc(slot_in[slot], 16)

            def load_chunk(ci):
                if ci >= 2:
                    used(sp, ci - 2)
                for dst, src in chunk_src(ci):
                    sp.dma_start(dst, src).then_inc(slot_in[f"R{ci % 2}"], 16)

            for i in range(4):
                sp.dma_start(xs[:, 2 * i:2 * i + 2, :], xr[:, 2 * i:2 * i + 2, :]).then_inc(x_in[i], 16)
                if i < 3:
                    load_ada(i)
            sp.wait_ge(btab_ev, 3)
            sp.dma_start(bias_d.ap(), btab[:, :]).then_inc(btab_out, 16)
            sp.wait_ge(btab_out, 16)
            sp.dma_start(skewA[:, :, :], bass.AP(bias_d, 0, [[1, P], [TAB, H_A], [1, S]])).then_inc(btab_in, 16)
            sp.dma_start(skewB[:, :, :], bass.AP(bias_d, H_A * TAB + 768, [[1, P], [TAB, H_B], [1, 256]])).then_inc(btab_in, 16)
            load_ada(3)
            sp.wait_ge(ada_mm, 4)
            load_chunk(0)
            load_chunk(1)
            sp.wait_ge(ada_ev, 1)
            sp.dma_start(mod_d[0:4, :], modrow[0:P:32, :]).then_inc(ada_out, 16)
            sp.wait_ge(ada_out, 16)
            sp.dma_start(sscol[:, :], bass.AP(mod_d, 0, [[1, P], [P, 16]])).then_inc(ss_in, 16)
            load_adab(sp, 1)
            for ci in range(2, NPC + 2):
                load_chunk(ci)
            used(sp, NPC - 1)
            load_ada(4)
            load_ada(5)
            sp.wait_ge(zero_set, 1)
            for q in range(4):
                sp.dma_start(y_d[16 * P:MAXBLK * P, q * 256:(q + 1) * 256].rearrange("(a p) n -> p a n", p=P),
                             zero1k[:, :].unsqueeze(1).to_broadcast([P, 16, 256])).then_inc(y_zero, 16)
            for ch in range(6, NA_CH):
                load_ada(ch)
                if ch == 9:
                    sp.wait_ge(ada_ev, 2)
                    sp.dma_start(mod_d[4:8, :], modrow[0:P:32, :]).then_inc(ada_out, 16)
                    load_adab(sp, 2)
            sp.wait_ge(ada_ev, 3)
            sp.dma_start(mod_d[8:12, :], modrow[0:P:32, :]).then_inc(ada_out, 16)
            sp.wait_ge(logitA, 64)
            sp.dma_start(WOR[0][:, :, :], wo_rows[:, :, 0:512]).then_inc(wo_in[0], 16)
            sp.wait_ge(gst_out[0], 16 * 16)
            sp.wait_ge(gst_out[1], 16 * 16)
            sp.wait_ge(pvB, 32)
            for m in range(16):
                if m >= 2:
                    sp.wait_ge(merged, 5 * (m - 1))
                for g in range(2):
                    sp.dma_start(gin[:, m % 2, g, :], gate_d[g * NK + m // 2, m % 2]).then_inc(gin_in[m % 2], 16)
                if m in (4, 8):
                    load_chunk(NPC + 2 + (m // 4 - 1))
            for dst, src in [(rwz[:, 0:NK, :], router_w.rearrange("(k p) e -> p k e", p=P)), (lower[:, :], lower_h),
                             (iota[:, :], iota_h), (rev[:, :], rev_h),
                             (before[:, :, :], before_h.rearrange("p (a b) -> p a b", a=NE)),
                             (tokid[:, :], tokid_h), (rbias[:, :], bass.AP(router_b.tensor, 0, [[0, P], [1, NE]]))]:
                sp.dma_start(dst, src).then_inc(rt_in, 16)
            sp.wait_ge(merge_mm, 32)
            sp.dma_start(WOR[1][:, :, :], wo_rows[:, :, 512:1024]).then_inc(wo_in[1], 16)
            sp.wait_ge(ada_out, 48)

            def row(dst, src, signal):
                sp.dma_start(dst, bass.AP(src.tensor, src.offset, [[0, P], [1, D]])).then_inc(signal, 16)

            row(rowA[:, 0, :], mod_d[4:6, :], rows_in)
            row(rowA[:, 1, :], ln_g[0, 0], rows_in)
            row(rowA[:, 2, :], ln_b[0, 0], rows_in)
            row(rowA[:, 3, :], mod_d[8:10, :], rows_in)
            sp.wait_ge(merged, 80)
            row(sh2[:, :], mod_d[6:8, :], rows_in)
            w1r = w1.rearrange("a e (k p) n -> p (a e) k n", p=P)
            w3r = w3.rearrange("a e (k p) n -> p (a e) k n", p=P)
            w2r = w2.rearrange("a e (k p) n -> p (a e) k n", p=P)

            def load_expert(e, where, signal):
                for wi, (src, k) in enumerate(((w1r, NK), (w3r, NK), (w2r, 4))):
                    dst = EXP[:, where + wi * 4096:where + (wi + 1) * 4096].rearrange("p (k n) -> p k n", k=k)
                    sp.dma_start(dst, src[:, bass.ds(e, 1), :, :].rearrange("p e k n -> p (e k) n")
                                 ).then_inc(signal, 16)

            xt = x.rearrange("a (t p) d -> t p (a d)", p=P)
            for t in range(NT):
                if t >= 1:
                    sp.wait_ge(post_v, 18 * (t - 1) + 2)
                sp.dma_start(xin[:, 0, :], xt[t]).then_inc(xin_in, 16)
                if t >= 1:
                    sp.wait_ge(post_v, 18 * t)
                    sp.dma_start(h2_d[(t - 1) * P:t * P, :], h2[:, (t - 1) % 2, :]).then_inc(h2_out, 16)
            sp.wait_ge(y_mm, 2 * NT)
            load_expert(0, EVEN, exp_even)
            load_expert(1, ODD, exp_odd)
            sp.wait_ge(post_v, 18 * NT)
            sp.dma_start(h2_d[(NT - 1) * P:NT * P, :], h2[:, (NT - 1) % 2, :]).then_inc(h2_out, 16)
            row(rowB[:, 0, :], mod_d[10:12, :], rowB_in)
            row(rowB[:, 1, :], ln_g[0, 1], rowB_in)
            row(rowB[:, 2, :], ln_b[0, 1], rowB_in)
            sp.wait_ge(tabs, 1)
            sp.wait_ge(exp_even, 48)
            sp.sem_inc(exp_ready, 1)
            with sp.Fori(1, NE // 2) as pr:
                sp.wait_ge(exp_odd, pr * 48)
                sp.sem_inc(exp_ready, 1)
                end = sp.value_load(pend_i[0:1, bass.ds(pr * 2 - 2, 1)], min_val=1, max_val=MAXBLK)
                sp.wait_ge(y_v, end)
                load_expert(pr * 2, EVEN, exp_even)
                sp.wait_ge(exp_even, pr * 48 + 48)
                sp.sem_inc(exp_ready, 1)
                end2 = sp.value_load(pend_i[0:1, bass.ds(pr * 2 - 1, 1)], min_val=1, max_val=MAXBLK)
                sp.wait_ge(y_v, end2)
                load_expert(pr * 2 + 1, ODD, exp_odd)
            sp.wait_ge(exp_odd, 48 * NE // 2)
            sp.sem_inc(exp_ready, 1)
            for t in range(NT):
                sp.wait_ge(comb, 11 * (t + 1))
                sp.dma_start(out.rearrange("a (t p) d -> t p (a d)", p=P)[t], r2[:, t % 2, :]).then_inc(res_out[t % 2], 16)
            sp.wait_ge(res_out[0], 16 * NT // 2)
            sp.wait_ge(res_out[1], 16 * NT // 2)
            sp.wait_ge(ada_out, 48)
            sp.wait_ge(h2_out, 16 * NT)

        @block.gpsimd
        def _(pool):
            nc.gpsimd.memset(qpad[:, :, :, :], 0.0).then_inc(padz, 1)
            pool.wait_ge(padz, 1)
            pool.wait_ge(flip_v, 6)
            pool.wait_ge(flip_a, 6)
            nc.gpsimd.memset(biasA[0:64, :, S - 64:S], NEG).then_inc(mask_set, 1)
            for n_, region in enumerate((biasB[0:64, :, 0:64], biasB[0:64, :, 192:256], biasB[64:128, :, 0:128])):
                pool.wait_ge(mask_set, n_ + 1)
                nc.gpsimd.memset(region, NEG).then_inc(mask_set, 1)
            pool.wait_ge(mask_set, 4)
            nc.gpsimd.memset(zero1k[:, :], 0.0).then_inc(zero_set, 1)
            pool.wait_ge(proj_v, NVG)
            pool.wait_ge(proj_a, NAG)
            for u in range(32):
                h, i = u // NT, u % NT
                if u >= 2:
                    pool.wait_ge(scoreA, 2 * (u - 1))
                for m in range(2):
                    pool.wait_ge(*((padA, 2 * u + m) if u + m else (zero_set, 1)))
                    nc.gpsimd.tensor_copy(qpad[64 * m:64 * m + 64, u % 2, m, :],
                                          Qa[64 * m:64 * m + 64, h, i * P:(i + 1) * P]).then_inc(padA, 1)
            for u in range(32):
                i, t = u // 4, u % 4
                pool.wait_ge(scoreA, 64) if u == 0 else None
                if u >= 2:
                    pool.wait_ge(scoreB, 2 * (u - 1))
                for m in range(2):
                    pool.wait_ge(*((padB, 2 * u + m) if u + m else (padA, 64)))
                    nc.gpsimd.tensor_copy(qpad[64 * m:64 * m + 64, u % 2, m, :],
                                          Qb[64 * m:64 * m + 64, t, i * P:(i + 1) * P]).then_inc(padB, 1)
            pool.wait_ge(tabs, 1)
            pool.wait_ge(h2_out, 16 * NT)
            nblk = pool.value_load(nblk_i[0:1, 0:1], min_val=16, max_val=31)

            def gather(col):
                nc.gpsimd.indirect_dma_start(
                    out=xg[:, :], out_offset=None, in_=h2_d.ap(),
                    in_offset=bass.IndirectOffsetOnAxis(ap=idx_c[:, 0:1], axis=0)).then_inc(gathered, 16)

            nc.gpsimd.tensor_copy(idx_c[:, 0:1], idx_u[:, 0:1]).then_inc(idx_ok, 1)
            pool.wait_ge(idx_ok, 1)
            gather(0)
            with pool.Fori(1, nblk + 1) as b:
                pool.wait_ge(gathered, b * 16)
                nc.gpsimd.tensor_copy(idx_c[:, 0:1], idx_u[:, bass.ds(b, 1)]).then_inc(idx_ok, 1)
                pool.wait_ge(idx_ok, b + 1)
                pool.wait_ge(xg_tr, b)
                pool.sem_inc(pool_go, 1)
                gather(b)
            pool.wait_ge(y_out, nblk * 16 + 16)
            pool.wait_ge(gathered, nblk * 16 + 16)
            pool.wait_ge(xg_tr, nblk + 1)
            pool.sem_inc(pool_go, 1)
            for t in range(NT):
                if t >= 2:
                    pool.wait_ge(comb, 11 * (t - 2) + 2)
                for k in range(2):
                    nc.gpsimd.indirect_dma_start(
                        out=yg[:, t % 2, k, :], out_offset=None, in_=y_d.ap(),
                        in_offset=bass.IndirectOffsetOnAxis(ap=slot_u[:, k, t:t + 1], axis=0)
                    ).then_inc(comb_in[t % 2], 16)

        @block.scalar
        def _(act):
            act.dma_start(cc[:, :], c.rearrange("a (k p) -> p (a k)", p=P)).then_inc(c_in, 16)
            for dst, src in [(relb[:, :], rel_bias), (onehot[:, :], onehot_h), (flip[:, :], flip_h), (ident[:, :], ident_h),
                             (lamb[:, :, :], bass.AP(lam.tensor, 0, [[0, P], [64, 4], [1, 64]])),
                             (sinkc[:, :], bass.AP(sinks.tensor, 0, [[0, P], [1, H_B]])),
                             (subc[:, :], subln_w.rearrange("a (p o) -> p (a o)", o=1))]:
                act.dma_start(dst, src).then_inc(small_in, 16)
            load_adab(act, 0)
            act.wait_ge(c_in, 16)
            nc.scalar.activation(ce[:, :], cc[:, :], ACT.Exp, scale=-1.0).then_inc(silu_e, 1)
            act.wait_ge(lam_v, 2)
            nc.scalar.activation(lams[:, 2:4], lams[:, 0:2], ACT.Exp).then_inc(lam_e, 1)
            act.wait_ge(btab_mm, 2)
            nc.scalar.copy(btab[:, 384:768], ps[0:12, 6 * BANK:6 * BANK + 384]).then_inc(btab_ev, 1)
            act.wait_ge(ln0, 25)
            nc.scalar.activation(rstd[:, :], rstd[:, :], ACT.Sqrt).then_inc(ln0_sq, 1)
            for g in range(1, 12, 2):
                act.wait_ge(flip_mm, g + 1)
                nc.scalar.copy(flip_group(g)[1], bank(5 + g % 3)).then_inc(flip_a, 1)
            act.wait_ge(ss_one, 1)
            for k in range(NK):
                act.wait_ge(xt_mm, k + 1)
                if k >= 2:
                    act.wait_ge(h_hi, 2 * (k - 1))
                nc.scalar.activation(hraw[:, k % 2, :], ps[:, (1 + 2 * (k % 3)) * BANK:(3 + 2 * (k % 3)) * BANK],
                                     ACT.Identity, bias=sscol[:, k:k + 1], scale=sscol[:, 8 + k:9 + k]).then_inc(xt_a, 1)

            def high(ci):
                chunk_in(act, ci)
                if ci >= 2:
                    used(act, ci - 2)
                nc.scalar.copy(WH[ci % 2][:, :], WR[ci % 2][:, :]).then_inc(w_hi, 1)

            high(0)
            high(1)
            for g, (ci, kind, q, eng_) in enumerate(groups):
                if eng_ == "a":
                    act.wait_ge(proj_mm, g + 1)
                    if kind == "gl":
                        d, hf = q // 2, q % 2
                        n = d * 2 + hf
                        if n >= 2:
                            act.wait_ge(gst_out[n % 2], 16 * (n // 2))
                        nc.scalar.activation(gst[:, n % 2, :], bank(g % 8), ACT.Sigmoid).then_inc(proj_a, 1)
                        act.wait_ge(proj_a, taken(g))
                        act.dma_start(gate_d[d, hf], gst[:, n % 2, :]).then_inc(gst_out[n % 2], 16)
                    else:
                        dst, scale = proj_dst(g)
                        src = bank(g % 8)
                        if kind == "va":
                            src = src.rearrange("p (t n) -> p t n", t=2)
                        nc.scalar.activation(dst, src, ACT.Copy, scale=scale).then_inc(proj_a, 1)
                if g == LAST[ci]:
                    high(ci + 2)
            act.wait_ge(gst_out[0], 16 * 16)
            act.wait_ge(gst_out[1], 16 * 16)
            for u in range(32 + 3):
                v = u - 2
                if 0 <= v < 32:
                    i = v % NT
                    for g in range(ngrp(i)):
                        gg = grp0(v) + g
                        w = min(4, i + 1 - 4 * g) * P
                        act.wait_ge(trA, gg + 1)
                        if gg >= 4:
                            act.wait_ge(pvA, gg - 3)
                        nc.scalar.copy(aT[:, gg % 4, 0:w], bank(4 + gg % 2, w)).then_inc(aT_ev, 1)
                v = u - 3
                if v >= 0:
                    h, i = v // NT, v % NT
                    act.wait_ge(pvA, grp0(v) + ngrp(i))
                    nc.scalar.copy(Qa[:, h, i * P:(i + 1) * P], bank(6, P)).then_inc(oA, 1)
                    act.wait_ge(oA, 2 * v + 1)
                    nc.scalar.activation(junk[:, :], Qa[:, h, i * P:(i + 1) * P], ACT.Square,
                                         accum_out=msA[:, v:v + 1]).then_inc(oA, 1)
                if u < 32:
                    n = P * (u % NT + 1)
                    for m in range(2):
                        act.wait_ge(logitA, 2 * u + m + 1)
                        nc.scalar.activation(L[:, u % 3, m, 0:n], L[:, u % 3, m, 0:n], ACT.Exp, bias=nmA[:, u, m:m + 1],
                                             scale=-1.0, accum_out=smA[:, u, m:m + 1]).then_inc(expA, 1)
            for u in range(32 + 2):
                v = u - 2
                if v >= 0:
                    act.wait_ge(trB, v + 1)
                    if v >= 4:
                        act.wait_ge(pvB, v - 3)
                    n = BANK if v // 4 else 256
                    nc.scalar.copy(aT[:, v % 4, 0:n], bank(4 + v % 2, n)).then_inc(bT_ev, 1)
                if u < 32:
                    i = u // 4
                    a = 0 if i else P
                    for j in range(2):
                        act.wait_ge(logitB, 2 * u + j + 1)
                        nc.scalar.activation(LB[:, u % 4, j, a:256], LB[:, u % 4, j, a:256], ACT.Exp, bias=nmB[:, u, j:j + 1],
                                             scale=-1.0, accum_out=smB[:, u, j:j + 1]).then_inc(expB, 1)
            act.wait_ge(fin_v, 1)
            nc.scalar.activation(nmB[:, :, :], nmB[:, :, :], ACT.Exp).then_inc(fin_a, 1)
            act.wait_ge(fin_v, 2)
            nc.scalar.activation(msA[:, :], msA[:, :], ACT.Sqrt).then_inc(fin_a, 1)
            for f in range(16):
                act.wait_ge(finT, f + 1)
                cols = slice((f % 2) * 512, (f % 2) * 512 + 512)
                if f < 8:
                    nc.scalar.activation(Oh[:, f // 2, cols], bank(f % 8), ACT.Copy, scale=subc[:, 0:1]).then_inc(o_hi, 1)
                else:
                    nc.scalar.copy(Oh[:, f // 2, cols], bank(f % 8)).then_inc(o_hi, 1)
            for ci in (NPC + 2, NPC + 3):
                high(ci)
            act.wait_ge(merge_mm, 32)
            for n in range(2):
                act.wait_ge(wo_in[n], 16)
                for k in range(NK):
                    nc.scalar.copy(WOH[n][:, k, :], WOR[n][:, k, :]).then_inc(wo_hi, 1)
            for t in range(NT):
                act.wait_ge(post_v, 18 * t + 6)
                nc.scalar.activation(rstd[:, 0:1], rstd[:, 0:1], ACT.Sqrt).then_inc(post_a, 1)
                act.wait_ge(post_v, 18 * t + 14)
                nc.scalar.activation(rstd[:, 1:2], rstd[:, 1:2], ACT.Sqrt).then_inc(post_a, 1)
                act.wait_ge(h2T_mm, t + 1)
                if t >= 1:
                    act.wait_ge(rout_mm, t)
                nc.scalar.copy(h2T[:, :, :].rearrange("p k q -> p (k q)"), bank(4, BANK, 2)).then_inc(h2T_ev, 1)
            act.wait_ge(rout_ev, NT)
            nc.scalar.activation(s_[:, :, :], lg[:, :, :], ACT.Sigmoid).then_inc(route_a, 1)
            act.wait_ge(tabs, 1)
            act.wait_ge(y_zero, 64)
            nblk = act.value_load(nblk_i[0:1, 0:1], min_val=16, max_val=31)
            xTf = xT[:, :, :].rearrange("p k q -> p (k q)")
            act.wait_ge(xg_tr, 1)
            nc.scalar.copy(xTf[:, 0:512], bank(2)).then_inc(xT_a, 1)
            act.sem_inc(y_out, 16)
            act.sem_inc(y_a, 1)
            with act.Fori(0, nblk) as b:
                act.wait_ge(gate_mm, b + 1)
                nc.scalar.activation(sig[:, :], bank(0), ACT.Sigmoid).then_inc(sig_a, 1)
                act.wait_ge(xg_tr, b + 2)
                nc.scalar.copy(xTf[:, 0:512], bank(2)).then_inc(xT_a, 1)
                act.wait_ge(down_mm, b + 1)
                act.wait_ge(y_out, b * 16 + 16)
                nc.scalar.copy(ysb[:, 0:512], bank(5)).then_inc(y_a, 1)
                act.wait_ge(y_a, b + 2)
                act.wait_ge(y_v, b + 2)
                act.dma_start(y_d[bass.ds(b * P, P), :], ysb[:, :]).then_inc(y_out, 16)
            for t in range(NT):
                act.wait_ge(comb, 11 * t + 8)
                nc.scalar.activation(rstd[:, 0:1], rstd[:, 0:1], ACT.Sqrt).then_inc(comb_a, 1)

        @block.vector
        def _(dve):
            v = nc.vector
            dve.wait_ge(silu_e, 1)
            v.tensor_scalar(ce[:, :], ce[:, :], 1.0, None, ALU.add).then_inc(silu_v, 1)
            dve.wait_ge(silu_v, 1)
            v.reciprocal(ce[:, :], ce[:, :]).then_inc(silu_v, 1)
            dve.wait_ge(silu_v, 2)
            v.tensor_tensor(csil[:, :], ce[:, :], cc[:, :], ALU.mult).then_inc(silu_v, 1)
            dve.wait_ge(small_in, 112)
            v.tensor_tensor(lamb[:, 0:3:2, :], lamb[:, 0:3:2, :], lamb[:, 1:4:2, :], ALU.mult).then_inc(lam_v, 1)
            dve.wait_ge(lam_v, 1)
            v.tensor_reduce(lams[:, 0:2], lamb[:, 0:3:2, :], AX, ALU.add).then_inc(lam_v, 1)
            for g in (0, 2):
                dve.wait_ge(btab_mm, g + 1)
                v.tensor_copy(btab[:, g * 384:(g + 1) * 384], ps[0:12, (5 + g) * BANK:(5 + g) * BANK + 384]).then_inc(btab_ev, 1)
            v.tensor_scalar(negsink[:, :], sinkc[:, :], -1.0, None, ALU.mult).then_inc(lam_v, 1)
            dve.wait_ge(lam_e, 1)
            v.tensor_tensor(lams[:, 0:1], lams[:, 3:4], lams[:, 2:3], ALU.subtract).then_inc(lam_v, 1)
            dve.wait_ge(lam_v, 4)
            v.tensor_scalar(lams[:, 0:1], lams[:, 0:1], -LAM_INIT, None, ALU.add).then_inc(lam_v, 1)
            v.tensor_scalar(subc[:, :], subc[:, :], 1.0 - LAM_INIT, None, ALU.mult).then_inc(lam_v, 1)
            for t in range(NT):
                dve.wait_ge(x_in[t // 2], 16)
                if t >= 2:
                    dve.wait_ge(ln0, 3 * (t - 1))
                for hf in range(2):
                    v.bn_stats(stat[:, t % 2, 6 * hf:6 * hf + 6], xs[:, t, hf * 512:(hf + 1) * 512]).then_inc(ln0, 1)
                dve.wait_ge(ln0, 3 * t + 2)
                v.bn_aggr(mv[:, t, :], stat[:, t % 2, :]).then_inc(ln0, 1)
            dve.wait_ge(ln0, 24)
            v.tensor_scalar(rstd[:, :], mv[:, :, 1], EPS, None, ALU.add).then_inc(ln0, 1)
            dve.wait_ge(ln0_sq, 1)
            v.reciprocal(rstd[:, :], rstd[:, :]).then_inc(ln0, 1)
            dve.wait_ge(ln0, 26)
            for t in range(NT):
                v.tensor_scalar(xs[:, t, :], xs[:, t, :], mv[:, t, 0:1], rstd[:, t:t + 1], ALU.subtract, ALU.mult).then_inc(ln0, 1)
            for g in range(0, 12, 2):
                dve.wait_ge(flip_mm, g + 1)
                v.tensor_copy(flip_group(g)[1], bank(5 + g % 3)).then_inc(flip_v, 1)
            dve.wait_ge(adab_in, 64)
            dve.wait_ge(ada_mm, 4)
            v.tensor_tensor(modrow[:, :], bank(0), adab[:, :], ALU.add).then_inc(ada_ev, 1)
            dve.wait_ge(ss_in, 16)
            v.tensor_scalar(sscol[:, 8:16], sscol[:, 8:16], 1.0, None, ALU.add).then_inc(ss_one, 1)
            for k in range(NK):
                dve.wait_ge(xt_a, k + 1)
                v.tensor_copy(hTh[:, k, :], hraw[:, k % 2, :]).then_inc(h_hi, 1)
                dve.wait_ge(h_hi, 2 * k + 1)
                v.tensor_tensor(hTl[:, k, :], hraw[:, k % 2, :], hTh[:, k, :].bitcast(F32), ALU.subtract).then_inc(h_hi, 1)

            def low(ci):
                dve.wait_ge(w_hi, ci + 1)
                v.tensor_tensor(WL[ci % 2][:, :], WR[ci % 2][:, :], WH[ci % 2][:, :].bitcast(F32), ALU.subtract).then_inc(w_lo, 1)

            low(0)
            low(1)
            for g, (ci, kind, q, eng_) in enumerate(groups):
                if eng_ == "v":
                    dst, scale = proj_dst(g)
                    src = bank(g % 8)
                    if kind == "va":
                        src = src.rearrange("p (t n) -> p t n", t=2)
                    dve.wait_ge(proj_mm, g + 1)
                    v.tensor_scalar(dst, src, scale, None, ALU.mult).then_inc(proj_v, 1)
                if g == LAST[ci]:
                    low(ci + 2)
            dve.wait_ge(mask_set, 4)
            for u in range(32 + 1):
                if u < 32:
                    h, i = u // NT, u % NT
                    n = P * (i + 1)
                    for m in range(2):
                        dve.wait_ge(scoreA, 2 * u + m + 1)
                        if u >= 3:
                            dve.wait_ge(trA, grp0(u - 3) + ngrp((u - 3) % NT))
                        if u == 0:
                            dve.wait_ge(proj_mm, NGRP)
                        v.tensor_tensor_reduce(L[:, u % 3, m, 0:n], bank(2 * m, n), biasA[:, h, S - n:S], -1.0, BIG,
                                               ALU.add, ALU.min, nmA[:, u, m:m + 1]).then_inc(logitA, 1)
                w = u - 1
                if w >= 0:
                    n = P * (w % NT + 1)
                    dve.wait_ge(expA, 2 * w + 2)
                    v.reciprocal(smA[:, w, :], smA[:, w, :]).then_inc(attnA, 1)
                    dve.wait_ge(attnA, 4 * w + 1)
                    v.tensor_scalar(smA[:, w, 1:2], smA[:, w, 1:2], lams[:, 0:1], None, ALU.mult).then_inc(attnA, 1)
                    dve.wait_ge(attnA, 4 * w + 2)
                    v.tensor_scalar(L[:, w % 3, 1, 0:n], L[:, w % 3, 1, 0:n], smA[:, w, 1:2], None, ALU.mult).then_inc(attnA, 1)
                    dve.wait_ge(attnA, 4 * w + 3)
                    v.scalar_tensor_tensor(L[:, w % 3, 0, 0:n], L[:, w % 3, 0, 0:n], smA[:, w, 0:1], L[:, w % 3, 1, 0:n],
                                           ALU.mult, ALU.add).then_inc(attnA, 1)
                if u in (15, 31):
                    rd = 1 if u == 15 else 2
                    dve.wait_ge(ada_mm, 4 * (rd + 1))
                    dve.wait_ge(ada_out, 16 * rd)
                    dve.wait_ge(adab_in, 64 * (rd + 1))
                    v.tensor_tensor(modrow[:, :], bank(7), adab[:, :], ALU.add).then_inc(ada_ev, 1)
            dve.wait_ge(gst_out[0], 16 * 16)
            dve.wait_ge(gst_out[1], 16 * 16)
            for u in range(32 + 4):
                if u < 32:
                    i, t = u // 4, u % 4
                    a = 0 if i else P
                    for j in range(2):
                        hd = t + 4 * j
                        dve.wait_ge(scoreB, 2 * u + j + 1)
                        if u >= 4:
                            dve.wait_ge(trB, u - 3)
                        if u == 0:
                            dve.wait_ge(trA, 48)
                        v.tensor_tensor_reduce(LB[:, u % 4, j, a:256], ps[:, (2 * (u % 2) + j) * BANK:(2 * (u % 2) + j) * BANK + 256 - a],
                                               biasB[:, hd, a:256], -1.0, negsink[:, hd:hd + 1],
                                               ALU.add, ALU.min, nmB[:, u, j:j + 1]).then_inc(logitB, 1)
                w = u - 4
                if w >= 0:
                    i, t = w // 4, w % 4
                    dve.wait_ge(pvB, w + 1)
                    src = bank(6 + w % 2, 384).rearrange("p (j n) -> p j n", j=2)[:, :, 0:64]
                    v.tensor_copy(Qb[:, t, i * P:(i + 1) * P].rearrange("p (j n) -> p j n", j=2), src).then_inc(oB, 1)
            dve.wait_ge(expB, 64)
            n4 = nmB[:, :, :].rearrange("p (i t) j -> p i t j", i=NT)
            snk = sinkc[:, :].rearrange("p (j t) -> p t j", j=2)
            cntf = [0]

            def fin(ins):
                cntf[0] += 1
                ins.then_inc(finq, 1)
                dve.wait_ge(finq, cntf[0])

            for i in range(NT - 1):
                fin(v.tensor_tensor(n4[:, i], n4[:, i], snk, ALU.add))
            v.tensor_tensor(n4[:, NT - 1], n4[:, NT - 1], snk, ALU.add).then_inc(fin_v, 1)
            dve.wait_ge(oA, 64)
            v.tensor_scalar(msA[:, :], msA[:, :], 1.0 / P, EPS, ALU.mult, ALU.add).then_inc(fin_v, 1)
            dve.wait_ge(fin_a, 1)
            fin(v.tensor_tensor(smB[:, :, :], smB[:, :, :], nmB[:, :, :], ALU.add))
            fin(v.reciprocal(smB[:, :, :], smB[:, :, :]))
            dve.wait_ge(fin_a, 2)
            fin(v.reciprocal(msA[:, :], msA[:, :]))
            for h in range(H_A):
                qv = Qa[:, h, :].rearrange("p (i n) -> p i n", i=NT)
                v.tensor_tensor(qv, qv, msA[:, h * NT:(h + 1) * NT].unsqueeze(2).to_broadcast([P, NT, P]), ALU.mult).then_inc(fin_v, 1)
            dve.wait_ge(oB, 32)
            s4 = smB[:, :, :].rearrange("p (i t) j -> p t i j", i=NT)
            for t in range(4):
                qv = Qb[:, t, :].rearrange("p (i j n) -> p i j n", i=NT, j=2)
                v.tensor_tensor(qv, qv, s4[:, t].unsqueeze(3).to_broadcast([P, NT, 2, 64]), ALU.mult).then_inc(fin_v, 1)
            for f in range(16):
                cols = slice((f % 2) * 512, (f % 2) * 512 + 512)
                dve.wait_ge(o_hi, f + 1)
                hi = Oh[:, f // 2, cols].bitcast(F32)
                if f < 8:
                    v.scalar_tensor_tensor(Ol[:, f // 2, cols], bank(f % 8), subc[:, 0:1], hi, ALU.mult,
                                           ALU.subtract).then_inc(finT_v, 1)
                else:
                    v.tensor_tensor(Ol[:, f // 2, cols], bank(f % 8), hi, ALU.subtract).then_inc(finT_v, 1)
            for m in range(16):
                st, d, hf = m % 2, m // 2, m % 2
                cols = slice(hf * 512, (hf + 1) * 512)
                dve.wait_ge(gin_in[st], 32 * (m // 2 + 1))
                for g in range(2):
                    dve.wait_ge(merge_mm, 2 * m + g + 1)
                    v.tensor_tensor(gin[:, st, g, :], gin[:, st, g, :], bank(2 * (m % 4) + g), ALU.mult).then_inc(merged, 1)
                dve.wait_ge(merged, 5 * m + 2)
                v.tensor_tensor(gin[:, st, 0, :], gin[:, st, 0, :], gin[:, st, 1, :], ALU.add).then_inc(merged, 1)
                dve.wait_ge(merged, 5 * m + 3)
                v.tensor_copy(mTh[:, d, cols], gin[:, st, 0, :]).then_inc(merged, 1)
                dve.wait_ge(merged, 5 * m + 4)
                v.tensor_tensor(mTl[:, d, cols], gin[:, st, 0, :], mTh[:, d, cols].bitcast(F32), ALU.subtract).then_inc(merged, 1)
                if m in (5, 9):
                    low(NPC + 2 + (m - 5) // 4)
            for n in range(2):
                for k in range(NK):
                    dve.wait_ge(wo_hi, 8 * n + k + 1)
                    v.tensor_tensor(WOL[n][:, k, :], WOR[n][:, k, :], WOH[n][:, k, :].bitcast(F32), ALU.subtract).then_inc(wo_lo, 1)
            v.memset(rwz[:, NK:16, :], 0.0).then_inc(rwp_v, 1)
            dve.wait_ge(rows_in, 80)
            v.tensor_scalar(rowA[:, 3, :], rowA[:, 3, :], 1.0, None, ALU.add).then_inc(rows_one, 1)
            dve.wait_ge(rows_one, 1)
            for t in range(NT):
                n = [18 * t]

                def st_(ins):
                    n[0] += 1
                    ins.then_inc(post_v, 1)
                    dve.wait_ge(post_v, n[0])

                X = X2[:, t, :]
                dve.wait_ge(y_mm, 2 * t + 2)
                st_(v.tensor_tensor(X, bank(2 * (t % 2), BANK, 2), rowA[:, 0, :], ALU.mult))
                dve.wait_ge(xin_in, 16 * t + 16)
                st_(v.scalar_tensor_tensor(X, xin[:, 0, :], ALPHA, X, ALU.mult, ALU.add))
                for r_ in range(2):
                    for hf in range(2):
                        st_(v.bn_stats(stat[:, 0, 6 * hf:6 * hf + 6], X2[:, t, hf * 512:(hf + 1) * 512]))
                    st_(v.bn_aggr(mv[:, 0, :], stat[:, 0, :]))
                    st_(v.tensor_scalar(rstd[:, r_:r_ + 1], mv[:, 0, 1:2], EPS, None, ALU.add))
                    dve.wait_ge(post_a, 2 * t + r_ + 1)
                    st_(v.reciprocal(rstd[:, r_:r_ + 1], rstd[:, r_:r_ + 1]))
                    if r_ == 0:
                        st_(v.tensor_scalar(X, X, mv[:, 0, 0:1], rstd[:, 0:1], ALU.subtract, ALU.mult))
                        st_(v.tensor_tensor(X, X, rowA[:, 1, :], ALU.mult))
                        st_(v.tensor_tensor(X, X, rowA[:, 2, :], ALU.add))
                    else:
                        Hh = h2[:, t % 2, :]
                        if t >= 2:
                            dve.wait_ge(h2_out, 16 * (t - 1))
                            dve.wait_ge(h2T_mm, t - 1)
                        st_(v.tensor_scalar(Hh, X, mv[:, 0, 0:1], rstd[:, 1:2], ALU.subtract, ALU.mult))
                        st_(v.tensor_tensor(Hh, Hh, rowA[:, 3, :], ALU.mult))
                        st_(v.tensor_tensor(Hh, Hh, sh2[:, :], ALU.add))
                if t >= 1:
                    dve.wait_ge(y_zero, 64) if t == 1 else None
                    dve.wait_ge(rout_mm, t)
                    v.tensor_copy(lg[:, t - 1, :], ps[:, 6 * BANK:6 * BANK + NE]).then_inc(rout_ev, 1)
            dve.wait_ge(rout_mm, NT)
            v.tensor_copy(lg[:, NT - 1, :], ps[:, 6 * BANK:6 * BANK + NE]).then_inc(rout_ev, 1)
            q = [0]

            def ro(ins):
                q[0] += 1
                ins.then_inc(route, 1)
                dve.wait_ge(route, q[0])

            def b3(row, n):
                return row.unsqueeze(1).to_broadcast([P, NT, n])

            dve.wait_ge(rt_in, 16 * 7)
            ro(v.memset(ones[:, :], 1.0))
            dve.wait_ge(route_a, 1)
            ro(v.tensor_tensor(bi[:, :, :], s_[:, :, :], b3(rbias[:, :], NE), ALU.add))
            b4 = bi[:, :, :].rearrange("p t (g e) -> p t g e", g=NG)
            ro(v.tensor_tensor(g0_[:, :, :], b4[:, :, :, 0], b4[:, :, :, 1], ALU.max))
            ro(v.tensor_tensor(g1_[:, :, :], b4[:, :, :, 0], b4[:, :, :, 1], ALU.min))
            ro(v.tensor_tensor(g2_[:, :, :], b4[:, :, :, 2], b4[:, :, :, 3], ALU.max))
            ro(v.tensor_tensor(g3_[:, :, :], b4[:, :, :, 2], b4[:, :, :, 3], ALU.min))
            ro(v.tensor_tensor(g4_[:, :, :], g0_[:, :, :], g2_[:, :, :], ALU.min))
            ro(v.tensor_tensor(g1_[:, :, :], g1_[:, :, :], g3_[:, :, :], ALU.max))
            ro(v.tensor_tensor(g1_[:, :, :], g1_[:, :, :], g4_[:, :, :], ALU.max))
            ro(v.tensor_tensor(g0_[:, :, :], g0_[:, :, :], g2_[:, :, :], ALU.max))
            ro(v.tensor_tensor(g0_[:, :, :], g0_[:, :, :], g1_[:, :, :], ALU.add))

            def first_max(dst, src, n, revrow):
                ro(v.tensor_reduce(m1[:, :], src, AX, ALU.max))
                ro(v.tensor_tensor(dst, src, m1[:, :].unsqueeze(2).to_broadcast([P, NT, n]), ALU.is_equal))
                ro(v.tensor_tensor(dst, dst, b3(revrow, n), ALU.mult))
                ro(v.tensor_reduce(m1[:, :], dst, AX, ALU.max))
                ro(v.tensor_tensor(dst, dst, m1[:, :].unsqueeze(2).to_broadcast([P, NT, n]), ALU.is_equal))

            first_max(g2_[:, :, :], g0_[:, :, :], NG, rev[:, NE:NE + NG])
            gb = g2_[:, :, :].unsqueeze(3).to_broadcast([P, NT, NG, EPG])
            t04 = t0[:, :, :].rearrange("p t (g e) -> p t g e", g=NG)
            ro(v.tensor_tensor(t04, b4, gb, ALU.mult))
            ro(v.tensor_scalar(g3_[:, :, :], g2_[:, :, :], -1.0, 1e30, ALU.add, ALU.mult))
            gb3 = g3_[:, :, :].unsqueeze(3).to_broadcast([P, NT, NG, EPG])
            ro(v.tensor_tensor(t04, t04, gb3, ALU.add))
            first_max(oh[0][:, :, :], t0[:, :, :], NE, rev[:, 0:NE])
            ro(v.scalar_tensor_tensor(t0[:, :, :], oh[0][:, :, :], -2e30, t0[:, :, :], ALU.mult, ALU.add))
            first_max(oh[1][:, :, :], t0[:, :, :], NE, rev[:, 0:NE])
            for k in range(2):
                ro(v.tensor_tensor(t1[:, :, :], oh[k][:, :, :], s_[:, :, :], ALU.mult))
                ro(v.tensor_reduce(ms_[:, k, :], t1[:, :, :], AX, ALU.add))
            ro(v.tensor_tensor(m1[:, :], ms_[:, 0, :], ms_[:, 1, :], ALU.add))
            ro(v.reciprocal(m1[:, :], m1[:, :]))
            for k in range(2):
                ro(v.tensor_tensor(wk[:, k, :], ms_[:, k, :], m1[:, :], ALU.mult))
            ro(v.tensor_tensor(t1[:, :, :], oh[0][:, :, :], oh[1][:, :, :], ALU.add))
            ro(v.memset(Mex[:, 0, :], 0.0))
            for t in range(1, NT):
                ro(v.tensor_tensor(Mex[:, t, :], Mex[:, t - 1, :], t1[:, t - 1, :], ALU.add))
            ro(v.tensor_tensor(nb_[:, :], Mex[:, NT - 1, :], t1[:, NT - 1, :], ALU.add))
            RANK_READY[0] = q[0]
            dve.wait_ge(rank_mm, 1)
            ro(v.tensor_copy(rank[:, :, :].rearrange("p t e -> p (t e)"), bank(0, P)))
            dve.wait_ge(rank_mm, 2)
            ro(v.tensor_copy(cnt[:, :], bank(1, NE)))
            c3 = c8[:, 0:NE * 8].rearrange("p (e j) -> p e j", j=8)
            ro(v.tensor_scalar(mul8[:, :], iota[:, 0:8], 128.0, None, ALU.mult))
            ro(v.tensor_tensor(c3, cnt[:, :].unsqueeze(2).to_broadcast([P, NE, 8]),
                               mul8[:, :].unsqueeze(1).to_broadcast([P, NE, 8]), ALU.is_gt))
            ro(v.tensor_reduce(nb_[:, :], c3, AX, ALU.add))
            bg = big[:, 0:NE, :]
            ro(v.tensor_tensor(bg, before[:, :, :], nb_[:, :].unsqueeze(1).to_broadcast([P, NE, NE]), ALU.mult))
            ro(v.tensor_reduce(pst[:, :], bg, AX, ALU.add))
            ro(v.tensor_tensor(pen[:, :], pst[:, :], nb_[:, :], ALU.add))
            for k in range(2):
                ro(v.tensor_tensor(t1[:, :, :], oh[k][:, :, :], rank[:, :, :], ALU.mult))
                ro(v.tensor_reduce(Rk[:, k, :], t1[:, :, :], AX, ALU.add))
                ro(v.tensor_tensor(t1[:, :, :], oh[k][:, :, :], b3(pst[:, :], NE), ALU.mult))
                ro(v.tensor_reduce(Pk[:, k, :], t1[:, :, :], AX, ALU.add))
            c4 = c8[:, :].rearrange("p (a j) -> p a j", j=8)
            Rf = Rk[:, :, :].rearrange("p k t -> p (k t)")
            rf = rb_[:, :, :].rearrange("p k t -> p (k t)")
            Pf = Pk[:, :, :].rearrange("p k t -> p (k t)")
            ro(v.tensor_tensor(c4, Rf.unsqueeze(2).to_broadcast([P, 16, 8]),
                               mul8[:, :].unsqueeze(1).to_broadcast([P, 16, 8]), ALU.is_ge))
            ro(v.tensor_reduce(rf, c4, AX, ALU.add))
            ro(v.tensor_scalar(rf, rf, -1.0, None, ALU.add))
            ro(v.tensor_tensor(Pf, Pf, rf, ALU.add))
            ro(v.scalar_tensor_tensor(Rf, rf, -128.0, Rf, ALU.mult, ALU.add))
            ro(v.scalar_tensor_tensor(rf, Pf, 128.0, Rf, ALU.mult, ALU.add))
            ro(v.tensor_copy(slot_u[:, :, :].rearrange("p k t -> p (k t)"), rf))
            for a in range(16):
                t = a % NT
                v.tensor_scalar(Aoh[:, a, :], iota[:, :], Rf[:, a:a + 1], None, ALU.is_equal).then_inc(route, 1)
                v.tensor_scalar(Boh[:, a, :], iota[:, 0:MAXBLK], Pf[:, a:a + 1], tokid[:, t:t + 1],
                                ALU.is_equal, ALU.mult).then_inc(route, 1)
                q[0] += 2
            OH_READY[0] = q[0]
            ro(v.tensor_tensor(big[:, :, :], iota[:, 0:MAXBLK].unsqueeze(2).to_broadcast([P, MAXBLK, NE]),
                               pen[:, :].unsqueeze(1).to_broadcast([P, MAXBLK, NE]), ALU.is_ge))
            ro(v.tensor_reduce(ef[:, :], big[:, :, :], AX, ALU.add))
            ro(v.tensor_scalar(ef[:, :], ef[:, :], 1.0, 16.0, ALU.add, ALU.min))
            ro(v.tensor_copy(blk_e[:, :], ef[:, :]))
            ro(v.tensor_copy(nblk_i[:, :], pen[:, NE - 1:NE]))
            ro(v.tensor_scalar(pen[:, :], pen[:, :], 1.0, None, ALU.add))
            ro(v.tensor_copy(pend_i[:, :], pen[:, :]))
            dve.wait_ge(idx_mm, 1)
            v.tensor_copy(idx_u[:, :], bank(2, MAXBLK)).then_inc(tabs, 1)
            dve.wait_ge(tabs, 1)
            nblk = dve.value_load(nblk_i[0:1, 0:1], min_val=16, max_val=31)
            xTf = xT[:, :, :].rearrange("p k q -> p (k q)")
            dve.wait_ge(xg_tr, 1)
            v.tensor_copy(xTf[:, 512:1024], bank(3)).then_inc(xT_v, 1)
            dve.sem_inc(y_v, 1)
            with dve.Fori(0, nblk) as b:
                dve.wait_ge(sig_a, b + 1)
                v.tensor_tensor(sig[:, :], sig[:, :], bank(0), ALU.mult).then_inc(glu_v, 1)
                dve.wait_ge(glu_v, b + 1)
                dve.wait_ge(up_mm, b + 1)
                v.tensor_tensor(hh[:, :], sig[:, :], bank(1), ALU.mult).then_inc(hh_v, 1)
                dve.wait_ge(hh_tr, b + 1)
                v.tensor_copy(hhT[:, :, :].rearrange("p k q -> p (k q)"), bank(4)).then_inc(hhT_v, 1)
                dve.wait_ge(xg_tr, b + 2)
                v.tensor_copy(xTf[:, 512:1024], bank(3)).then_inc(xT_v, 1)
                dve.wait_ge(down_mm, b + 1)
                dve.wait_ge(y_out, b * 16 + 16)
                v.tensor_copy(ysb[:, 512:1024], bank(6)).then_inc(y_v, 1)
            dve.wait_ge(rowB_in, 48)
            for t in range(NT):
                n = [11 * t]

                def cb(ins):
                    n[0] += 1
                    ins.then_inc(comb, 1)
                    dve.wait_ge(comb, n[0])

                A_, B_, R = yg[:, t % 2, 0, :], yg[:, t % 2, 1, :], r2[:, t % 2, :]
                dve.wait_ge(comb_in[t % 2], 32 * (t // 2 + 1))
                if t >= 2:
                    dve.wait_ge(res_out[t % 2], 16 * (t // 2))
                cb(v.tensor_scalar(R, A_, wk[:, 0, t:t + 1], None, ALU.mult))
                cb(v.scalar_tensor_tensor(R, B_, wk[:, 1, t:t + 1], R, ALU.mult, ALU.add))
                cb(v.tensor_tensor(R, R, rowB[:, 0, :], ALU.mult))
                cb(v.scalar_tensor_tensor(R, X2[:, t, :], ALPHA, R, ALU.mult, ALU.add))
                for hf in range(2):
                    cb(v.bn_stats(stat[:, 0, 6 * hf:6 * hf + 6], r2[:, t % 2, hf * 512:(hf + 1) * 512]))
                cb(v.bn_aggr(mv[:, 0, :], stat[:, 0, :]))
                cb(v.tensor_scalar(rstd[:, 0:1], mv[:, 0, 1:2], EPS, None, ALU.add))
                dve.wait_ge(comb_a, t + 1)
                v.reciprocal(rstd[:, 0:1], rstd[:, 0:1]).then_inc(comb_r, 1)
                dve.wait_ge(comb_r, t + 1)
                cb(v.tensor_scalar(R, R, mv[:, 0, 0:1], rstd[:, 0:1], ALU.subtract, ALU.mult))
                cb(v.tensor_tensor(R, R, rowB[:, 1, :], ALU.mult))
                cb(v.tensor_tensor(R, R, rowB[:, 2, :], ALU.add))

        @block.tensor
        def _(pe):
            mm = nc.tensor.matmul
            pe.wait_ge(small_in, 112)
            for g in range(3):
                mm(ps[0:12, (5 + g) * BANK:(5 + g) * BANK + 384], relb[:, :], onehot[:, g * 384:(g + 1) * 384],
                   start=True, stop=True).then_inc(btab_mm, 1)

            def ada(ch, b):
                ada_in(pe, ch)
                w = adas[ADA_SLOT[ch]][:, :].rearrange("p (k n) -> p k n", k=2)
                for kk in range(2):
                    k = 2 * (ch % 4) + kk
                    for j in range(4):
                        last = mm(ps[32 * j:32 * j + 32, b * BANK:(b + 1) * BANK], csil[:, k:k + 1].to_broadcast([P, 32]),
                                  w[:, kk, j * 512:(j + 1) * 512], start=(k == 0), stop=(k == NK - 1), skip_group_check=True)
                last.then_inc(ada_mm, 1)

            pe.wait_ge(silu_v, 3)
            for ch in range(4):
                ada(ch, 0)
                if ch == 2:
                    pe.wait_ge(btab_in, 32)
                    pe.wait_ge(btab_ev, 3)
                    for g in range(12):
                        if g >= 3:
                            pe.wait_ge((flip_v, flip_a)[(g - 3) % 2], (g - 3) // 2 + 1)
                        mm(bank(5 + g % 3), flip[:, :], flip_group(g)[0], start=True, stop=True).then_inc(flip_mm, 1)
            pe.wait_ge(ln0, 26 + NT)
            pe.wait_ge(flip_v, 6)
            pe.wait_ge(flip_a, 6)
            for k in range(NK):
                if k >= 3:
                    pe.wait_ge(xt_a, k - 2)
                b0 = 1 + 2 * (k % 3)
                for t in range(NT):
                    last = nc.tensor.transpose(ps[:, b0 * BANK + t * P:b0 * BANK + (t + 1) * P], xs[:, t, k * P:(k + 1) * P], ident[:, :])
                last.then_inc(xt_mm, 1)
            pe.wait_ge(h_hi, 2 * NK)

            def split_product(out_, lh, ll, rh, rl, first, last):
                mm(out_, lh, rh, start=first, stop=False)
                mm(out_, ll, rh, start=False, stop=False)
                return mm(out_, lh, rl, start=False, stop=last)

            for g, (ci, kind, q, eng_) in enumerate(groups):
                if kind != "vt" and (g == 0 or groups[g - 1][0] != ci):
                    pe.wait_ge(w_lo, ci + 1)
                if g >= 8:
                    pe.wait_ge(proj_a if groups[g - 8][3] == "a" else proj_v, taken(g - 8))
                out_ = bank(g % 8)
                if kind == "vt":
                    if q == 0:
                        for vg in [x for x in range(NGRP) if groups[x][1] == "vb"]:
                            pe.wait_ge(proj_a if groups[vg][3] == "a" else proj_v, taken(vg))
                    for t in range(4):
                        last = nc.tensor.transpose(out_[:, t * P:(t + 1) * P], vbT[:, (4 * q + t) * P:(4 * q + t + 1) * P],
                                                   ident[:, :])
                    last.then_inc(proj_mm, 1)
                    continue
                wh = WH[ci % 2][:, :].rearrange("p (k n) -> p k n", k=NK)
                wl = WL[ci % 2][:, :].rearrange("p (k n) -> p k n", k=NK)
                if kind == "va":
                    for t in range(2):
                        rows = slice((2 * (q % 4) + t) * P, (2 * (q % 4) + t + 1) * P)
                        for k in range(NK):
                            last = split_product(out_[:, t * 256:(t + 1) * 256], hTh[:, k, rows], hTl[:, k, rows], wh[:, k, :],
                                                 wl[:, k, :], k == 0, k == NK - 1)
                    last.then_inc(proj_mm, 1)
                    continue
                c0 = {"kb": 0, "vb": P}.get(kind, (q // 2 % 2) * P)
                half = slice((q % 2) * 512, (q % 2) * 512 + 512)
                for k in range(NK):
                    last = split_product(out_, wh[:, k, c0:c0 + P], wl[:, k, c0:c0 + P], hTh[:, k, half], hTl[:, k, half],
                                         k == 0, k == NK - 1)
                last.then_inc(proj_mm, 1)
            pe.wait_ge(proj_v, NVG)
            pe.wait_ge(proj_a, NAG)
            for u in range(32 + 3):
                if u < 32:
                    h, i = u // NT, u % NT
                    n = P * (i + 1)
                    pe.wait_ge(padA, 2 * u + 2)
                    for m in range(2):
                        if u >= 1:
                            pe.wait_ge(logitA, 2 * (u - 1) + m + 1)
                        for c0 in range(0, n, 512):
                            w = min(512, n - c0)
                            last = mm(ps[:, 2 * m * BANK + c0:2 * m * BANK + c0 + w], qpad[:, u % 2, m, :], Ka[:, h, c0:c0 + w], start=True, stop=True)
                        last.then_inc(scoreA, 1)
                v = u - 2
                if 0 <= v < 32:
                    h, i = v // NT, v % NT
                    pe.wait_ge(attnA, 4 * v + 4)
                    for g in range(ngrp(i)):
                        gg = grp0(v) + g
                        if gg >= 2:
                            pe.wait_ge(aT_ev, gg - 1)
                        for kt in range(4 * g, min(4 * g + 4, i + 1)):
                            last = nc.tensor.transpose(ps[:, (4 + gg % 2) * BANK + (kt % 4) * P:(4 + gg % 2) * BANK + (kt % 4 + 1) * P],
                                                       L[:, v % 3, 0, kt * P:(kt + 1) * P], ident[:, :])
                        last.then_inc(trA, 1)
                v = u - 3
                if v >= 0:
                    h, i = v // NT, v % NT
                    for g in range(ngrp(i)):
                        gg = grp0(v) + g
                        pe.wait_ge(aT_ev, gg + 1)
                        if g == 0 and v >= 1:
                            pe.wait_ge(oA, 2 * (v - 1) + 1)
                        for kt in range(4 * g, min(4 * g + 4, i + 1)):
                            last = mm(bank(6, P), aT[:, gg % 4, (kt % 4) * P:(kt % 4 + 1) * P], Va[:, kt, h * P:(h + 1) * P],
                                      start=(kt == 0), stop=(kt == i))
                        last.then_inc(pvA, 1)
                if u % 4 == 3 and u < 32:
                    ch = 4 + u // 4
                    if ch == 8:
                        pe.wait_ge(ada_ev, 2)
                    ada(ch, 7)
            pe.wait_ge(ada_ev, 3)
            pe.wait_ge(oA, 63)
            for u in range(32 + 3):
                if u < 32:
                    i, t = u // 4, u % 4
                    pe.wait_ge(padB, 2 * u + 2)
                    k0 = max(0, (i - 1) * P)
                    n = (i + 1) * P - k0
                    for j in range(2):
                        if u >= 2:
                            pe.wait_ge(logitB, 2 * (u - 2) + j + 1)
                        b0 = (2 * (u % 2) + j) * BANK
                        mm(ps[:, b0:b0 + n], qpad[:, u % 2, j, :], Kb[:, k0:k0 + n], start=True, stop=True).then_inc(scoreB, 1)
                v = u - 2
                if 0 <= v < 32:
                    i, t = v // 4, v % 4
                    nt = 2 if i else 1
                    pe.wait_ge(expB, 2 * v + 2)
                    if v >= 2:
                        pe.wait_ge(bT_ev, v - 1)
                    for j in range(2):
                        for kt in range(nt):
                            col = (4 + v % 2) * BANK + (j * nt + kt) * P
                            last = nc.tensor.transpose(ps[:, col:col + P], LB[:, v % 4, j, (2 - nt + kt) * P:(3 - nt + kt) * P], ident[:, :])
                    last.then_inc(trB, 1)
                v = u - 3
                if v >= 0:
                    i, t = v // 4, v % 4
                    nt = 2 if i else 1
                    pe.wait_ge(bT_ev, v + 1)
                    if v >= 2:
                        pe.wait_ge(oB, v - 1)
                    for j in range(2):
                        for kt in range(nt):
                            last = mm(ps[:, (6 + v % 2) * BANK + j * P:(6 + v % 2) * BANK + (j + 1) * P], aT[:, v % 4, (j * nt + kt) * P:(j * nt + kt + 1) * P],
                                      Vb[:, i - nt + 1 + kt, :], start=(kt == 0), stop=(kt == nt - 1))
                    last.then_inc(pvB, 1)
            pe.wait_ge(logitB, 64)
            pe.wait_ge(bT_ev, 32)
            for f in range(16):
                src, q = (Qa, f) if f < 8 else (Qb, f - 8)
                pe.wait_ge(fin_v, 3 + (f // 2 if f < 8 else 4 + q // 2))
                if f >= 8:
                    pe.wait_ge(finT_v, f - 7)
                for i4 in range(4):
                    i = 4 * (q % 2) + i4
                    last = nc.tensor.transpose(ps[:, (f % 8) * BANK + i4 * P:(f % 8) * BANK + (i4 + 1) * P], src[:, q // 2, i * P:(i + 1) * P], ident[:, :])
                last.then_inc(finT, 1)
            pe.wait_ge(finT_v, 16)
            for m in range(16):
                d, hf, ci = m // 2, m % 2, NPC + m // 4
                if m % 4 == 0:
                    pe.wait_ge(w_lo, ci + 1)
                if m >= 4:
                    pe.wait_ge(merged, 5 * (m - 4) + 2)
                wh = WH[ci % 2][:, :].rearrange("p (g k n) -> p g k n", g=2, k=4)
                wl = WL[ci % 2][:, :].rearrange("p (g k n) -> p g k n", g=2, k=4)
                cols, half = slice((d % 2) * P, (d % 2 + 1) * P), slice(hf * 512, (hf + 1) * 512)
                for g in range(2):
                    for k in range(4):
                        last = split_product(bank(2 * (m % 4) + g), wh[:, g, k, cols], wl[:, g, k, cols], Oh[:, 4 * g + k, half],
                                             Ol[:, 4 * g + k, half], k == 0, k == 3)
                    last.then_inc(merge_mm, 1)
            rwf = rwz[:, :, :].rearrange("p k e -> p (k e)")
            pe.wait_ge(merged, 80)
            for t in range(NT + 1):
                if t < NT:
                    if t >= 2:
                        pe.wait_ge(post_v, 18 * (t - 2) + 1)
                    rows = slice(t * P, (t + 1) * P)
                    for n in range(2):
                        for k in range(NK):
                            if t == 0:
                                pe.wait_ge(wo_lo, 8 * n + k + 1)
                            last = split_product(bank(2 * (t % 2) + n), mTh[:, k, rows], mTl[:, k, rows], WOH[n][:, k, :],
                                                 WOL[n][:, k, :], k == 0, k == NK - 1)
                        last.then_inc(y_mm, 1)
                if t >= 1:
                    s = t - 1
                    pe.wait_ge(post_v, 18 * (s + 1))
                    if s >= 1:
                        pe.wait_ge(h2T_ev, s)
                    for k in range(NK):
                        last = nc.tensor.transpose(ps[:, 4 * BANK + k * P:4 * BANK + (k + 1) * P], h2[:, s % 2, k * P:(k + 1) * P], ident[:, :])
                    last.then_inc(h2T_mm, 1)
                    pe.wait_ge(h2T_ev, s + 1)
                    pe.wait_ge(rwp_v, 1)
                    pe.wait_ge(rt_in, 16 * 7)
                    if s >= 1:
                        pe.wait_ge(rout_ev, s)
                    for k in range(NK):
                        last = mm(bank(6, P), h2T[:, k, :], rwf[:, k * NE:k * NE + P], start=(k == 0), stop=(k == NK - 1))
                    last.then_inc(rout_mm, 1)
            pe.wait_ge(route, RANK_READY[0])
            t1f = t1[:, :, :].rearrange("p t e -> p (t e)")
            mm(bank(0, P), lower[:, :], t1f, start=True, stop=False)
            mm(bank(0, P), ones[:, :], Mex[:, :, :].rearrange("p t e -> p (t e)"), start=False, stop=True).then_inc(rank_mm, 1)
            mm(bank(1, NE), ones[:, :], nb_[:, :], start=True, stop=True).then_inc(rank_mm, 1)
            pe.wait_ge(route, OH_READY[0])
            for a in range(16):
                last = mm(bank(2, MAXBLK), Aoh[:, a, :], Boh[:, a, :], start=(a == 0), stop=(a == 15))
            last.then_inc(idx_mm, 1)
            pe.wait_ge(tabs, 1)
            nblk = pe.value_load(nblk_i[0:1, 0:1], min_val=16, max_val=31)

            def transpose_rows():
                for k in range(NK):
                    last = nc.tensor.transpose(ps[:, 2 * BANK + k * P:2 * BANK + (k + 1) * P], xg[:, k * P:(k + 1) * P], ident[:, :])
                last.then_inc(xg_tr, 1)

            pe.wait_ge(gathered, 16)
            transpose_rows()
            with pe.Fori(0, nblk) as b:
                e1 = pe.value_load(blk_e[0:1, bass.ds(b, 1)], min_val=1, max_val=NE)
                off = (e1 % 2) * EVEN
                pe.wait_ge(exp_ready, e1)
                pe.wait_ge(xT_a, b + 1)
                pe.wait_ge(xT_v, b + 1)
                for wi, done in enumerate((gate_mm, up_mm)):
                    for k in range(NK):
                        last = mm(bank(wi), xT[:, k, :], EXP[:, bass.ds(off + (wi * 4096 + k * 512), 512)], start=(k == 0), stop=(k == NK - 1))
                    last.then_inc(done, 1)
                pe.wait_ge(hh_v, b + 1)
                for k in range(4):
                    last = nc.tensor.transpose(ps[:, 4 * BANK + k * P:4 * BANK + (k + 1) * P], hh[:, k * P:(k + 1) * P], ident[:, :])
                last.then_inc(hh_tr, 1)
                pe.wait_ge(gathered, b * 16 + 32)
                transpose_rows()
                pe.wait_ge(hhT_v, b + 1)
                pe.wait_ge(y_a, b + 1)
                pe.wait_ge(y_v, b + 1)
                for k in range(4):
                    for n in range(2):
                        last = mm(bank(5 + n), hhT[:, k, :], EXP[:, bass.ds(off + (8192 + k * 1024 + n * 512), 512)], start=(k == 0), stop=(k == 3))
                last.then_inc(down_mm, 1)


_INS = ["x", "c", "ada_w", "ada_b", "w_in", "lam", "subln_w", "sinks", "w_branch_a", "w_branch_b", "w_out",
        "ln_g", "ln_b", "rel_bias", "router_w", "router_b", "exp_w1", "exp_w3", "exp_w2"]


def _constants():
    import math

    import numpy as np

    rel = np.arange(TAB) - 1023
    nb = NBUCKET // 2
    exact = nb // 2
    n = np.abs(rel)
    far = exact + (np.log(np.maximum(n, 1).astype(np.float32) / np.float32(exact)) / np.float32(math.log(1024 / exact))
                   * np.float32(nb - exact)).astype(np.int32)
    bucket = np.where(rel > 0, nb, 0) + np.where(n < exact, n, np.minimum(far, nb - 1))
    f = np.float32
    i = np.arange(P)
    rows = lambda v: np.ascontiguousarray(np.broadcast_to(np.asarray(v, f).reshape(1, -1), (P, np.size(v))))
    e = np.arange(NE)
    return {
        "ident": np.eye(P, dtype=f),
        "onehot": (bucket[None, :] == np.arange(NBUCKET)[:, None]).astype(f),
        "lower": (i[:, None] < i[None, :]).astype(f),
        "iota": rows(i),
        "rev": rows(np.concatenate([NE - e, NG - np.arange(NG)])),
        "before": rows(e[None, :] < e[:, None]),
        "tokid": (i[:, None] + P * np.arange(NT)[None, :]).astype(f),
        "flip": np.ascontiguousarray(np.eye(P, dtype=f)[::-1]),
    }


def kernel(**inputs):
    import numpy as _np
    import concourse.bacc as _bacc
    from concourse import mybir as _mybir
    from concourse.bass_utils import run_bass_kernel_spmd as _run

    nc = _bacc.Bacc("TRN2", target_bir_lowering=False, num_devices=1)
    arrays, args = {}, []
    named = [(n, inputs[n]) for n in _INS] + list(_constants().items())
    for name, value in named:
        a = _np.ascontiguousarray(value)
        arrays[f"in_{name}_dram"] = a
        args.append(nc.dram_tensor(f"in_{name}_dram", a.shape, _mybir.dt.from_np(a.dtype), kind="ExternalInput").ap())
    args.append(nc.dram_tensor("out_0_dram", (1, S, D), F32, kind="ExternalOutput").ap())
    mixer_moe_kernel(nc, *args)
    r = _run(nc, [arrays], core_ids=[0])
    return r.results[0]["out_0_dram"]
```

```python
from contextlib import ExitStack

import concourse.bass as bass
from concourse import mybir

F32 = mybir.dt.float32
F32R = mybir.dt.float32r
U32 = mybir.dt.uint32
I32 = mybir.dt.int32
ALU = mybir.AluOpType
ACT = mybir.ActivationFunctionType
AX = mybir.AxisListType.X

P = 128
D = 1024
S = 1024
NT = S // P
NK = D // P
BANK = 512
H_A, H_B = 4, 8
QA, KA, VA, QB, KVB = 512, 512, 512, 512, 256
COL_Q, COL_K, COL_V, COL_QB, COL_KB = 0, 512, 1024, 1536, 2048
COL_G = 2304
NBUCKET = 32
TAB = 1152
ALPHA = 2.0 ** 0.25
LAM_INIT = 0.8 - 0.6
EPS = 1e-5
NEG = -1.0e30
BIG = 3.0e38
NE, NG, EPG = 16, 4, 4
FE = 512
MAXBLK = 32
KB = 256
SQ = 0.125


def mixer_moe_kernel(nc, x, c, ada_w, ada_b, w_in, lam, subln_w, sinks, w_a, w_b, w_out,
                     ln_g, ln_b, rel_bias, router_w, router_b, w1, w3, w2,
                     ident_h, onehot_h, lower_h, iota_h, rev_h, before_h, tokid_h, flip_h, out):
    base = (nc.sbuf_base + 63) // 64 * 64

    def at(name, kib, shape, dt=F32):
        return nc.alloc_sbuf_tensor_at(name, shape, dt, offset=base + int(kib * 1024))

    ctx = ExitStack()
    with ctx:
        ctx.enter_context(nc.allow_non_contiguous_dma(reason="columns of a few hundred bytes"))

        def sem(name):
            return ctx.enter_context(nc.semaphore(name))

        bias_d = nc.dram_tensor("bias_by_distance", [12, TAB], F32)
        mod_d = nc.dram_tensor("ada_mod", [12, BANK], F32)
        h2_d = nc.dram_tensor("moe_input", [S, D], F32)
        gate_d = nc.dram_tensor("gates", [2 * NK, 2, P, BANK], F32)
        y_d = nc.dram_tensor("expert_rows", [MAXBLK * P, D], F32)
        x2_d = nc.dram_tensor("moe_residual", [S, D], F32)

        o = [0.0]

        def packed(start, limit):
            at_ = [start]

            def place(name, shape, dt=F32):
                n = 1
                for v in shape[1:]:
                    n *= v
                t = at(name, at_[0], shape, dt)
                at_[0] += (n * 4 + 31) // 32 * 32 / 1024
                assert at_[0] <= limit, (name, at_[0])
                return t

            return place

        small = packed(0, 4)
        ident = small("ident", [P, P])
        cc = small("cc", [P, NK])
        csil = small("csil", [P, NK])
        ce = small("ce", [P, NK])
        sscol = small("sscol", [P, 16])
        negsink = small("negsink", [P, H_B])
        sinkc = small("sinkc", [P, H_B])
        lamb = small("lamb", [P, 4, 64])
        lams = small("lams", [P, 4])
        subc = small("subc", [P, 1])
        mv = small("mv", [P, NT, 2])
        rstd = small("rstd", [P, NT])
        stat = small("stat", [P, 2, 12])
        nmA = small("nmA", [P, 32, 2])
        smA = small("smA", [P, 32, 2])
        msA = small("msA", [P, 32])
        qpad = at("qpad", 4, [P, 2, 2, P])
        adab = at("adab", 6, [P, BANK])
        A0 = at("A0", 168, [P, 4096])
        A1 = at("A1", 184, [P, 4096])
        A2 = at("A2", 120, [P, 4096])
        A5 = at("A5", 8, [P, 4096])
        xs = at("xs", 72, [P, NT, D])
        onehot = at("onehot", 40, [NBUCKET, TAB])
        relb = at("relb", 45, [NBUCKET, 12])
        btab = at("btab", 46, [12, TAB])
        flip = at("flip", 200, [P, P])
        skewA = at("skewA", 104, [P, H_A, S])
        skewB = at("skewB", 136, [P, H_B, 256])
        hraw = at("hraw", 120, [P, 2, S])
        hTh = at("hTh", 8, [P, NK, S], F32R)
        hTl = at("hTl", 40, [P, NK, S], F32R)
        Qa = at("Qa", 72, [P, H_A, S])
        Ka = at("Ka", 88, [P, H_A, S])
        Va = at("Va", 104, [P, NT, VA])
        Qb = at("Qb", 120, [P, 4, S])
        Kb = at("Kb", 136, [P, S])
        Vb = at("Vb", 140, [P, NT, P])
        biasA = at("biasA", 144, [P, H_A, S])
        biasB = at("biasB", 160, [P, H_B, 256])
        WR = [at(f"WR{i}", 168 + 16 * i, [P, 2048]) for i in range(2)]
        WL = [at(f"WL{i}", 168 + 16 * i, [P, 2048], F32R) for i in range(2)]
        WH = [at(f"WH{i}", 176 + 16 * i, [P, 2048], F32R) for i in range(2)]
        gst = at("gst", 200, [P, 2, BANK])
        vbT = at("vbT", 200, [P, S])
        modrow = at("modrow", 204, [P, BANK])
        zero1k = at("zero1k", 206, [P, 256])
        L = at("L", 8, [P, 3, 2, S])
        LB = at("LB", 8, [P, 4, 2, 256])
        aT = at("aT", 32, [P, 4, BANK])
        A3 = at("A3", 40, [P, 4096])
        A4 = at("A4", 56, [P, 4096])
        nmB = at("nmB", 200, [P, 32, 2])
        smB = at("smB", 200.5, [P, 32, 2])
        junk = at("junk", 201, [P, P])
        Oh = at("Oh", 8, [P, NK, S], F32R)
        Ol = at("Ol", 40, [P, NK, S], F32R)
        gin = at("gin", 136, [P, 2, 2, BANK])
        mTh = at("mTh", 72, [P, NK, S], F32R)
        mTl = at("mTl", 104, [P, NK, S], F32R)
        WOR = [at("WOR0", 144, [P, NK, BANK]), at("WOR1", 24, [P, NK, BANK])]
        WOL = [at("WOL0", 144, [P, NK, BANK], F32R), at("WOL1", 24, [P, NK, BANK], F32R)]
        WOH = [at("WOH0", 8, [P, NK, BANK], F32R), at("WOH1", 40, [P, NK, BANK], F32R)]
        X2 = at("X2", 168, [P, NT, D])
        rowA = at("rowA", 56, [P, 4, D])
        sh2 = at("sh2", 136, [P, D])
        xin = at("xin", 140, [P, 1, D])
        h2 = at("h2", 160, [P, 2, D])
        h2T = at("h2T", 200, [P, NK, P])
        rwz = at("rwz", 4, [P, 16, NE])
        lg = at("lg", 206, [P, NT, NE])
        cst = packed(5, 8)
        lower = cst("lower", [P, P])
        iota = cst("iota", [P, P])
        before = cst("before", [P, NE, NE])
        rev = cst("rev", [P, NE + NG])
        tokid = cst("tokid", [P, NT])
        rbias = cst("rbias", [P, NE])
        mul8 = cst("mul8", [P, 8])
        keep = packed(204, 206)
        wk = keep("wk", [P, 2, NT])
        slot_u = keep("slot_u", [P, 2, NT], U32)
        idx_u = keep("idx_u", [P, MAXBLK], U32)
        blk_t = keep("blk_t", [P, MAXBLK], I32)
        turn_e = keep("turn_e", [P, NE], I32)
        freed_i = keep("freed_i", [P, NE + 3], I32)
        nturn_i = keep("nturn_i", [P, 2], I32)
        nblk_i = keep("nblk_i", [P, 1], I32)
        idx_c = keep("idx_c", [P, 1], U32)
        rt = packed(120, 136)
        s_ = rt("sco", [P, NT, NE])
        bi = rt("bia", [P, NT, NE])
        t0 = rt("t0", [P, NT, NE])
        t1 = rt("t1", [P, NT, NE])
        oh = [rt("oh0", [P, NT, NE]), rt("oh1", [P, NT, NE])]
        g0_, g1_, g2_, g3_, g4_ = (rt(f"g{i}", [P, NT, NG]) for i in range(5))
        m1 = rt("m1", [P, NT])
        ms_ = rt("ms", [P, 2, NT])
        Mex = rt("Mex", [P, NT, NE])
        rank = rt("rank", [P, NT, NE])
        cnt = rt("cnt", [P, NE])
        nb_ = rt("nb", [P, NE])
        pst = rt("pst", [P, NE])
        pen = rt("pen", [P, NE])
        live = rt("live", [P, NE])
        before2 = rt("before2", [P, NE, NE])
        iota2 = rt("iota2", [P, MAXBLK])
        turn = rt("turn", [P, NE])
        sel = rt("sel", [P, NE, NE])
        sel2 = rt("sel2", [P, NE, NE])
        tf = rt("tf", [P, NE])
        ff = rt("ff", [P, NE + 3])
        big = rt("big", [P, MAXBLK, NE])
        ef = rt("ef", [P, MAXBLK])
        Rk = rt("Rk", [P, 2, NT])
        Pk = rt("Pk", [P, 2, NT])
        rb_ = rt("rb", [P, 2, NT])
        c8 = rt("c8", [P, 2 * NT * 8])
        ones = rt("ones", [P, P])
        Aoh = at("Aoh", 144, [P, 16, P], F32R)
        bsel = at("bsel", 154, [P, 16, MAXBLK])
        Boh = at("Boh", 152, [P, 16, MAXBLK], F32R)
        NSLOT, SLOT = 3, 12 * 1024
        EXP = at("EXP", 8, [P, NSLOT * SLOT])
        xg = at("xg", 4, [P, D])
        RH = [at(f"RH{i}", 152 + 8 * i, [P, 1024], F32R) for i in range(4)]
        RL = [at(f"RL{i}", 156 + 8 * i, [P, 1024], F32R) for i in range(4)]
        xTh = at("xTh", 184, [P, NK, P], F32R)
        xTl = at("xTl", 188, [P, NK, P], F32R)
        sig = at("sig", 192, [P, FE])
        hh = at("hh", 194, [P, FE])
        hhTh = at("hhTh", 196, [P, 4, P], F32R)
        hhTl = at("hhTl", 198, [P, 4, P], F32R)
        ysb = at("ysb", 200, [P, D])
        yg = at("yg", 152, [P, 4, 2, D])
        r2 = at("r2", 184, [P, 4, D])

        ps = ctx.enter_context(nc.psum_tensor("ps", [P, 8 * BANK], F32))

        def bank(b, n=BANK, w=1):
            return ps[:, b * BANK:b * BANK + (w - 1) * BANK + n]

        small_in = sem("small_in")
        x_in = [sem(f"x_in{i}") for i in range(4)]
        slot_in = {n: sem(f"slot_in_{n}") for n in ("A0", "A1", "A2", "A3", "A4", "A5", "R0", "R1")}
        w_hi, w_lo = sem("w_hi"), sem("w_lo")
        h_hi, gst_out = sem("h_hi"), [sem("gst_out0"), sem("gst_out1")]
        gin_in = [sem("gin_in0"), sem("gin_in1")]
        wo_in, wo_hi, wo_lo = [sem("wo_in0"), sem("wo_in1")], sem("wo_hi"), sem("wo_lo")
        c_in, adab_in = sem("c_in"), sem("adab_in")
        padz = sem("padz")
        silu_e, silu_v = sem("silu_e"), sem("silu_v")
        ln0, ln0_sq = sem("ln0"), sem("ln0_sq")
        btab_mm, btab_ev, btab_out, btab_in, mask_set = (sem("btab_mm"), sem("btab_ev"), sem("btab_out"),
                                                         sem("btab_in"), sem("mask_set"))
        zero_set, y_zero, pool_go, load_go = sem("zero_set"), sem("y_zero"), sem("pool_go"), sem("load_go")
        lam_v, lam_e = sem("lam_v"), sem("lam_e")
        ada_mm, ada_ev, ada_out, ss_mm, ss_one = (sem("ada_mm"), sem("ada_ev"), sem("ada_out"), sem("ss_mm"),
                                                  sem("ss_one"))
        xt_mm, xt_a = sem("xt_mm"), sem("xt_a")
        o_hi = sem("o_hi")
        proj_mm, proj_v, proj_a = sem("proj_mm"), sem("proj_v"), sem("proj_a")
        padA, scoreA, logitA, expA, attnA, trA, aT_ev, pvA, oA = (sem("padA"), sem("scoreA"), sem("logitA"), sem("expA"), sem("attnA"),
                                                    sem("trA"), sem("aT_ev"), sem("pvA"), sem("oA"))
        padB, scoreB, logitB, expB, trB, bT_ev, pvB, oB = (sem("padB"), sem("scoreB"), sem("logitB"), sem("expB"), sem("trB"),
                                             sem("bT_ev"), sem("pvB"), sem("oB"))
        fin_v, fin_a, finT, finT_v = sem("fin_v"), sem("fin_a"), sem("finT"), sem("finT_v")
        merge_mm, merged = sem("merge_mm"), sem("merged")
        rows_in, rows_one, rowB_in = sem("rows_in"), sem("rows_one"), sem("rowB_in")
        xin_in, y_mm, post_v, post_a, h2_out = (sem("xin_in"), sem("y_mm"), sem("post_v"), sem("post_a"),
                                                sem("h2_out"))
        h2T_mm, h2T_ev, rout_mm, rout_ev, rwp_v = (sem("h2T_mm"), sem("h2T_ev"), sem("rout_mm"), sem("rout_ev"),
                                                   sem("rwp_v"))
        rt_in, route, route_a, rank_mm, idx_mm, tabs = (sem("rt_in"), sem("route"), sem("route_a"), sem("rank_mm"),
                                                        sem("idx_mm"), sem("tabs"))
        exp_in, exp_ready, x2_out = [sem(f"exp_in_{n}") for n in ("w1", "w3", "w2")], sem("exp_ready"), sem("x2_out")
        x2_in = sem("x2_in")
        idx_ok, gathered, xg_tr, xT_hi, xT_lo = (sem("idx_ok"), sem("gathered"), sem("xg_tr"), sem("xT_hi"),
                                                 sem("xT_lo"))
        chunk_hi, chunk_lo, chunk_used = sem("chunk_hi"), sem("chunk_lo"), sem("chunk_used")
        sig_a, silu_g, hh_v, hh_tr, hhT_hi, hhT_lo = (sem("sig_a"), sem("silu_g"), sem("hh_v"), sem("hh_tr"),
                                                      sem("hhT_hi"), sem("hhT_lo"))
        y_a, y_out = sem("y_a"), sem("y_out")
        comb_in = [sem(f"comb_in{i}") for i in range(4)]
        finq = sem("finq")
        RANK_READY, OH_READY = [0], [0]
        comb, comb_w0, comb_norm, comb_rs, comb_out, res_out = (sem("comb"), sem("comb_w0"), sem("comb_norm"), sem("comb_rs"), sem("comb_out"),
                                                       [sem(f"res_out{i}") for i in range(4)])

        POST = 16
        COMB = 9

        w_rows = w_in.rearrange("a (k p) n -> p (a k) n", p=P)
        ada_rows = ada_w.rearrange("a s (k p) n -> p (a s) k n", p=P)
        wo_rows = w_out.rearrange("a (k p) n -> p (a k) n", p=P)
        wa_rows = w_a.rearrange("a (k p) n -> p (a k) n", p=P)
        wb_rows = w_b.rearrange("a (j t p) n -> j p (a t) n", j=2, p=64)
        ADA_AT = [7 + 3 * i for i in range(8)]
        NA_CH = 12
        adas = {"A0": A0, "A1": A1, "A2": A2, "A3": A3, "A4": A4, "A5": A5}
        ADA_SLOT = ["A0", "A1", "A2", "A5"] + ["A3", "A4"] * 4

        def ada_src(ch):
            rd, kp = ch // 4, ch % 4
            c0 = rd * 2048
            parts = []
            while c0 < (rd + 1) * 2048:
                sub, off = c0 // 3072, c0 % 3072
                n = min(3072 - off, (rd + 1) * 2048 - c0)
                parts.append((c0 - rd * 2048, n, ada_rows[:, sub, 2 * kp:2 * kp + 2, off:off + n]))
                c0 += n
            return parts

        chunks = ([("ka", i) for i in range(2)] + [("va", i) for i in range(2)] + [("qa", i) for i in range(2)]
                  + [("kv", 0)] + [("qb", i) for i in range(2)] + [("gl", i) for i in range(8)]
                  + [("br", i) for i in range(4)])
        NPC = 17
        COL = {"va": COL_V, "ka": COL_K, "qa": COL_Q, "kv": COL_KB, "qb": COL_QB, "gl": COL_G}
        groups = []
        for ci in range(NPC):
            kind, i = chunks[ci]
            for q in range(4):
                k2 = ("kb" if q < 2 else "vb") if kind == "kv" else kind
                eng_ = "a" if kind == "gl" or len(groups) % 2 else "v"
                groups.append((ci, k2, 4 * i + q if kind != "kv" else q % 2, eng_))
            if ci == 1:
                FLIP0 = len(groups)
                groups += [(ci, "fl", q, "va"[q % 2]) for q in range(12)]
            if ci == 8:
                groups += [(ci, "vt", 0, "v"), (ci, "vt", 1, "a")]
        NGRP = len(groups)
        NVG = sum(g[3] == "v" for g in groups)
        NAG = NGRP - NVG

        LAST = [max(g for g in range(NGRP) if groups[g][0] == ci) for ci in range(NPC)]

        def used(eng, ci):
            if ci < NPC:
                eng.wait_ge(proj_mm, LAST[ci] + 1)
            else:
                eng.wait_ge(merge_mm, 8 * (ci - NPC + 1))

        def taken(g):
            return sum(x[3] == groups[g][3] for x in groups[:g + 1])

        def chunk_src(ci):
            kind, i = chunks[ci]
            if kind == "br":
                lo_ = WR[ci % 2][:, :].rearrange("p (g k n) -> p g k n", g=2, k=4)
                c0 = i * 256
                return [(lo_[:, 0], wa_rows[:, :, c0:c0 + 256])] + [
                    (lo_[64 * j:64 * j + 64, 1], wb_rows[j][:, :, c0:c0 + 256]) for j in range(2)]
            v = WR[ci % 2][:, :].rearrange("p (k n) -> p k n", k=NK)
            c0 = COL[kind]
            if kind == "qb":
                return [(v[:, :, (2 * t + j) * 64:(2 * t + j + 1) * 64],
                         w_rows[:, :, c0 + (4 * j + 2 * i + t) * 64:c0 + (4 * j + 2 * i + t + 1) * 64])
                        for t in range(2) for j in range(2)]
            return [(v[:, :, :], w_rows[:, :, c0 + i * 256:c0 + (i + 1) * 256])]

        def chunk_in(eng, ci):
            n = sum(len(chunk_src(q)) for q in range(ci % 2, ci + 1, 2))
            eng.wait_ge(slot_in[f"R{ci % 2}"], 16 * n)

        def ada_in(eng, ch):
            n = sum(len(ada_src(q)) for q in range(ch + 1) if ADA_SLOT[q] == ADA_SLOT[ch])
            eng.wait_ge(slot_in[ADA_SLOT[ch]], 16 * n)

        def ngrp(i):
            return i // 4 + 1

        def grp0(v):
            return (v // NT) * 12 + sum(ngrp(i) for i in range(v % NT))

        def proj_dst(g):
            _, kind, q, _ = groups[g]
            if kind == "va":
                return Va[:, 2 * (q % 4):2 * (q % 4) + 2, (q // 4) * 256:(q // 4) * 256 + 256], 1.0
            cols = slice((q % 2) * 512, (q % 2) * 512 + 512)
            if kind == "ka":
                return Ka[:, q // 2, cols], 1.0
            if kind == "qa":
                return Qa[:, q // 2, cols], SQ
            if kind == "qb":
                return Qb[:, q // 2, cols], SQ
            if kind == "kb":
                return Kb[:, cols], 1.0
            if kind == "vb":
                return vbT[:, cols], 1.0
            if kind == "fl":
                return flip_group(q)[1], 1.0
            if kind == "vt":
                return Vb[:, 4 * q:4 * q + 4, :].rearrange("p t n -> p (t n)"), 1.0
            raise ValueError(kind)

        def comb_row(nturn, n):
            return EXP[:, bass.ds((nturn % NSLOT) * SLOT + n * D, D)]

        NCH = 12

        def expert_slot(eng, b):
            e1 = eng.value_load(blk_t[0:1, bass.ds(b, 1)], min_val=1, max_val=NE)
            return e1, ((e1 + (NSLOT - 1)) % NSLOT) * SLOT

        def flip_group(g):
            if g < 8:
                return (skewA[:, g // 2, (g % 2) * 512:(g % 2) * 512 + 512], biasA[:, g // 2, (g % 2) * 512:(g % 2) * 512 + 512])
            g -= 8
            return (skewB[:, 2 * g:2 * g + 2, :].rearrange("p h n -> p (h n)"),
                    biasB[:, 2 * g:2 * g + 2, :].rearrange("p h n -> p (h n)"))

        block = ctx.enter_context(nc.Block())

        def bc(row, n=P):
            return bass.AP(row.tensor, row.offset, [[0, n]] + [list(v) for v in row.ap[-1:]])

        def load_adab(eng, rd):
            for j in range(4):
                eng.dma_start(adab[32 * j:32 * j + 32, :], bass.AP(ada_b.tensor, (4 * rd + j) * 512, [[0, 32], [1, 512]])
                              ).then_inc(adab_in, 16)

        @block.sync
        def _(sp):
            xr = x.rearrange("a (t p) d -> p (a t) d", p=P)

            def load_ada(ch):
                slot = ADA_SLOT[ch]
                prev = [q for q in range(ch) if ADA_SLOT[q] == slot]
                if prev:
                    sp.wait_ge(ada_mm, prev[-1] + 1)
                v = adas[slot][:, :].rearrange("p (k n) -> p k n", k=2)
                for a, n, src in ada_src(ch):
                    sp.dma_start(v[:, :, a:a + n], src).then_inc(slot_in[slot], 16)

            def load_chunk(ci):
                if ci >= 2:
                    used(sp, ci - 2)
                for dst, src in chunk_src(ci):
                    sp.dma_start(dst, src).then_inc(slot_in[f"R{ci % 2}"], 16)

            def load_x(i):
                sp.dma_start(xs[:, 2 * i:2 * i + 2, :], xr[:, 2 * i:2 * i + 2, :]).then_inc(x_in[i], 16)

            load_x(0)
            load_x(1)
            sp.wait_ge(small_in, 112)
            load_x(2)
            load_x(3)
            load_ada(0)
            sp.wait_ge(btab_ev, 3)
            sp.dma_start(bias_d.ap(), btab[:, :]).then_inc(btab_out, 16)
            load_ada(1)
            load_ada(2)
            load_ada(3)
            for ci in range(2):
                sp.wait_ge(ada_mm, ci + 1)
                load_chunk(ci)
            sp.wait_ge(btab_out, 16)
            sp.dma_start(skewA[:, :, :], bass.AP(bias_d, 0, [[1, P], [TAB, H_A], [1, S]])).then_inc(btab_in, 16)
            sp.dma_start(skewB[:, :, :], bass.AP(bias_d, H_A * TAB + 768, [[1, P], [TAB, H_B], [1, 256]])).then_inc(btab_in, 16)
            sp.wait_ge(ada_ev, 1)
            load_adab(sp, 1)
            for ci in range(2, NPC + 2):
                load_chunk(ci)
            used(sp, NPC - 1)
            load_ada(4)
            load_ada(5)
            sp.wait_ge(zero_set, 1)
            for q in range(4):
                sp.dma_start(y_d[16 * P:MAXBLK * P, q * 256:(q + 1) * 256].rearrange("(a p) n -> p a n", p=P),
                             zero1k[:, :].unsqueeze(1).to_broadcast([P, 16, 256])).then_inc(y_zero, 16)
            for ch in range(6, NA_CH):
                load_ada(ch)
                if ch == 9:
                    sp.wait_ge(ada_ev, 2)
                    sp.dma_start(mod_d[4:8, :], modrow[0:P:32, :]).then_inc(ada_out, 16)
                    load_adab(sp, 2)
            sp.wait_ge(ada_ev, 3)
            sp.dma_start(mod_d[8:12, :], modrow[0:P:32, :]).then_inc(ada_out, 16)
            sp.wait_ge(logitA, 64)
            sp.dma_start(WOR[0][:, :, :], wo_rows[:, :, 0:512]).then_inc(wo_in[0], 16)
            sp.wait_ge(gst_out[0], 16 * 16)
            sp.wait_ge(gst_out[1], 16 * 16)
            sp.wait_ge(pvB, 32)
            for m in range(16):
                if m >= 2:
                    sp.wait_ge(merged, 5 * (m - 1))
                for g in range(2):
                    sp.dma_start(gin[:, m % 2, g, :], gate_d[g * NK + m // 2, m % 2]).then_inc(gin_in[m % 2], 16)
                if m in (4, 8):
                    load_chunk(NPC + 2 + (m // 4 - 1))
            for dst, src in [(rwz[:, 0:NK, :], router_w.rearrange("(k p) e -> p k e", p=P)), (lower[:, :], lower_h),
                             (iota[:, :], iota_h), (rev[:, :], rev_h),
                             (before[:, :, :], before_h.rearrange("p (a b) -> p a b", a=NE)),
                             (tokid[:, :], tokid_h), (rbias[:, :], bass.AP(router_b.tensor, 0, [[0, P], [1, NE]]))]:
                sp.dma_start(dst, src).then_inc(rt_in, 16)
            sp.wait_ge(merge_mm, 32)
            sp.dma_start(WOR[1][:, :, :], wo_rows[:, :, 512:1024]).then_inc(wo_in[1], 16)
            sp.wait_ge(ada_out, 32)

            def row(dst, src, signal):
                sp.dma_start(dst, bass.AP(src.tensor, src.offset, [[0, P], [1, D]])).then_inc(signal, 16)

            row(rowA[:, 0, :], mod_d[4:6, :], rows_in)
            row(rowA[:, 1, :], ln_g[0, 0], rows_in)
            row(rowA[:, 2, :], ln_b[0, 0], rows_in)
            row(rowA[:, 3, :], mod_d[8:10, :], rows_in)
            sp.wait_ge(merged, 80)
            row(sh2[:, :], mod_d[6:8, :], rows_in)
            w1r = w1.rearrange("a e (k p) n -> p (a e) k n", p=P)
            w3r = w3.rearrange("a e (k p) n -> p (a e) k n", p=P)
            w2r = w2.rearrange("a e (k p) n -> p (a e) k n", p=P)

            def load_matrix(m, e, off):
                src, k = ((w1r, NK), (w3r, NK), (w2r, 4))[m]
                c0 = off + m * 4096
                dst = EXP[:, c0:c0 + 4096] if isinstance(off, int) else EXP[:, bass.ds(c0, 4096)]
                sp.dma_start(dst.rearrange("p (k n) -> p k n", k=k),
                             src[:, bass.ds(e, 1), :, :].rearrange("p e k n -> p (e k) n")).then_inc(exp_in[m], 16)

            xt = x.rearrange("a (t p) d -> t p (a d)", p=P)
            for t in range(NT):
                if t >= 1:
                    sp.wait_ge(post_v, POST * (t - 1) + 2)
                sp.dma_start(xin[:, 0, :], xt[t]).then_inc(xin_in, 16)
                if t >= 1:
                    sp.wait_ge(post_v, POST * t)
                    sp.dma_start(h2_d[(t - 1) * P:t * P, :], h2[:, (t - 1) % 2, :]).then_inc(h2_out, 16)
                    sp.dma_start(x2_d[(t - 1) * P:t * P, :], X2[:, t - 1, :]).then_inc(x2_out, 16)
            sp.wait_ge(y_mm, 2 * NT)
            for m in range(3):
                load_matrix(m, 0, 0)
            sp.wait_ge(post_v, POST * NT)
            sp.dma_start(h2_d[(NT - 1) * P:NT * P, :], h2[:, (NT - 1) % 2, :]).then_inc(h2_out, 16)
            sp.dma_start(x2_d[(NT - 1) * P:NT * P, :], X2[:, NT - 1, :]).then_inc(x2_out, 16)
            for m in range(3):
                sp.wait_ge(exp_in[(m + 1) % 3], 32 if m == 2 else 16)
                load_matrix(m, 1, SLOT)
            sp.wait_ge(tabs, 3)
            sp.wait_ge(gathered, 16)
            nturn = sp.value_load(nturn_i[0:1, 0:1], min_val=NSLOT, max_val=NE)

            def wait_reg(sem_, value):
                sp.wait_ge(sem_, value)
                sp.sem_inc(load_go, 1)

            before_last = sp.value_load(nturn_i[0:1, 1:2], min_val=NSLOT - 1, max_val=NE - 1)
            with sp.Fori(1, before_last) as j:
                for m in range(3):
                    wait_reg(exp_in[m], j * 16)
                sp.sem_inc(exp_ready, 1)
                freed = sp.value_load(freed_i[0:1, bass.ds(j + 1, 1)], min_val=1, max_val=MAXBLK)
                wait_reg(chunk_lo, freed * NCH)
                e = sp.value_load(turn_e[0:1, bass.ds(j + 1, 1)], min_val=0, max_val=NE - 1)
                for m in range(3):
                    wait_reg(exp_in[(m + 1) % 3], j * 16 + (32 if m == 2 else 16))
                    load_matrix(m, e, ((j + 1) % NSLOT) * SLOT)
            for m in range(3):
                wait_reg(exp_in[m], before_last * 16)
            sp.sem_inc(exp_ready, 1)
            for m in range(3):
                wait_reg(exp_in[m], nturn * 16)
            sp.sem_inc(exp_ready, 1)
            freed = sp.value_load(freed_i[0:1, bass.ds(nturn, 1)], min_val=1, max_val=MAXBLK)
            wait_reg(chunk_lo, freed * NCH)
            sp.wait_ge(x2_out, 16 * NT)
            for n_, src in enumerate((mod_d[10:12, :], ln_g[0, 1], ln_b[0, 1])):
                row(comb_row(nturn, NT + n_), src, rowB_in)
            x2r = EXP[:, bass.ds((nturn % NSLOT) * SLOT, NT * D)].rearrange("p (t d) -> p t d", t=NT)
            sp.dma_start(x2r, x2_d.ap().rearrange("(t p) d -> p t d", p=P)).then_inc(x2_in, 16)
            for t in range(NT):
                sp.wait_ge(comb_out, t + 1)
                sp.dma_start(out.rearrange("a (t p) d -> t p (a d)", p=P)[t], r2[:, t % 4, :]).then_inc(res_out[t % 4], 16)
            for i in range(4):
                sp.wait_ge(res_out[i], 16 * NT // 4)
            sp.wait_ge(ada_out, 32)
            sp.wait_ge(h2_out, 16 * NT)
            sp.wait_ge(x2_out, 16 * NT)

        @block.gpsimd
        def _(pool):
            nc.gpsimd.memset(qpad[:, :, :, :], 0.0).then_inc(padz, 1)
            pool.wait_ge(padz, 1)
            for g in range(FLIP0 + 10, FLIP0 + 12):
                pool.wait_ge(proj_a if groups[g][3] == "a" else proj_v, taken(g))
            nc.gpsimd.memset(biasA[0:64, :, S - 64:S], NEG).then_inc(mask_set, 1)
            for n_, region in enumerate((biasB[0:64, :, 0:64], biasB[0:64, :, 192:256], biasB[64:128, :, 0:128])):
                pool.wait_ge(mask_set, n_ + 1)
                nc.gpsimd.memset(region, NEG).then_inc(mask_set, 1)
            pool.wait_ge(mask_set, 4)
            nc.gpsimd.memset(zero1k[:, :], 0.0).then_inc(zero_set, 1)
            for g in [x for x in range(NGRP) if groups[x][1] == "qa"][-2:]:
                pool.wait_ge(proj_a if groups[g][3] == "a" else proj_v, taken(g))
            for u in range(32):
                h, i = u // NT, u % NT
                if u >= 2:
                    pool.wait_ge(scoreA, 2 * (u - 1))
                for m in range(2):
                    pool.wait_ge(*((padA, 2 * u + m) if u + m else (zero_set, 1)))
                    nc.gpsimd.tensor_copy(qpad[64 * m:64 * m + 64, u % 2, m, :],
                                          Qa[64 * m:64 * m + 64, h, i * P:(i + 1) * P]).then_inc(padA, 1)
            for u in range(32):
                i, t = u // 4, u % 4
                pool.wait_ge(scoreA, 64) if u == 0 else None
                if u >= 2:
                    pool.wait_ge(scoreB, 2 * (u - 1))
                for m in range(2):
                    pool.wait_ge(*((padB, 2 * u + m) if u + m else (padA, 64)))
                    nc.gpsimd.tensor_copy(qpad[64 * m:64 * m + 64, u % 2, m, :],
                                          Qb[64 * m:64 * m + 64, t, i * P:(i + 1) * P]).then_inc(padB, 1)
            pool.wait_ge(tabs, 1)
            pool.wait_ge(h2_out, 16 * NT)
            nblk = pool.value_load(nblk_i[0:1, 0:1], min_val=16, max_val=31)

            def gather(col):
                nc.gpsimd.indirect_dma_start(
                    out=xg[:, :], out_offset=None, in_=h2_d.ap(),
                    in_offset=bass.IndirectOffsetOnAxis(ap=idx_c[:, 0:1], axis=0)).then_inc(gathered, 16)

            nc.gpsimd.tensor_copy(idx_c[:, 0:1], idx_u[:, 0:1]).then_inc(idx_ok, 1)
            pool.wait_ge(idx_ok, 1)
            gather(0)
            with pool.Fori(1, nblk + 1) as b:
                pool.wait_ge(gathered, b * 16)
                nc.gpsimd.tensor_copy(idx_c[:, 0:1], idx_u[:, bass.ds(b, 1)]).then_inc(idx_ok, 1)
                pool.wait_ge(idx_ok, b + 1)
                pool.wait_ge(xg_tr, b * 2)
                pool.sem_inc(pool_go, 1)
                gather(b)
            pool.wait_ge(y_out, nblk * 16 + 16)
            pool.wait_ge(gathered, nblk * 16 + 16)
            pool.wait_ge(xg_tr, nblk * 2 + 2)
            pool.sem_inc(pool_go, 1)

            def rows_of(t):
                for k in range(2):
                    nc.gpsimd.indirect_dma_start(
                        out=yg[:, t % 4, k, :], out_offset=None, in_=y_d.ap(),
                        in_offset=bass.IndirectOffsetOnAxis(ap=slot_u[:, k, t:t + 1], axis=0)
                    ).then_inc(comb_in[t % 4], 16)

            nturn = pool.value_load(nturn_i[0:1, 0:1], min_val=NSLOT, max_val=NE)
            for t in range(4):
                rows_of(t)
            for t in range(NT + 1):
                if t < NT:
                    if t + 4 < NT:
                        pool.wait_ge(comb_w0, t + 1)
                        pool.wait_ge(comb, COMB * t + 1)
                        rows_of(t + 4)
                if t >= 1:
                    pool.wait_ge(comb_norm, t)
                    R = r2[:, (t - 1) % 4, :]
                    nc.gpsimd.tensor_tensor(R, R, comb_row(nturn, NT + 2), ALU.add).then_inc(comb_out, 1)

        @block.scalar
        def _(act):
            act.dma_start(cc[:, :], c.rearrange("a (k p) -> p (a k)", p=P)).then_inc(c_in, 16)
            for dst, src in [(relb[:, :], rel_bias), (onehot[:, :], onehot_h), (flip[:, :], flip_h), (ident[:, :], ident_h),
                             (lamb[:, :, :], bass.AP(lam.tensor, 0, [[0, P], [64, 4], [1, 64]])),
                             (sinkc[:, :], bass.AP(sinks.tensor, 0, [[0, P], [1, H_B]])),
                             (subc[:, :], subln_w.rearrange("a (p o) -> p (a o)", o=1))]:
                act.dma_start(dst, src).then_inc(small_in, 16)
            load_adab(act, 0)
            act.wait_ge(c_in, 16)
            nc.scalar.activation(ce[:, :], cc[:, :], ACT.Exp, scale=-1.0).then_inc(silu_e, 1)
            act.wait_ge(lam_v, 2)
            nc.scalar.activation(lams[:, 2:4], lams[:, 0:2], ACT.Exp).then_inc(lam_e, 1)
            act.wait_ge(btab_mm, 2)
            nc.scalar.copy(btab[:, 384:768], ps[0:12, 6 * BANK:6 * BANK + 384]).then_inc(btab_ev, 1)
            act.wait_ge(ln0, 25)
            nc.scalar.activation(rstd[:, :], rstd[:, :], ACT.Sqrt).then_inc(ln0_sq, 1)
            act.wait_ge(ss_one, 2)
            for k in range(NK):
                act.wait_ge(xt_mm, k + 1)
                if k >= 2:
                    act.wait_ge(h_hi, 2 * (k - 1))
                nc.scalar.activation(hraw[:, k % 2, :], ps[:, (1 + 2 * (k % 3)) * BANK:(3 + 2 * (k % 3)) * BANK],
                                     ACT.Identity, bias=sscol[:, k:k + 1], scale=sscol[:, 8 + k:9 + k]).then_inc(xt_a, 1)

            def high(ci):
                chunk_in(act, ci)
                if ci >= 2:
                    used(act, ci - 2)
                nc.scalar.copy(WH[ci % 2][:, :], WR[ci % 2][:, :]).then_inc(w_hi, 1)

            high(0)
            high(1)
            for g, (ci, kind, q, eng_) in enumerate(groups):
                if eng_ == "a":
                    act.wait_ge(proj_mm, g + 1)
                    if kind == "gl":
                        d, hf = q // 2, q % 2
                        n = d * 2 + hf
                        if n >= 2:
                            act.wait_ge(gst_out[n % 2], 16 * (n // 2))
                        nc.scalar.activation(gst[:, n % 2, :], bank(g % 8), ACT.Sigmoid).then_inc(proj_a, 1)
                        act.wait_ge(proj_a, taken(g))
                        act.dma_start(gate_d[d, hf], gst[:, n % 2, :]).then_inc(gst_out[n % 2], 16)
                    else:
                        dst, scale = proj_dst(g)
                        src = bank(g % 8)
                        if kind == "va":
                            src = src.rearrange("p (t n) -> p t n", t=2)
                        nc.scalar.activation(dst, src, ACT.Copy, scale=scale).then_inc(proj_a, 1)
                if g == LAST[ci] and ci < NPC - 1:
                    high(ci + 2)
            act.wait_ge(gst_out[0], 16 * 16)
            act.wait_ge(gst_out[1], 16 * 16)
            for u in range(32 + 3):
                if u == 5:
                    high(NPC + 1)
                v = u - 2
                if 0 <= v < 32:
                    i = v % NT
                    for g in range(ngrp(i)):
                        gg = grp0(v) + g
                        w = min(4, i + 1 - 4 * g) * P
                        act.wait_ge(trA, gg + 1)
                        if gg >= 4:
                            act.wait_ge(pvA, gg - 3)
                        nc.scalar.copy(aT[:, gg % 4, 0:w], bank(4 + gg % 2, w)).then_inc(aT_ev, 1)
                v = u - 3
                if v >= 0:
                    h, i = v // NT, v % NT
                    act.wait_ge(pvA, grp0(v) + ngrp(i))
                    nc.scalar.copy(Qa[:, h, i * P:(i + 1) * P], bank(6, P)).then_inc(oA, 1)
                    act.wait_ge(oA, 2 * v + 1)
                    nc.scalar.activation(junk[:, :], Qa[:, h, i * P:(i + 1) * P], ACT.Square,
                                         accum_out=msA[:, v:v + 1]).then_inc(oA, 1)
                if u < 32:
                    n = P * (u % NT + 1)
                    for m in range(2):
                        act.wait_ge(logitA, 2 * u + m + 1)
                        nc.scalar.activation(L[:, u % 3, m, 0:n], L[:, u % 3, m, 0:n], ACT.Exp, bias=nmA[:, u, m:m + 1],
                                             scale=-1.0, accum_out=smA[:, u, m:m + 1]).then_inc(expA, 1)
            for u in range(32 + 2):
                v = u - 2
                if v >= 0:
                    act.wait_ge(trB, v + 1)
                    if v >= 4:
                        act.wait_ge(pvB, v - 3)
                    n = BANK if v // 4 else 256
                    nc.scalar.copy(aT[:, v % 4, 0:n], bank(4 + v % 2, n)).then_inc(bT_ev, 1)
                if u < 32:
                    i = u // 4
                    a = 0 if i else P
                    for j in range(2):
                        act.wait_ge(logitB, 2 * u + j + 1)
                        nc.scalar.activation(LB[:, u % 4, j, a:256], LB[:, u % 4, j, a:256], ACT.Exp, bias=nmB[:, u, j:j + 1],
                                             scale=-1.0, accum_out=smB[:, u, j:j + 1]).then_inc(expB, 1)
                if u == 8:
                    act.wait_ge(fin_v, 1)
                    nc.scalar.activation(msA[:, :], msA[:, :], ACT.Sqrt).then_inc(fin_a, 1)
            act.wait_ge(fin_v, 6)
            nc.scalar.activation(nmB[:, :, :], nmB[:, :, :], ACT.Exp).then_inc(fin_a, 1)
            for f in range(16):
                act.wait_ge(finT, f + 1)
                cols = slice((f % 2) * 512, (f % 2) * 512 + 512)
                if f < 8:
                    nc.scalar.activation(Oh[:, f // 2, cols], bank(f % 8), ACT.Copy, scale=subc[:, 0:1]).then_inc(o_hi, 1)
                else:
                    nc.scalar.copy(Oh[:, f // 2, cols], bank(f % 8)).then_inc(o_hi, 1)
            for ci in (NPC + 2, NPC + 3):
                high(ci)
            act.wait_ge(merge_mm, 32)
            for n in range(2):
                act.wait_ge(wo_in[n], 16)
                for k in range(NK):
                    nc.scalar.copy(WOH[n][:, k, :], WOR[n][:, k, :]).then_inc(wo_hi, 1)
            for t in range(NT):
                act.wait_ge(post_v, POST * t + 6)
                nc.scalar.activation(rstd[:, 0:1], rstd[:, 0:1], ACT.Sqrt).then_inc(post_a, 1)
                act.wait_ge(post_v, POST * t + 13)
                nc.scalar.activation(rstd[:, 1:2], rstd[:, 1:2], ACT.Sqrt).then_inc(post_a, 1)
                act.wait_ge(h2T_mm, t + 1)
                if t >= 1:
                    act.wait_ge(rout_mm, t)
                nc.scalar.copy(h2T[:, :, :].rearrange("p k q -> p (k q)"), bank(4, BANK, 2)).then_inc(h2T_ev, 1)
            act.wait_ge(rout_ev, NT)
            nc.scalar.activation(s_[:, :, :], lg[:, :, :], ACT.Sigmoid).then_inc(route_a, 1)
            act.wait_ge(tabs, 2)
            act.wait_ge(y_zero, 64)
            nblk = act.value_load(nblk_i[0:1, 0:1], min_val=16, max_val=31)
            xThf = xTh[:, :, :].rearrange("p k q -> p (k q)")
            hhThf = hhTh[:, :, :].rearrange("p k q -> p (k q)")

            def chunk_high(off, ch):
                nc.scalar.copy(RH[ch % 4][:, :], EXP[:, bass.ds(off + ch * 1024, 1024)]).then_inc(chunk_hi, 1)

            act.wait_ge(x2_out, 16 * NT)
            act.wait_ge(xg_tr, 2)
            nc.scalar.copy(xThf, bank(2, BANK, 2)).then_inc(xT_hi, 1)
            act.sem_inc(y_out, 16)
            act.sem_inc(y_a, 1)

            def y_take(b):
                act.wait_ge(chunk_used, b * NCH + NCH)
                act.wait_ge(y_out, b * 16 + 16)
                nc.scalar.copy(ysb[:, :], bank(5, BANK, 2)).then_inc(y_a, 1)

            def y_send(b):
                act.wait_ge(y_a, b + 2)
                act.dma_start(y_d[b * P:(b + 1) * P, :] if isinstance(b, int) else y_d[bass.ds(b * P, P), :], ysb[:, :]
                              ).then_inc(y_out, 16)

            def high_block(b, first=False):
                e1, off = expert_slot(act, b)
                act.wait_ge(exp_ready, e1)
                for ch in range(NCH):
                    if not first or ch >= 4:
                        act.wait_ge(chunk_used, b * NCH + (ch - 3))
                    chunk_high(off, ch)
                    if ch == 3 and not first:
                        y_take(b - 1)
                    if ch == 5 and not first:
                        y_send(b - 1)
                    if ch == 7:
                        nc.scalar.activation(sig[:, :], bank(0), ACT.Sigmoid).then_inc(sig_a, 1)
                act.wait_ge(hh_tr, b + 1)
                for hf in range(2):
                    nc.scalar.copy(hhThf[:, hf * 256:(hf + 1) * 256], bank((4, 7)[hf], 256)).then_inc(hhT_hi, 1)
                act.wait_ge(xg_tr, b * 2 + 4)
                nc.scalar.copy(xThf, bank(2, BANK, 2)).then_inc(xT_hi, 1)

            high_block(0, first=True)
            with act.Fori(1, nblk) as b:
                high_block(b)
            y_take(nblk - 1)
            y_send(nblk - 1)
            act.wait_ge(xT_lo, nblk + 1)
            for t in range(-1, NT):
                if t + 1 < NT:
                    n_ = t + 1
                    act.wait_ge(comb_in[n_ % 4], 32 * (n_ // 4 + 1))
                    if n_ >= 4:
                        act.wait_ge(res_out[n_ % 4], 16 * (n_ // 4))
                    nc.scalar.activation(r2[:, n_ % 4, :], yg[:, n_ % 4, 0, :], ACT.Copy, scale=wk[:, 0, n_:n_ + 1]).then_inc(comb_w0, 1)
                if t >= 0:
                    act.wait_ge(comb, COMB * t + 7)
                    nc.scalar.activation(rstd[:, t:t + 1], rstd[:, t:t + 1], ACT.Sqrt).then_inc(comb_rs, 1)
                    act.wait_ge(comb, COMB * t + 9)
                    nc.scalar.activation(r2[:, t % 4, :], r2[:, t % 4, :], ACT.Copy, scale=rstd[:, t:t + 1]).then_inc(comb_norm, 1)

        @block.vector
        def _(dve):
            v = nc.vector
            dve.wait_ge(silu_e, 1)
            v.tensor_scalar(ce[:, :], ce[:, :], 1.0, None, ALU.add).then_inc(silu_v, 1)
            dve.wait_ge(silu_v, 1)
            v.reciprocal(ce[:, :], ce[:, :]).then_inc(silu_v, 1)
            dve.wait_ge(silu_v, 2)
            v.tensor_tensor(csil[:, :], ce[:, :], cc[:, :], ALU.mult).then_inc(silu_v, 1)
            dve.wait_ge(small_in, 112)
            v.tensor_tensor(lamb[:, 0:3:2, :], lamb[:, 0:3:2, :], lamb[:, 1:4:2, :], ALU.mult).then_inc(lam_v, 1)
            dve.wait_ge(lam_v, 1)
            v.tensor_reduce(lams[:, 0:2], lamb[:, 0:3:2, :], AX, ALU.add).then_inc(lam_v, 1)
            for g in (0, 2):
                dve.wait_ge(btab_mm, g + 1)
                v.tensor_copy(btab[:, g * 384:(g + 1) * 384], ps[0:12, (5 + g) * BANK:(5 + g) * BANK + 384]).then_inc(btab_ev, 1)
            v.tensor_scalar(negsink[:, :], sinkc[:, :], -1.0, None, ALU.mult).then_inc(lam_v, 1)
            dve.wait_ge(lam_e, 1)
            v.tensor_tensor(lams[:, 0:1], lams[:, 3:4], lams[:, 2:3], ALU.subtract).then_inc(lam_v, 1)
            dve.wait_ge(lam_v, 4)
            v.tensor_scalar(lams[:, 0:1], lams[:, 0:1], -LAM_INIT, None, ALU.add).then_inc(lam_v, 1)
            v.tensor_scalar(subc[:, :], subc[:, :], 1.0 - LAM_INIT, None, ALU.mult).then_inc(lam_v, 1)
            for t in range(NT):
                dve.wait_ge(x_in[t // 2], 16)
                if t >= 2:
                    dve.wait_ge(ln0, 3 * (t - 1))
                for hf in range(2):
                    v.bn_stats(stat[:, t % 2, 6 * hf:6 * hf + 6], xs[:, t, hf * 512:(hf + 1) * 512]).then_inc(ln0, 1)
                dve.wait_ge(ln0, 3 * t + 2)
                v.bn_aggr(mv[:, t, :], stat[:, t % 2, :]).then_inc(ln0, 1)
            dve.wait_ge(ln0, 24)
            v.tensor_scalar(rstd[:, :], mv[:, :, 1], EPS, None, ALU.add).then_inc(ln0, 1)
            dve.wait_ge(ln0_sq, 1)
            v.reciprocal(rstd[:, :], rstd[:, :]).then_inc(ln0, 1)
            dve.wait_ge(ln0, 26)
            for t in range(NT):
                v.tensor_scalar(xs[:, t, :], xs[:, t, :], mv[:, t, 0:1], rstd[:, t:t + 1], ALU.subtract, ALU.mult).then_inc(ln0, 1)
            dve.wait_ge(adab_in, 64)
            dve.wait_ge(ada_mm, 4)
            v.tensor_tensor(modrow[:, :], bank(0), adab[:, :], ALU.add).then_inc(ada_ev, 1)
            dve.wait_ge(ss_mm, 1)
            pc = bank(0).rearrange("p (c r o) -> p r c o", c=4, r=4)[:, :, :, 0]
            v.tensor_copy(sscol[:, 0:8].rearrange("p (r c) -> p r c", r=2), pc[:, 0:2]).then_inc(ss_one, 1)
            v.tensor_scalar(sscol[:, 8:16].rearrange("p (r c) -> p r c", r=2), pc[:, 2:4], 1.0, None, ALU.add).then_inc(ss_one, 1)
            for k in range(NK):
                dve.wait_ge(xt_a, k + 1)
                v.tensor_copy(hTh[:, k, :], hraw[:, k % 2, :]).then_inc(h_hi, 1)
                dve.wait_ge(h_hi, 2 * k + 1)
                v.tensor_tensor(hTl[:, k, :], hraw[:, k % 2, :], hTh[:, k, :].bitcast(F32), ALU.subtract).then_inc(h_hi, 1)

            def low(ci):
                dve.wait_ge(w_hi, ci + 1)
                v.tensor_tensor(WL[ci % 2][:, :], WR[ci % 2][:, :], WH[ci % 2][:, :].bitcast(F32), ALU.subtract).then_inc(w_lo, 1)

            low(0)
            low(1)
            for g, (ci, kind, q, eng_) in enumerate(groups):
                if eng_ == "v":
                    dst, scale = proj_dst(g)
                    src = bank(g % 8)
                    if kind == "va":
                        src = src.rearrange("p (t n) -> p t n", t=2)
                    dve.wait_ge(proj_mm, g + 1)
                    v.tensor_scalar(dst, src, scale, None, ALU.mult).then_inc(proj_v, 1)
                if g == LAST[ci] and ci < NPC - 1:
                    low(ci + 2)
            dve.wait_ge(mask_set, 4)
            for u in range(32 + 1):
                if u == 6:
                    low(NPC + 1)
                if u < 32:
                    h, i = u // NT, u % NT
                    n = P * (i + 1)
                    for m in range(2):
                        dve.wait_ge(scoreA, 2 * u + m + 1)
                        if u >= 3:
                            dve.wait_ge(trA, grp0(u - 3) + ngrp((u - 3) % NT))
                        if u == 0:
                            dve.wait_ge(proj_mm, NGRP)
                        v.tensor_tensor_reduce(L[:, u % 3, m, 0:n], bank(2 * m, n), biasA[:, h, S - n:S], -1.0, BIG,
                                               ALU.add, ALU.min, nmA[:, u, m:m + 1]).then_inc(logitA, 1)
                w = u - 1
                if w >= 0:
                    n = P * (w % NT + 1)
                    dve.wait_ge(expA, 2 * w + 2)
                    v.reciprocal(smA[:, w, :], smA[:, w, :]).then_inc(attnA, 1)
                    dve.wait_ge(attnA, 4 * w + 1)
                    v.tensor_scalar(smA[:, w, 1:2], smA[:, w, 1:2], lams[:, 0:1], None, ALU.mult).then_inc(attnA, 1)
                    dve.wait_ge(attnA, 4 * w + 2)
                    v.tensor_scalar(L[:, w % 3, 1, 0:n], L[:, w % 3, 1, 0:n], smA[:, w, 1:2], None, ALU.mult).then_inc(attnA, 1)
                    dve.wait_ge(attnA, 4 * w + 3)
                    v.scalar_tensor_tensor(L[:, w % 3, 0, 0:n], L[:, w % 3, 0, 0:n], smA[:, w, 0:1], L[:, w % 3, 1, 0:n],
                                           ALU.mult, ALU.add).then_inc(attnA, 1)
                if u in (ADA_AT[3] + 1, ADA_AT[7] + 2):
                    rd = 1 if u == ADA_AT[3] + 1 else 2
                    dve.wait_ge(ada_mm, 4 * (rd + 1))
                    if rd == 2:
                        dve.wait_ge(ada_out, 16)
                    dve.wait_ge(adab_in, 64 * (rd + 1))
                    v.tensor_tensor(modrow[:, :], bank(7), adab[:, :], ALU.add).then_inc(ada_ev, 1)
            cntf = [0]

            def fin(ins):
                cntf[0] += 1
                ins.then_inc(finq, 1)
                dve.wait_ge(finq, cntf[0])

            dve.wait_ge(gst_out[0], 16 * 16)
            dve.wait_ge(gst_out[1], 16 * 16)
            for u in range(32 + 4):
                if u < 32:
                    i, t = u // 4, u % 4
                    a = 0 if i else P
                    for j in range(2):
                        hd = t + 4 * j
                        dve.wait_ge(scoreB, 2 * u + j + 1)
                        if u >= 4:
                            dve.wait_ge(trB, u - 3)
                        if u == 0:
                            dve.wait_ge(trA, 48)
                        v.tensor_tensor_reduce(LB[:, u % 4, j, a:256], ps[:, (2 * (u % 2) + j) * BANK:(2 * (u % 2) + j) * BANK + 256 - a],
                                               biasB[:, hd, a:256], -1.0, negsink[:, hd:hd + 1],
                                               ALU.add, ALU.min, nmB[:, u, j:j + 1]).then_inc(logitB, 1)
                if u == 4:
                    dve.wait_ge(oA, 64)
                    v.tensor_scalar(msA[:, :], msA[:, :], 1.0 / P, EPS, ALU.mult, ALU.add).then_inc(fin_v, 1)
                if u == 11:
                    dve.wait_ge(fin_a, 1)
                    fin(v.reciprocal(msA[:, :], msA[:, :]))
                if 12 <= u < 12 + H_A:
                    h = u - 12
                    qv = Qa[:, h, :].rearrange("p (i n) -> p i n", i=NT)
                    v.tensor_tensor(qv, qv, msA[:, h * NT:(h + 1) * NT].unsqueeze(2).to_broadcast([P, NT, P]), ALU.mult
                                    ).then_inc(fin_v, 1)
                w = u - 4
                if w >= 0:
                    i, t = w // 4, w % 4
                    dve.wait_ge(pvB, w + 1)
                    src = bank(6 + w % 2, 384).rearrange("p (j n) -> p j n", j=2)[:, :, 0:64]
                    v.tensor_copy(Qb[:, t, i * P:(i + 1) * P].rearrange("p (j n) -> p j n", j=2), src).then_inc(oB, 1)
            dve.wait_ge(expB, 64)
            n4 = nmB[:, :, :].rearrange("p (i t) j -> p i t j", i=NT)
            snk = sinkc[:, :].rearrange("p (j t) -> p t j", j=2)
            v.tensor_tensor(n4, n4, snk.unsqueeze(1).to_broadcast([P, NT, 4, 2]), ALU.add).then_inc(fin_v, 1)
            dve.wait_ge(fin_a, 2)
            fin(v.tensor_tensor(smB[:, :, :], smB[:, :, :], nmB[:, :, :], ALU.add))
            fin(v.reciprocal(smB[:, :, :], smB[:, :, :]))
            dve.wait_ge(oB, 32)
            s4 = smB[:, :, :].rearrange("p (i t) j -> p t i j", i=NT)
            for t in range(4):
                qv = Qb[:, t, :].rearrange("p (i j n) -> p i j n", i=NT, j=2)
                v.tensor_tensor(qv, qv, s4[:, t].unsqueeze(3).to_broadcast([P, NT, 2, 64]), ALU.mult).then_inc(fin_v, 1)
            for f in range(16):
                cols = slice((f % 2) * 512, (f % 2) * 512 + 512)
                dve.wait_ge(o_hi, f + 1)
                hi = Oh[:, f // 2, cols].bitcast(F32)
                if f < 8:
                    v.scalar_tensor_tensor(Ol[:, f // 2, cols], bank(f % 8), subc[:, 0:1], hi, ALU.mult,
                                           ALU.subtract).then_inc(finT_v, 1)
                else:
                    v.tensor_tensor(Ol[:, f // 2, cols], bank(f % 8), hi, ALU.subtract).then_inc(finT_v, 1)
            for m in range(16):
                st, d, hf = m % 2, m // 2, m % 2
                cols = slice(hf * 512, (hf + 1) * 512)
                dve.wait_ge(gin_in[st], 32 * (m // 2 + 1))
                for g in range(2):
                    dve.wait_ge(merge_mm, 2 * m + g + 1)
                    v.tensor_tensor(gin[:, st, g, :], gin[:, st, g, :], bank(2 * (m % 4) + g), ALU.mult).then_inc(merged, 1)
                dve.wait_ge(merged, 5 * m + 2)
                v.tensor_tensor(gin[:, st, 0, :], gin[:, st, 0, :], gin[:, st, 1, :], ALU.add).then_inc(merged, 1)
                dve.wait_ge(merged, 5 * m + 3)
                v.tensor_copy(mTh[:, d, cols], gin[:, st, 0, :]).then_inc(merged, 1)
                dve.wait_ge(merged, 5 * m + 4)
                v.tensor_tensor(mTl[:, d, cols], gin[:, st, 0, :], mTh[:, d, cols].bitcast(F32), ALU.subtract).then_inc(merged, 1)
                if m in (5, 9):
                    low(NPC + 2 + (m - 5) // 4)
            for n in range(2):
                for k in range(NK):
                    dve.wait_ge(wo_hi, 8 * n + k + 1)
                    v.tensor_tensor(WOL[n][:, k, :], WOR[n][:, k, :], WOH[n][:, k, :].bitcast(F32), ALU.subtract).then_inc(wo_lo, 1)
            v.memset(rwz[:, NK:16, :], 0.0).then_inc(rwp_v, 1)
            dve.wait_ge(rows_in, 80)
            v.tensor_scalar(rowA[:, 3, :], rowA[:, 3, :], 1.0, None, ALU.add).then_inc(rows_one, 1)
            dve.wait_ge(rows_one, 1)
            for t in range(NT):
                n = [POST * t]

                def st_(ins, wait=True):
                    n[0] += 1
                    ins.then_inc(post_v, 1)
                    if wait:
                        dve.wait_ge(post_v, n[0])

                if t >= 2:
                    dve.wait_ge(y_zero, 64) if t == 2 else None
                    dve.wait_ge(rout_mm, t - 1)
                    v.tensor_copy(lg[:, t - 2, :], ps[:, 6 * BANK:6 * BANK + NE]).then_inc(rout_ev, 1)
                X, Hh = X2[:, t, :], h2[:, t % 2, :]
                dve.wait_ge(y_mm, 2 * t + 2)
                st_(v.tensor_tensor(X, bank(2 * (t % 2), BANK, 2), rowA[:, 0, :], ALU.mult))
                dve.wait_ge(xin_in, 16 * t + 16)
                st_(v.scalar_tensor_tensor(X, xin[:, 0, :], ALPHA, X, ALU.mult, ALU.add))
                for r_ in range(2):
                    dst, gain, bias_ = ((X, rowA[:, 1, :], rowA[:, 2, :]), (Hh, rowA[:, 3, :], sh2[:, :]))[r_]
                    for hf in range(2):
                        st_(v.bn_stats(stat[:, 0, 6 * hf:6 * hf + 6], X2[:, t, hf * 512:(hf + 1) * 512]), hf == 1)
                    st_(v.bn_aggr(mv[:, 0, :], stat[:, 0, :]))
                    st_(v.tensor_scalar(rstd[:, r_:r_ + 1], mv[:, 0, 1:2], EPS, None, ALU.add), False)
                    if r_ == 1 and t >= 2:
                        dve.wait_ge(h2_out, 16 * (t - 1))
                        dve.wait_ge(h2T_mm, t - 1)
                    st_(v.scalar_tensor_tensor(dst, X, mv[:, 0, 0:1], gain, ALU.subtract, ALU.mult))
                    dve.wait_ge(post_a, 2 * t + r_ + 1)
                    st_(v.reciprocal(rstd[:, r_:r_ + 1], rstd[:, r_:r_ + 1]))
                    st_(v.scalar_tensor_tensor(dst, dst, rstd[:, r_:r_ + 1], bias_, ALU.mult, ALU.add))
            for t in range(NT - 2, NT):
                dve.wait_ge(rout_mm, t + 1)
                v.tensor_copy(lg[:, t, :], ps[:, 6 * BANK:6 * BANK + NE]).then_inc(rout_ev, 1)
            q = [0]

            def ro(ins, wait=True):
                q[0] += 1
                ins.then_inc(route, 1)
                if wait:
                    dve.wait_ge(route, q[0])

            def b3(row, n):
                return row.unsqueeze(1).to_broadcast([P, NT, n])

            dve.wait_ge(rt_in, 16 * 7)
            ro(v.memset(ones[:, :], 1.0), False)
            ro(v.tensor_copy(before2[:, :, :], before[:, :, :]), False)
            ro(v.tensor_copy(iota2[:, :], iota[:, 0:MAXBLK]), False)
            dve.wait_ge(route_a, 1)
            ro(v.tensor_tensor(bi[:, :, :], s_[:, :, :], b3(rbias[:, :], NE), ALU.add))
            b4 = bi[:, :, :].rearrange("p t (g e) -> p t g e", g=NG)
            ro(v.tensor_tensor(g0_[:, :, :], b4[:, :, :, 0], b4[:, :, :, 1], ALU.max), False)
            ro(v.tensor_tensor(g1_[:, :, :], b4[:, :, :, 0], b4[:, :, :, 1], ALU.min), False)
            ro(v.tensor_tensor(g2_[:, :, :], b4[:, :, :, 2], b4[:, :, :, 3], ALU.max), False)
            ro(v.tensor_tensor(g3_[:, :, :], b4[:, :, :, 2], b4[:, :, :, 3], ALU.min))
            ro(v.tensor_tensor(g4_[:, :, :], g0_[:, :, :], g2_[:, :, :], ALU.min), False)
            ro(v.tensor_tensor(g1_[:, :, :], g1_[:, :, :], g3_[:, :, :], ALU.max))
            ro(v.tensor_tensor(g1_[:, :, :], g1_[:, :, :], g4_[:, :, :], ALU.max))
            ro(v.tensor_tensor(g0_[:, :, :], g0_[:, :, :], g2_[:, :, :], ALU.max))
            ro(v.tensor_tensor(g0_[:, :, :], g0_[:, :, :], g1_[:, :, :], ALU.add))

            def first_max(dst, src, n, revrow):
                ro(v.tensor_reduce(m1[:, :], src, AX, ALU.max))
                ro(v.tensor_tensor(dst, src, m1[:, :].unsqueeze(2).to_broadcast([P, NT, n]), ALU.is_equal))
                ro(v.tensor_tensor(dst, dst, b3(revrow, n), ALU.mult))
                ro(v.tensor_reduce(m1[:, :], dst, AX, ALU.max))
                ro(v.tensor_tensor(dst, dst, m1[:, :].unsqueeze(2).to_broadcast([P, NT, n]), ALU.is_equal))

            first_max(g2_[:, :, :], g0_[:, :, :], NG, rev[:, NE:NE + NG])
            gb = g2_[:, :, :].unsqueeze(3).to_broadcast([P, NT, NG, EPG])
            t04 = t0[:, :, :].rearrange("p t (g e) -> p t g e", g=NG)
            ro(v.tensor_tensor(t04, b4, gb, ALU.mult))
            ro(v.tensor_scalar(g3_[:, :, :], g2_[:, :, :], -1.0, 1e30, ALU.add, ALU.mult))
            gb3 = g3_[:, :, :].unsqueeze(3).to_broadcast([P, NT, NG, EPG])
            ro(v.tensor_tensor(t04, t04, gb3, ALU.add))
            first_max(oh[0][:, :, :], t0[:, :, :], NE, rev[:, 0:NE])
            ro(v.scalar_tensor_tensor(t0[:, :, :], oh[0][:, :, :], -2e30, t0[:, :, :], ALU.mult, ALU.add))
            first_max(oh[1][:, :, :], t0[:, :, :], NE, rev[:, 0:NE])
            ro(v.tensor_tensor(t1[:, :, :], oh[0][:, :, :], oh[1][:, :, :], ALU.add))
            ro(v.memset(Mex[:, 0, :], 0.0))
            for t in range(1, NT):
                ro(v.tensor_tensor(Mex[:, t, :], Mex[:, t - 1, :], t1[:, t - 1, :], ALU.add))
            ro(v.tensor_tensor(nb_[:, :], Mex[:, NT - 1, :], t1[:, NT - 1, :], ALU.add))
            RANK_READY[0] = q[0]
            dve.wait_ge(rank_mm, 1)
            ro(v.tensor_copy(rank[:, :, :].rearrange("p t e -> p (t e)"), bank(0, P)))
            dve.wait_ge(rank_mm, 2)
            ro(v.tensor_copy(cnt[:, :], bank(1, NE)))
            c3 = c8[:, 0:NE * 8].rearrange("p (e j) -> p e j", j=8)
            ro(v.tensor_scalar(mul8[:, :], iota[:, 0:8], 128.0, None, ALU.mult))
            ro(v.tensor_tensor(c3, cnt[:, :].unsqueeze(2).to_broadcast([P, NE, 8]),
                               mul8[:, :].unsqueeze(1).to_broadcast([P, NE, 8]), ALU.is_gt))
            ro(v.tensor_reduce(nb_[:, :], c3, AX, ALU.add))
            bg = big[:, 0:NE, :]
            ro(v.tensor_tensor(bg, before[:, :, :], nb_[:, :].unsqueeze(1).to_broadcast([P, NE, NE]), ALU.mult))
            ro(v.tensor_reduce(pst[:, :], bg, AX, ALU.add))
            ro(v.tensor_tensor(pen[:, :], pst[:, :], nb_[:, :], ALU.add))
            for k in range(2):
                ro(v.tensor_tensor(t1[:, :, :], oh[k][:, :, :], rank[:, :, :], ALU.mult))
                ro(v.tensor_reduce(Rk[:, k, :], t1[:, :, :], AX, ALU.add))
                ro(v.tensor_tensor(t1[:, :, :], oh[k][:, :, :], b3(pst[:, :], NE), ALU.mult))
                ro(v.tensor_reduce(Pk[:, k, :], t1[:, :, :], AX, ALU.add))
            c4 = c8[:, :].rearrange("p (a j) -> p a j", j=8)
            Rf = Rk[:, :, :].rearrange("p k t -> p (k t)")
            rf = rb_[:, :, :].rearrange("p k t -> p (k t)")
            Pf = Pk[:, :, :].rearrange("p k t -> p (k t)")
            ro(v.tensor_tensor(c4, Rf.unsqueeze(2).to_broadcast([P, 16, 8]),
                               mul8[:, :].unsqueeze(1).to_broadcast([P, 16, 8]), ALU.is_ge))
            ro(v.tensor_reduce(rf, c4, AX, ALU.add))
            ro(v.tensor_scalar(rf, rf, -1.0, None, ALU.add))
            ro(v.tensor_tensor(Pf, Pf, rf, ALU.add))
            ro(v.scalar_tensor_tensor(Rf, rf, -128.0, Rf, ALU.mult, ALU.add))
            ro(v.tensor_tensor(Aoh[:, :, :], iota[:, :].unsqueeze(1).to_broadcast([P, 16, P]),
                               Rf.unsqueeze(2).to_broadcast([P, 16, P]), ALU.is_equal), False)
            ro(v.tensor_tensor(bsel[:, :, :], iota[:, 0:MAXBLK].unsqueeze(1).to_broadcast([P, 16, MAXBLK]),
                               Pf.unsqueeze(2).to_broadcast([P, 16, MAXBLK]), ALU.is_equal))
            ro(v.tensor_tensor(Boh[:, :, :].rearrange("p (k t) b -> p k t b", k=2), bsel[:, :, :].rearrange("p (k t) b -> p k t b", k=2),
                               tokid[:, :].unsqueeze(1).unsqueeze(3).to_broadcast([P, 2, NT, MAXBLK]), ALU.mult))
            OH_READY[0] = q[0]
            ro(v.scalar_tensor_tensor(rf, Pf, 128.0, Rf, ALU.mult, ALU.add))
            ro(v.tensor_copy(slot_u[:, :, :].rearrange("p k t -> p (k t)"), rf))
            ro(v.tensor_copy(nblk_i[:, :], pen[:, NE - 1:NE]))
            for k in range(2):
                ro(v.tensor_tensor(t0[:, :, :], oh[k][:, :, :], s_[:, :, :], ALU.mult))
                ro(v.tensor_reduce(ms_[:, k, :], t0[:, :, :], AX, ALU.add))
            ro(v.tensor_tensor(m1[:, :], ms_[:, 0, :], ms_[:, 1, :], ALU.add))
            ro(v.reciprocal(m1[:, :], m1[:, :]))
            for k in range(2):
                ro(v.tensor_tensor(wk[:, k, :], ms_[:, k, :], m1[:, :], ALU.mult))
            dve.wait_ge(idx_mm, 1)
            v.tensor_copy(idx_u[:, :], bank(2, MAXBLK)).then_inc(tabs, 1)
            i16 = iota2[:, 0:NE]
            ro(v.tensor_scalar(live[:, :], nb_[:, :], 0.0, None, ALU.is_gt))
            ro(v.scalar_tensor_tensor(live[:, :], i16, float(NSLOT), live[:, :], ALU.is_lt, ALU.max))
            ro(v.tensor_tensor(big[:, :, :], iota2[:, :].unsqueeze(2).to_broadcast([P, MAXBLK, NE]),
                               pen[:, :].unsqueeze(1).to_broadcast([P, MAXBLK, NE]), ALU.is_ge))
            ro(v.tensor_tensor(big[:, :, :], big[:, :, :], live[:, :].unsqueeze(1).to_broadcast([P, MAXBLK, NE]), ALU.mult))
            ro(v.tensor_reduce(ef[:, :], big[:, :, :], AX, ALU.add))
            ro(v.tensor_scalar(ef[:, :], ef[:, :], 1.0, 16.0, ALU.add, ALU.min))
            v.tensor_copy(blk_t[:, :], ef[:, :]).then_inc(tabs, 1)
            ro(v.tensor_tensor(bg, before2[:, :, :], live[:, :].unsqueeze(1).to_broadcast([P, NE, NE]), ALU.mult))
            ro(v.tensor_reduce(turn[:, :], bg, AX, ALU.add))
            ro(v.tensor_tensor(sel[:, :, :], i16.unsqueeze(2).to_broadcast([P, NE, NE]),
                               turn[:, :].unsqueeze(1).to_broadcast([P, NE, NE]), ALU.is_equal))
            ro(v.tensor_tensor(sel[:, :, :], sel[:, :, :], live[:, :].unsqueeze(1).to_broadcast([P, NE, NE]), ALU.mult))
            ro(v.tensor_tensor(sel2[:, :, :], sel[:, :, :], i16.unsqueeze(1).to_broadcast([P, NE, NE]), ALU.mult))
            ro(v.tensor_reduce(tf[:, :], sel2[:, :, :], AX, ALU.add))
            v.tensor_copy(turn_e[:, :], tf[:, :])
            v.memset(ff[:, 0:3], 0.0)
            ro(v.tensor_tensor(sel2[:, :, :], sel[:, :, :], pen[:, :].unsqueeze(1).to_broadcast([P, NE, NE]), ALU.mult))
            ro(v.tensor_reduce(ff[:, 3:NE + 3], sel2[:, :, :], AX, ALU.add))
            ro(v.tensor_scalar(ff[:, :], ff[:, :], 1.0, None, ALU.add))
            ro(v.tensor_copy(freed_i[:, :], ff[:, :]))
            ro(v.tensor_tensor(tf[:, 0:1], turn[:, NE - 1:NE], live[:, NE - 1:NE], ALU.add))
            ro(v.tensor_scalar(tf[:, 1:2], tf[:, 0:1], -1.0, None, ALU.add))
            v.tensor_copy(nturn_i[:, :], tf[:, 0:2]).then_inc(tabs, 1)
            dve.wait_ge(tabs, 3)
            nblk = dve.value_load(nblk_i[0:1, 0:1], min_val=16, max_val=31)
            xTlf = xTl[:, :, :].rearrange("p k q -> p (k q)")
            xThf = xTh[:, :, :].rearrange("p k q -> p (k q)")
            hhTlf = hhTl[:, :, :].rearrange("p k q -> p (k q)")
            hhThf = hhTh[:, :, :].rearrange("p k q -> p (k q)")

            def chunk_low(off, ch):
                v.tensor_tensor(RL[ch % 4][:, :], EXP[:, bass.ds(off + ch * 1024, 1024)], RH[ch % 4][:, :].bitcast(F32),
                                ALU.subtract).then_inc(chunk_lo, 1)

            def rows_low(n):
                dve.wait_ge(xT_hi, n)
                v.tensor_tensor(xTlf, bank(2, BANK, 2), xThf.bitcast(F32), ALU.subtract).then_inc(xT_lo, 1)

            dve.sem_inc(chunk_lo, NCH)
            rows_low(1)
            with dve.Fori(0, nblk) as b:
                e1, off = expert_slot(dve, b)
                for ch in range(9):
                    dve.wait_ge(chunk_hi, b * NCH + (ch + 1))
                    chunk_low(off, ch)
                    if ch == 7:
                        dve.wait_ge(sig_a, b + 1)
                        v.tensor_tensor(sig[:, :], sig[:, :], bank(0), ALU.mult).then_inc(silu_g, 1)
                dve.wait_ge(silu_g, b + 1)
                dve.wait_ge(chunk_used, b * NCH + 8)
                v.tensor_tensor(hh[:, :], sig[:, :], bank(1), ALU.mult).then_inc(hh_v, 1)
                dve.wait_ge(chunk_hi, b * NCH + 10)
                chunk_low(off, 9)
                for hf in range(2):
                    dve.wait_ge(hhT_hi, b * 2 + (hf + 1))
                    v.tensor_tensor(hhTlf[:, hf * 256:(hf + 1) * 256], bank((4, 7)[hf], 256),
                                    hhThf[:, hf * 256:(hf + 1) * 256].bitcast(F32), ALU.subtract).then_inc(hhT_lo, 1)
                for ch in range(10, NCH):
                    dve.wait_ge(chunk_hi, b * NCH + (ch + 1))
                    chunk_low(off, ch)
                rows_low(b + 2)
            dve.wait_ge(rowB_in, 48)
            nturn = dve.value_load(nturn_i[0:1, 0:1], min_val=NSLOT, max_val=NE)
            dve.wait_ge(x2_in, 16)
            for t in range(NT):
                n = [COMB * t]

                def cb(ins, wait=True):
                    n[0] += 1
                    ins.then_inc(comb, 1)
                    if wait:
                        dve.wait_ge(comb, n[0])

                R = r2[:, t % 4, :]
                dve.wait_ge(comb_w0, t + 1)
                cb(v.scalar_tensor_tensor(R, yg[:, t % 4, 1, :], wk[:, 1, t:t + 1], R, ALU.mult, ALU.add))
                cb(v.tensor_tensor(R, R, comb_row(nturn, NT), ALU.mult))
                cb(v.scalar_tensor_tensor(R, comb_row(nturn, t), ALPHA, R, ALU.mult, ALU.add))
                for hf in range(2):
                    cb(v.bn_stats(stat[:, t % 2, 6 * hf:6 * hf + 6], r2[:, t % 4, hf * 512:(hf + 1) * 512]), hf == 1)
                cb(v.bn_aggr(mv[:, t, :], stat[:, t % 2, :]))
                cb(v.tensor_scalar(rstd[:, t:t + 1], mv[:, t, 1:2], EPS, None, ALU.add), False)
                cb(v.scalar_tensor_tensor(R, R, mv[:, t, 0:1], comb_row(nturn, NT + 1), ALU.subtract, ALU.mult), False)
                dve.wait_ge(comb_rs, t + 1)
                cb(v.reciprocal(rstd[:, t:t + 1], rstd[:, t:t + 1]), False)

        @block.tensor
        def _(pe):
            mm = nc.tensor.matmul
            pe.wait_ge(small_in, 112)
            for g in range(3):
                mm(ps[0:12, (5 + g) * BANK:(5 + g) * BANK + 384], relb[:, :], onehot[:, g * 384:(g + 1) * 384],
                   start=True, stop=True).then_inc(btab_mm, 1)

            def ada(ch, b):
                ada_in(pe, ch)
                w = adas[ADA_SLOT[ch]][:, :].rearrange("p (k n) -> p k n", k=2)
                for kk in range(2):
                    k = 2 * (ch % 4) + kk
                    for j in range(4):
                        last = mm(ps[32 * j:32 * j + 32, b * BANK:(b + 1) * BANK], csil[:, k:k + 1].to_broadcast([P, 32]),
                                  w[:, kk, j * 512:(j + 1) * 512], start=(k == 0), stop=(k == NK - 1), skip_group_check=True)
                last.then_inc(ada_mm, 1)

            pe.wait_ge(silu_v, 3)
            for ch in range(4):
                ada(ch, 0)
            pe.wait_ge(ada_ev, 1)
            for q in range(4):
                last = nc.tensor.transpose(ps[:, q * P:(q + 1) * P], modrow[:, q * P:(q + 1) * P], ident[:, :])
            last.then_inc(ss_mm, 1)
            pe.wait_ge(ln0, 26 + NT)
            pe.wait_ge(btab_ev, 3)
            pe.wait_ge(ss_one, 2)
            for k in range(NK):
                if k >= 3:
                    pe.wait_ge(xt_a, k - 2)
                b0 = 1 + 2 * (k % 3)
                for t in range(NT):
                    last = nc.tensor.transpose(ps[:, b0 * BANK + t * P:b0 * BANK + (t + 1) * P], xs[:, t, k * P:(k + 1) * P], ident[:, :])
                last.then_inc(xt_mm, 1)
            pe.wait_ge(h_hi, 2 * NK)

            def split_product(out_, lh, ll, rh, rl, first, last):
                mm(out_, lh, rh, start=first, stop=False)
                mm(out_, ll, rh, start=False, stop=False)
                return mm(out_, lh, rl, start=False, stop=last)

            for g, (ci, kind, q, eng_) in enumerate(groups):
                if g == 0 or groups[g - 1][0] != ci:
                    pe.wait_ge(w_lo, ci + 1)
                if g >= 8:
                    pe.wait_ge(proj_a if groups[g - 8][3] == "a" else proj_v, taken(g - 8))
                out_ = bank(g % 8)
                if kind == "fl":
                    if q == 0:
                        pe.wait_ge(btab_in, 32)
                    mm(out_, flip[:, :], flip_group(q)[0], start=True, stop=True).then_inc(proj_mm, 1)
                    continue
                if kind == "vt":
                    if q == 0:
                        for vg in [x for x in range(NGRP) if groups[x][1] == "vb"]:
                            pe.wait_ge(proj_a if groups[vg][3] == "a" else proj_v, taken(vg))
                    for t in range(4):
                        last = nc.tensor.transpose(out_[:, t * P:(t + 1) * P], vbT[:, (4 * q + t) * P:(4 * q + t + 1) * P],
                                                   ident[:, :])
                    last.then_inc(proj_mm, 1)
                    continue
                wh = WH[ci % 2][:, :].rearrange("p (k n) -> p k n", k=NK)
                wl = WL[ci % 2][:, :].rearrange("p (k n) -> p k n", k=NK)
                if kind == "va":
                    for t in range(2):
                        rows = slice((2 * (q % 4) + t) * P, (2 * (q % 4) + t + 1) * P)
                        for k in range(NK):
                            last = split_product(out_[:, t * 256:(t + 1) * 256], hTh[:, k, rows], hTl[:, k, rows], wh[:, k, :],
                                                 wl[:, k, :], k == 0, k == NK - 1)
                    last.then_inc(proj_mm, 1)
                    continue
                c0 = {"kb": 0, "vb": P}.get(kind, (q // 2 % 2) * P)
                half = slice((q % 2) * 512, (q % 2) * 512 + 512)
                for k in range(NK):
                    last = split_product(out_, wh[:, k, c0:c0 + P], wl[:, k, c0:c0 + P], hTh[:, k, half], hTl[:, k, half],
                                         k == 0, k == NK - 1)
                last.then_inc(proj_mm, 1)
            pe.wait_ge(proj_v, NVG)
            pe.wait_ge(proj_a, NAG)
            for u in range(32 + 3):
                if u < 32:
                    h, i = u // NT, u % NT
                    n = P * (i + 1)
                    pe.wait_ge(padA, 2 * u + 2)
                    for m in range(2):
                        if u >= 1:
                            pe.wait_ge(logitA, 2 * (u - 1) + m + 1)
                        for c0 in range(0, n, 512):
                            w = min(512, n - c0)
                            last = mm(ps[:, 2 * m * BANK + c0:2 * m * BANK + c0 + w], qpad[:, u % 2, m, :], Ka[:, h, c0:c0 + w], start=True, stop=True)
                        last.then_inc(scoreA, 1)
                v = u - 2
                if 0 <= v < 32:
                    h, i = v // NT, v % NT
                    pe.wait_ge(attnA, 4 * v + 4)
                    for g in range(ngrp(i)):
                        gg = grp0(v) + g
                        if gg >= 2:
                            pe.wait_ge(aT_ev, gg - 1)
                        for kt in range(4 * g, min(4 * g + 4, i + 1)):
                            last = nc.tensor.transpose(ps[:, (4 + gg % 2) * BANK + (kt % 4) * P:(4 + gg % 2) * BANK + (kt % 4 + 1) * P],
                                                       L[:, v % 3, 0, kt * P:(kt + 1) * P], ident[:, :])
                        last.then_inc(trA, 1)
                v = u - 3
                if v >= 0:
                    h, i = v // NT, v % NT
                    for g in range(ngrp(i)):
                        gg = grp0(v) + g
                        pe.wait_ge(aT_ev, gg + 1)
                        if g == 0 and v >= 1:
                            pe.wait_ge(oA, 2 * (v - 1) + 1)
                        for kt in range(4 * g, min(4 * g + 4, i + 1)):
                            last = mm(bank(6, P), aT[:, gg % 4, (kt % 4) * P:(kt % 4 + 1) * P], Va[:, kt, h * P:(h + 1) * P],
                                      start=(kt == 0), stop=(kt == i))
                        last.then_inc(pvA, 1)
                if u in ADA_AT:
                    ch = 4 + ADA_AT.index(u)
                    if ch == 8:
                        pe.wait_ge(ada_ev, 2)
                    ada(ch, 7)
            pe.wait_ge(ada_ev, 3)
            pe.wait_ge(oA, 63)
            for u in range(32 + 3):
                if u < 32:
                    i, t = u // 4, u % 4
                    pe.wait_ge(padB, 2 * u + 2)
                    k0 = max(0, (i - 1) * P)
                    n = (i + 1) * P - k0
                    for j in range(2):
                        if u >= 2:
                            pe.wait_ge(logitB, 2 * (u - 2) + j + 1)
                        b0 = (2 * (u % 2) + j) * BANK
                        mm(ps[:, b0:b0 + n], qpad[:, u % 2, j, :], Kb[:, k0:k0 + n], start=True, stop=True).then_inc(scoreB, 1)
                v = u - 2
                if 0 <= v < 32:
                    i, t = v // 4, v % 4
                    nt = 2 if i else 1
                    pe.wait_ge(expB, 2 * v + 2)
                    if v >= 2:
                        pe.wait_ge(bT_ev, v - 1)
                    for j in range(2):
                        for kt in range(nt):
                            col = (4 + v % 2) * BANK + (j * nt + kt) * P
                            last = nc.tensor.transpose(ps[:, col:col + P], LB[:, v % 4, j, (2 - nt + kt) * P:(3 - nt + kt) * P], ident[:, :])
                    last.then_inc(trB, 1)
                v = u - 3
                if v >= 0:
                    i, t = v // 4, v % 4
                    nt = 2 if i else 1
                    pe.wait_ge(bT_ev, v + 1)
                    if v >= 2:
                        pe.wait_ge(oB, v - 1)
                    for j in range(2):
                        for kt in range(nt):
                            last = mm(ps[:, (6 + v % 2) * BANK + j * P:(6 + v % 2) * BANK + (j + 1) * P], aT[:, v % 4, (j * nt + kt) * P:(j * nt + kt + 1) * P],
                                      Vb[:, i - nt + 1 + kt, :], start=(kt == 0), stop=(kt == nt - 1))
                    last.then_inc(pvB, 1)
            pe.wait_ge(logitB, 64)
            pe.wait_ge(bT_ev, 32)
            for f in range(16):
                src, q = (Qa, f) if f < 8 else (Qb, f - 8)
                pe.wait_ge(fin_v, 2 + f // 2 if f < 8 else 7 + q // 2)
                if f == 6:
                    pe.wait_ge(oB, 32)
                if f >= 8:
                    pe.wait_ge(finT_v, f - 7)
                for i4 in range(4):
                    i = 4 * (q % 2) + i4
                    last = nc.tensor.transpose(ps[:, (f % 8) * BANK + i4 * P:(f % 8) * BANK + (i4 + 1) * P], src[:, q // 2, i * P:(i + 1) * P], ident[:, :])
                last.then_inc(finT, 1)
            for m in range(16):
                d, hf, ci = m // 2, m % 2, NPC + m // 4
                if m % 4 == 0:
                    pe.wait_ge(w_lo, ci + 1)
                if m >= 4:
                    pe.wait_ge(merged, 5 * (m - 4) + 2)
                wh = WH[ci % 2][:, :].rearrange("p (g k n) -> p g k n", g=2, k=4)
                wl = WL[ci % 2][:, :].rearrange("p (g k n) -> p g k n", g=2, k=4)
                cols, half = slice((d % 2) * P, (d % 2 + 1) * P), slice(hf * 512, (hf + 1) * 512)
                for g in range(2):
                    if m == 0:
                        pe.wait_ge(finT_v, (9, 16)[g])
                    for k in range(4):
                        last = split_product(bank(2 * (m % 4) + g), wh[:, g, k, cols], wl[:, g, k, cols], Oh[:, 4 * g + k, half],
                                             Ol[:, 4 * g + k, half], k == 0, k == 3)
                    last.then_inc(merge_mm, 1)
            rwf = rwz[:, :, :].rearrange("p k e -> p (k e)")
            pe.wait_ge(merged, 80)
            def route_rows(s):
                pe.wait_ge(h2T_ev, s + 1)
                if s == 0:
                    pe.wait_ge(rwp_v, 1)
                    pe.wait_ge(rt_in, 16 * 7)
                if s >= 1:
                    pe.wait_ge(rout_ev, s)
                for k in range(NK):
                    last = mm(bank(6, P), h2T[:, k, :], rwf[:, k * NE:k * NE + P], start=(k == 0), stop=(k == NK - 1))
                last.then_inc(rout_mm, 1)

            for t in range(NT + 1):
                rows = slice(t * P, (t + 1) * P)
                for n in range(2):
                    if t < NT:
                        if t >= 2 and n == 0:
                            pe.wait_ge(post_v, POST * (t - 2) + 1)
                        for k in range(NK):
                            if t == 0:
                                pe.wait_ge(wo_lo, 8 * n + k + 1)
                            last = split_product(bank(2 * (t % 2) + n), mTh[:, k, rows], mTl[:, k, rows], WOH[n][:, k, :],
                                                 WOL[n][:, k, :], k == 0, k == NK - 1)
                        last.then_inc(y_mm, 1)
                    if t >= 2 and n == 0:
                        route_rows(t - 2)
                if t >= 1:
                    s = t - 1
                    pe.wait_ge(post_v, POST * (s + 1))
                    if s >= 1:
                        pe.wait_ge(h2T_ev, s)
                    for k in range(NK):
                        last = nc.tensor.transpose(ps[:, 4 * BANK + k * P:4 * BANK + (k + 1) * P], h2[:, s % 2, k * P:(k + 1) * P], ident[:, :])
                    last.then_inc(h2T_mm, 1)
            route_rows(NT - 1)
            pe.wait_ge(route, RANK_READY[0])
            t1f = t1[:, :, :].rearrange("p t e -> p (t e)")
            mm(bank(0, P), lower[:, :], t1f, start=True, stop=False)
            mm(bank(0, P), ones[:, :], Mex[:, :, :].rearrange("p t e -> p (t e)"), start=False, stop=True).then_inc(rank_mm, 1)
            mm(bank(1, NE), ones[:, :], nb_[:, :], start=True, stop=True).then_inc(rank_mm, 1)
            pe.wait_ge(route, OH_READY[0])
            for a in range(16):
                last = mm(bank(2, MAXBLK), Aoh[:, a, :], Boh[:, a, :], start=(a == 0), stop=(a == 15))
            last.then_inc(idx_mm, 1)
            pe.wait_ge(tabs, 1)
            nblk = pe.value_load(nblk_i[0:1, 0:1], min_val=16, max_val=31)

            def transpose_rows(half):
                for k in range(4 * half, 4 * half + 4):
                    last = nc.tensor.transpose(ps[:, 2 * BANK + k * P:2 * BANK + (k + 1) * P], xg[:, k * P:(k + 1) * P], ident[:, :])
                last.then_inc(xg_tr, 1)

            pe.wait_ge(gathered, 16)
            transpose_rows(0)
            transpose_rows(1)
            with pe.Fori(0, nblk) as b:
                pe.wait_ge(xT_lo, b + 1)
                for ch in range(8):
                    pe.wait_ge(chunk_lo, b * NCH + (NCH + ch + 1))
                    for kk in range(2):
                        k = 2 * (ch % 4) + kk
                        cols = slice(kk * FE, (kk + 1) * FE)
                        last = split_product(bank(ch // 4), xTh[:, k, :], xTl[:, k, :], RH[ch % 4][:, cols], RL[ch % 4][:, cols],
                                             k == 0, k == NK - 1)
                    last.then_inc(chunk_used, 1)
                pe.wait_ge(gathered, b * 16 + 32)
                transpose_rows(0)
                pe.wait_ge(hh_v, b + 1)
                for k in range(4):
                    last = nc.tensor.transpose(bank((4, 7)[k // 2])[:, (k % 2) * P:(k % 2 + 1) * P], hh[:, k * P:(k + 1) * P], ident[:, :])
                last.then_inc(hh_tr, 1)
                transpose_rows(1)
                pe.wait_ge(y_a, b + 1)
                for k in range(4):
                    pe.wait_ge(chunk_lo, b * NCH + (NCH + 8 + k + 1))
                    pe.wait_ge(hhT_hi, b * 2 + (k // 2 + 1))
                    for n in range(2):
                        cols = slice(n * BANK, (n + 1) * BANK)
                        mm(bank(5 + n), hhTh[:, k, :], RH[k][:, cols], start=(k == 0), stop=False)
                        mm(bank(5 + n), hhTh[:, k, :], RL[k][:, cols], start=False, stop=False)
                    pe.wait_ge(hhT_lo, b * 2 + (k // 2 + 1))
                    for n in range(2):
                        last = mm(bank(5 + n), hhTl[:, k, :], RH[k][:, n * BANK:(n + 1) * BANK], start=False, stop=(k == 3))
                    last.then_inc(chunk_used, 1)


_INS = ["x", "c", "ada_w", "ada_b", "w_in", "lam", "subln_w", "sinks", "w_branch_a", "w_branch_b", "w_out",
        "ln_g", "ln_b", "rel_bias", "router_w", "router_b", "exp_w1", "exp_w3", "exp_w2"]


def _constants():
    import math

    import numpy as np

    rel = np.arange(TAB) - 1023
    nb = NBUCKET // 2
    exact = nb // 2
    n = np.abs(rel)
    far = exact + (np.log(np.maximum(n, 1).astype(np.float32) / np.float32(exact)) / np.float32(math.log(1024 / exact))
                   * np.float32(nb - exact)).astype(np.int32)
    bucket = np.where(rel > 0, nb, 0) + np.where(n < exact, n, np.minimum(far, nb - 1))
    f = np.float32
    i = np.arange(P)
    rows = lambda v: np.ascontiguousarray(np.broadcast_to(np.asarray(v, f).reshape(1, -1), (P, np.size(v))))
    e = np.arange(NE)
    return {
        "ident": np.eye(P, dtype=f),
        "onehot": (bucket[None, :] == np.arange(NBUCKET)[:, None]).astype(f),
        "lower": (i[:, None] < i[None, :]).astype(f),
        "iota": rows(i),
        "rev": rows(np.concatenate([NE - e, NG - np.arange(NG)])),
        "before": rows(e[None, :] < e[:, None]),
        "tokid": (i[:, None] + P * np.arange(NT)[None, :]).astype(f),
        "flip": np.ascontiguousarray(np.eye(P, dtype=f)[::-1]),
    }


def kernel(**inputs):
    import numpy as _np
    import concourse.bacc as _bacc
    from concourse import mybir as _mybir
    from concourse.bass_utils import run_bass_kernel_spmd as _run

    nc = _bacc.Bacc("TRN2", target_bir_lowering=False, num_devices=1)
    arrays, args = {}, []
    named = [(n, inputs[n]) for n in _INS] + list(_constants().items())
    for name, value in named:
        a = _np.ascontiguousarray(value)
        arrays[f"in_{name}_dram"] = a
        args.append(nc.dram_tensor(f"in_{name}_dram", a.shape, _mybir.dt.from_np(a.dtype), kind="ExternalInput").ap())
    args.append(nc.dram_tensor("out_0_dram", (1, S, D), F32, kind="ExternalOutput").ap())
    mixer_moe_kernel(nc, *args)
    r = _run(nc, [arrays], core_ids=[0])
    return r.results[0]["out_0_dram"]
```
